# Optimizing a Trainium2 kernel written in Bass

```python
import jax, jax.numpy as jnp
from jax import lax
import numpy as np

D_MODEL = 1024
BATCH = 1
SEQ = 512
DEPTH = 1

PLE_DIM = 256
ROPE_THETA = 500000.0
EPS = 1e-6
NEG_INF = -1e30

MIX_WIDTH = D_MODEL
MLA_V_DIM = 64
MLA_NOPE_DIM = 64
MLA_ROPE_DIM = 32
MLA_QK_DIM = MLA_NOPE_DIM + MLA_ROPE_DIM
MLA_WIDTH = MIX_WIDTH // 2
MLA_HEADS = MLA_WIDTH // MLA_V_DIM
MLA_Q_RANK = 3 * D_MODEL // 8
MLA_KV_RANK = 4 * MLA_V_DIM
Q_BLOCK = 128
DIL_HEAD_DIM = 64
DIL_WIDTH = MIX_WIDTH - MLA_WIDTH
DIL_HEADS = DIL_WIDTH // DIL_HEAD_DIM
DIL_ROT_DIM = DIL_HEAD_DIM // 4
DIL_PATTERNS = ((128, 1), (512, 4), (2048, 16))
IN_SPLITS = (MLA_Q_RANK, MLA_KV_RANK, MLA_ROPE_DIM, DIL_WIDTH, DIL_WIDTH, DIL_WIDTH)
IN_WIDTH = sum(IN_SPLITS)
PEER_KEYS = 128
PEER_EXPERTS = PEER_KEYS * PEER_KEYS
PEER_HEADS = 8
PEER_QDIM = 128
PEER_HALF = PEER_QDIM // 2
PEER_TOPK = 16
PEER_CHUNK = 128


def rms_norm(x, g):
    xf = x.astype(jnp.float32)
    y = xf * lax.rsqrt(jnp.mean(xf * xf, axis=-1, keepdims=True) + EPS)
    return (y * g.astype(jnp.float32)).astype(x.dtype)

def rope_tables(seq, rot_dim):
    inv = ROPE_THETA ** (-jnp.arange(0, rot_dim, 2, dtype=jnp.float32) / rot_dim)
    ang = jnp.arange(seq, dtype=jnp.float32)[:, None] * inv[None, :]
    return jnp.cos(ang), jnp.sin(ang)

def apply_rope(x, cos, sin, rot_dim):
    half = rot_dim // 2
    shape = (x.shape[1],) + (1,) * (x.ndim - 3) + (half,)
    c = cos.reshape(shape).astype(x.dtype)
    s = sin.reshape(shape).astype(x.dtype)
    x1 = x[..., :half]
    x2 = x[..., half:rot_dim]
    return jnp.concatenate([x1 * c - x2 * s, x2 * c + x1 * s, x[..., rot_dim:]], axis=-1)

def mla_attention(q_nope, q_rope, k_nope, k_rope, v):
    B, S, H, _ = q_nope.shape
    nq = S // Q_BLOCK
    scale = MLA_QK_DIM ** -0.5

    def blocks(t):
        return jnp.moveaxis(t.reshape((B, nq, Q_BLOCK) + t.shape[2:]), 1, 0)

    def one_block(args):
        qn, qr = args
        s = jnp.einsum('bqhd,bkhd->bhqk', qn, k_nope) + jnp.einsum('bqhr,bkr->bhqk', qr, k_rope)
        w = jax.nn.softmax(s.astype(jnp.float32) * scale, axis=-1).astype(v.dtype)
        return jnp.einsum('bhqk,bkhd->bqhd', w, v)

    out = lax.map(one_block, (blocks(q_nope), blocks(q_rope)))
    return jnp.moveaxis(out, 0, 1).reshape(B, S, H, v.shape[-1])

def banded_attention(q, k, v, radius):
    N, L, hd = q.shape
    blk = radius
    nb = -(-L // blk)
    lp = nb * blk
    qb = jnp.pad(q, ((0, 0), (0, lp - L), (0, 0))).reshape(N, nb, blk, hd)

    def windows(t):
        tp = jnp.pad(t, ((0, 0), (blk, lp - L + blk), (0, 0))).reshape(N, nb + 2, blk, hd)
        return jnp.concatenate([tp[:, :-2], tp[:, 1:-1], tp[:, 2:]], axis=2)

    kw, vw = windows(k), windows(v)
    qpos = jnp.arange(nb)[:, None] * blk + jnp.arange(blk)[None, :]
    kpos = jnp.arange(nb)[:, None] * blk - blk + jnp.arange(3 * blk)[None, :]
    kp = kpos[:, None, :]
    mask = (jnp.abs(qpos[:, :, None] - kp) <= radius) & (kp >= 0) & (kp < L)
    s = jnp.einsum('nbqd,nbkd->nbqk', qb, kw).astype(jnp.float32) * (hd ** -0.5)
    s = jnp.where(mask, s, NEG_INF)
    m = jnp.max(s, axis=-1, keepdims=True)
    e = jnp.exp(s - m)
    den = jnp.sum(e, axis=-1, keepdims=True)
    out = jnp.einsum('nbqk,nbkd->nbqd', (e / den).astype(v.dtype), vw)
    lse = (m + jnp.log(den))[..., 0]
    return out.reshape(N, lp, hd)[:, :L], lse.reshape(N, lp)[:, :L]

def dilated_pattern(q, k, v, window, dil):
    B, S, H, hd = q.shape
    L = S // dil

    def to_sub(t):
        return t.reshape(B, L, dil, H, hd).transpose(0, 2, 3, 1, 4).reshape(B * dil * H, L, hd)

    o, l = banded_attention(to_sub(q), to_sub(k), to_sub(v), window // (2 * dil))
    o = o.reshape(B, dil, H, L, hd).transpose(0, 3, 1, 2, 4).reshape(B, S, H, hd)
    l = l.reshape(B, dil, H, L).transpose(0, 3, 1, 2).reshape(B, S, H)
    return o, l

def dilated_attention(q, k, v):
    outs, lses = [], []
    for window, dil in DIL_PATTERNS:
        o, l = dilated_pattern(q, k, v, window, dil)
        outs.append(o)
        lses.append(l)
    wts = jax.nn.softmax(jnp.stack(lses, axis=0), axis=0).astype(q.dtype)
    return jnp.einsum('pbsh,pbshd->bshd', wts, jnp.stack(outs, axis=0))

def peer_ffn(xn, w_q, keys1, keys2, u_tab, v_tab):
    B, S, D = xn.shape
    T = B * S
    xt = xn.reshape(T, D)
    q = (xt @ w_q).reshape(T, PEER_HEADS, 2, PEER_HALF)
    s1 = jnp.einsum('thd,kd->thk', q[:, :, 0], keys1)
    s2 = jnp.einsum('thd,kd->thk', q[:, :, 1], keys2)
    v1, i1 = lax.top_k(s1, PEER_TOPK)
    v2, i2 = lax.top_k(s2, PEER_TOPK)
    cand = (v1[..., :, None] + v2[..., None, :]).reshape(T, PEER_HEADS, PEER_TOPK * PEER_TOPK)
    cidx = (i1[..., :, None] * PEER_KEYS + i2[..., None, :]).reshape(T, PEER_HEADS, PEER_TOPK * PEER_TOPK)
    top, pos = lax.top_k(cand, PEER_TOPK)
    eidx = jnp.take_along_axis(cidx, pos, axis=-1)
    g = jax.nn.softmax(top.astype(jnp.float32), axis=-1).astype(xn.dtype)
    nc = T // PEER_CHUNK

    def chunk(args):
        xc, ec, gc = args
        a = jax.nn.gelu(jnp.einsum('td,thkd->thk', xc, u_tab[ec]), approximate=False)
        return jnp.einsum('thk,thkd->td', gc * a, v_tab[ec])

    y = lax.map(chunk, (xt.reshape(nc, PEER_CHUNK, D),
                        eidx.reshape(nc, PEER_CHUNK, PEER_HEADS, PEER_TOPK),
                        g.reshape(nc, PEER_CHUNK, PEER_HEADS, PEER_TOPK)))
    return y.reshape(B, S, D)

def first_inputs(seed: int = 0) -> dict:
    key = jax.random.key(seed)
    ks = jax.random.split(key, 24)
    f32 = jnp.float32

    def nrm(k, shape, scale):
        return jax.random.normal(k, shape, f32) * scale

    def gain(k, shape):
        return 1.0 + 0.01 * jax.random.normal(k, shape, f32)

    L = DEPTH
    return {
        "x": nrm(ks[0], (BATCH, SEQ, D_MODEL), 1.0),
        "p": nrm(ks[1], (DEPTH, BATCH, SEQ, PLE_DIM), 1.0),
        "g_mix": gain(ks[2], (L, D_MODEL)),
        "w_in": nrm(ks[3], (L, D_MODEL, IN_WIDTH), D_MODEL ** -0.5),
        "g_cq": gain(ks[4], (L, MLA_Q_RANK)),
        "w_uq": nrm(ks[5], (L, MLA_Q_RANK, MLA_HEADS * MLA_QK_DIM), MLA_Q_RANK ** -0.5),
        "g_ckv": gain(ks[6], (L, MLA_KV_RANK)),
        "w_ukv": nrm(ks[7], (L, MLA_KV_RANK, MLA_HEADS * (MLA_NOPE_DIM + MLA_V_DIM)), MLA_KV_RANK ** -0.5),
        "g_out_mla": gain(ks[8], (L, MLA_WIDTH)),
        "g_out_dil": gain(ks[9], (L, DIL_WIDTH)),
        "w_out": nrm(ks[10], (L, MIX_WIDTH, D_MODEL), MIX_WIDTH ** -0.5),
        "g_ffn": gain(ks[11], (L, D_MODEL)),
        "w_peer_q": nrm(ks[12], (L, D_MODEL, PEER_HEADS * PEER_QDIM), D_MODEL ** -0.5),
        "peer_keys1": nrm(ks[13], (L, PEER_KEYS, PEER_HALF), PEER_HALF ** -0.5),
        "peer_keys2": nrm(ks[14], (L, PEER_KEYS, PEER_HALF), PEER_HALF ** -0.5),
        "peer_u": nrm(ks[15], (L, PEER_EXPERTS, D_MODEL), D_MODEL ** -0.5),
        "peer_v": nrm(ks[16], (L, PEER_EXPERTS, D_MODEL), 0.5),
        "g_ple": gain(ks[17], (L, D_MODEL)),
        "w_ple_gate": nrm(ks[18], (L, D_MODEL, D_MODEL), D_MODEL ** -0.5),
        "w_ple_proj": nrm(ks[19], (L, PLE_DIM, D_MODEL), PLE_DIM ** -0.5),
        "g_final": gain(ks[20], (D_MODEL,)),
    }

def first_block(x, p, g_mix, w_in, g_cq, w_uq, g_ckv, w_ukv, g_out_mla, g_out_dil, w_out,
              g_ffn, w_peer_q, peer_keys1, peer_keys2, peer_u, peer_v,
              g_ple, w_ple_gate, w_ple_proj, g_final):
    B, S, _ = x.shape
    cos_m, sin_m = rope_tables(S, MLA_ROPE_DIM)
    cos_d, sin_d = rope_tables(S, DIL_ROT_DIM)
    offs = np.cumsum(IN_SPLITS)[:-1].tolist()
    h = x
    for i in range(DEPTH):
        hn = rms_norm(h, g_mix[i])
        c_q, c_kv, k_r, q_d, k_d, v_d = jnp.split(hn @ w_in[i], offs, axis=-1)
        q = (rms_norm(c_q, g_cq[i]) @ w_uq[i]).reshape(B, S, MLA_HEADS, MLA_QK_DIM)
        q_nope = q[..., :MLA_NOPE_DIM]
        q_rope = apply_rope(q[..., MLA_NOPE_DIM:], cos_m, sin_m, MLA_ROPE_DIM)
        kv = (rms_norm(c_kv, g_ckv[i]) @ w_ukv[i]).reshape(B, S, MLA_HEADS, MLA_NOPE_DIM + MLA_V_DIM)
        k_nope = kv[..., :MLA_NOPE_DIM]
        v_m = kv[..., MLA_NOPE_DIM:]
        k_rope = apply_rope(k_r, cos_m, sin_m, MLA_ROPE_DIM)
        o_mla = mla_attention(q_nope, q_rope, k_nope, k_rope, v_m).reshape(B, S, MLA_WIDTH)
        qd = apply_rope(q_d.reshape(B, S, DIL_HEADS, DIL_HEAD_DIM), cos_d, sin_d, DIL_ROT_DIM)
        kd = apply_rope(k_d.reshape(B, S, DIL_HEADS, DIL_HEAD_DIM), cos_d, sin_d, DIL_ROT_DIM)
        vd = v_d.reshape(B, S, DIL_HEADS, DIL_HEAD_DIM)
        o_dil = dilated_attention(qd, kd, vd).reshape(B, S, DIL_WIDTH)
        mixed = jnp.concatenate([rms_norm(o_mla, g_out_mla[i]), rms_norm(o_dil, g_out_dil[i])], axis=-1)
        h = h + mixed @ w_out[i]
        h = h + peer_ffn(rms_norm(h, g_ffn[i]), w_peer_q[i], peer_keys1[i], peer_keys2[i],
                         peer_u[i], peer_v[i])
        gate = jax.nn.sigmoid(rms_norm(h, g_ple[i]) @ w_ple_gate[i])
        h = h + gate * (p[i] @ w_ple_proj[i])
    return rms_norm(h, g_final)


_first_inputs = first_inputs


def first_inputs(seed=0):
    import zlib

    import numpy as np

    out = dict(_first_inputs(seed))
    spreads = {}
    factors = {'g_cq': 4.061,
     'g_ckv': 3.209,
     'g_out_mla': 20.425,
     'g_out_dil': 19.89,
     'g_ffn': 13.693,
     'g_ple': 64.0,
     'g_final': 34.918}
    for name, (base, spread) in spreads.items():
        noise = np.random.default_rng([zlib.crc32(name.encode()), seed]).standard_normal(out[name].shape)
        drawn = base * np.exp(spread * noise) if base else spread * noise
        out[name] = __import__('jax').numpy.asarray(drawn.astype(out[name].dtype))
    for name, factor in factors.items():
        out[name] = (out[name] * factor).astype(out[name].dtype)
    return out


_narrow_inputs = first_inputs


def first_inputs(seed=0):

    out = dict(_narrow_inputs(seed))
    wider = {'g_out_mla': 3.7, 'g_out_dil': 3.8, 'g_ple': 12.0, 'g_final': 6.65}
    for name, times in wider.items():
        mean = out[name].mean()
        out[name] = (mean + times * (out[name] - mean)).astype(out[name].dtype)
    return out


DEPTH_2 = 2

ATT_HEADS = 8
ATT_KV_HEADS = 2
HEAD_DIM = 64
Q_RANK = 256
IDX_HEADS = 8
IDX_DIM = 64
TOPK_MAX = 256
ML_HEADS = 4
ML_DIM = 128
CONV_W = 4
CHUNK = 64
D_FF = 4 * D_MODEL
ROT_DIM = HEAD_DIM // 4

ATT_W = ATT_HEADS * HEAD_DIM
KV_W = ATT_KV_HEADS * HEAD_DIM
ML_W = ML_HEADS * ML_DIM
MIX_W = ATT_W + ML_W
IN_SIZES = (Q_RANK, KV_W, KV_W, IDX_DIM, IDX_HEADS, ML_W, ML_W, ML_W, ML_W, ML_HEADS, ML_HEADS)
IN_W = sum(IN_SIZES)
IDX_SCALE = (IDX_HEADS ** -0.5) * (IDX_DIM ** -0.5)


def rms_norm_2(x, g):
    xf = x.astype(jnp.float32)
    y = xf * lax.rsqrt(jnp.mean(xf * xf, axis=-1, keepdims=True) + EPS)
    return (y * g.astype(jnp.float32)).astype(x.dtype)

def rope_tables_2(positions):
    half = ROT_DIM // 2
    inv = ROPE_THETA ** (-(jnp.arange(half, dtype=jnp.float32) * 2.0) / ROT_DIM)
    ang = positions.astype(jnp.float32)[..., None] * inv
    return jnp.cos(ang), jnp.sin(ang)

def apply_partial_rope(x, cos, sin):
    half = ROT_DIM // 2
    c = cos[:, :, None, :].astype(x.dtype)
    s = sin[:, :, None, :].astype(x.dtype)
    x1 = x[..., :half]
    x2 = x[..., half:ROT_DIM]
    return jnp.concatenate([x1 * c - x2 * s, x2 * c + x1 * s, x[..., ROT_DIM:]], axis=-1)

def causal_dwconv(x, w, b):
    S = x.shape[1]
    xp = jnp.pad(x, ((0, 0), (CONV_W - 1, 0), (0, 0)))
    acc = xp[:, 0:S] * w[0]
    for j in range(1, CONV_W):
        acc = acc + xp[:, j:j + S] * w[j]
    return acc + b

def dsa_attention(q, k, v, q_idx, k_idx, w_idx):
    B, S, H, D = q.shape
    G = H // ATT_KV_HEADS
    n_sel = min(TOPK_MAX, S // 4)
    nb = S // Q_BLOCK
    key_pos = jnp.arange(S)
    scale = D ** -0.5

    def blk(a):
        return a.reshape(B, nb, Q_BLOCK, *a.shape[2:]).swapaxes(0, 1)

    def one_block(args):
        qb, qib, wb, qpos = args
        logits = jnp.einsum('bqhd,bsd->bqhs', qib, k_idx)
        score = jnp.einsum('bqh,bqhs->bqs', wb, jax.nn.relu(logits)).astype(jnp.float32)
        causal = key_pos[None, :] <= qpos[:, None]
        score = jnp.where(causal[None], score, -jnp.inf)
        _, sel = lax.top_k(score, n_sel)
        k_sel = jax.vmap(lambda kb, ib: kb[ib])(k, sel)
        v_sel = jax.vmap(lambda vb, ib: vb[ib])(v, sel)
        valid = sel <= qpos[None, :, None]
        qg = qb.reshape(B, Q_BLOCK, ATT_KV_HEADS, G, D)
        s = jnp.einsum('bqgrd,bqkgd->bqgrk', qg, k_sel).astype(jnp.float32) * scale
        s = jnp.where(valid[:, :, None, None, :], s, -jnp.inf)
        pr = jax.nn.softmax(s, axis=-1).astype(v.dtype)
        o = jnp.einsum('bqgrk,bqkgd->bqgrd', pr, v_sel)
        return o.reshape(B, Q_BLOCK, H, D)

    out = lax.map(one_block, (blk(q), blk(q_idx), blk(w_idx), key_pos.reshape(nb, Q_BLOCK)))
    return out.swapaxes(0, 1).reshape(B, S, H, D)

def mlstm_chunkwise(q, k, v, i_pre, f_pre):
    B, S, H, D = q.shape
    nc = S // CHUNK
    f32 = jnp.float32
    qf = q.astype(f32) * (D ** -0.5)
    kf = k.astype(f32)
    vf = v.astype(f32)
    log_f = jax.nn.log_sigmoid(f_pre.astype(f32))
    log_i = i_pre.astype(f32)

    def chunks(a):
        a = a.reshape(B, nc, CHUNK, H, *a.shape[3:])
        return jnp.moveaxis(a, (1, 3), (0, 2))

    tri = jnp.tril(jnp.ones((CHUNK, CHUNK), dtype=bool))

    def step(carry, xs):
        C, n, m = carry
        qc, kc, vc, lic, lfc = xs
        b = jnp.cumsum(lfc, axis=-1)
        log_d = b[..., :, None] - b[..., None, :] + lic[..., None, :]
        log_d = jnp.where(tri, log_d, -jnp.inf)
        inter = b + m[..., None]
        m_t = jnp.maximum(inter, jnp.max(log_d, axis=-1))
        dmat = jnp.exp(log_d - m_t[..., None])
        inter_w = jnp.exp(inter - m_t)
        qk = jnp.einsum('bhtd,bhsd->bhts', qc, kc) * dmat
        num = inter_w[..., None] * jnp.einsum('bhtd,bhde->bhte', qc, C) + jnp.einsum('bhts,bhse->bhte', qk, vc)
        den = inter_w * jnp.einsum('bhtd,bhd->bht', qc, n) + jnp.sum(qk, axis=-1)
        h = num / jnp.maximum(jnp.abs(den), jnp.exp(-m_t))[..., None]
        b_last = b[..., -1]
        log_g = b_last[..., None] - b + lic
        m_new = jnp.maximum(b_last + m, jnp.max(log_g, axis=-1))
        g = jnp.exp(log_g - m_new[..., None])
        decay = jnp.exp(b_last + m - m_new)
        C_new = decay[..., None, None] * C + jnp.einsum('bhs,bhsd,bhse->bhde', g, kc, vc)
        n_new = decay[..., None] * n + jnp.einsum('bhs,bhsd->bhd', g, kc)
        return (C_new, n_new, m_new), h

    init = (jnp.zeros((B, H, D, D), f32), jnp.zeros((B, H, D), f32), jnp.zeros((B, H), f32))
    _, hs = lax.scan(step, init, (chunks(qf), chunks(kf), chunks(vf), chunks(log_i), chunks(log_f)))
    hs = jnp.moveaxis(hs, (0, 2), (1, 3)).reshape(B, S, H, D)
    return hs.astype(q.dtype)

def hybrid_layer(h, p_i, cos, sin, g_mix, w_in, g_cq, w_q_up, w_iq_up, g_qn, g_kn, g_ik,
                 conv_w, conv_b, i_bias, f_bias, g_mh, w_out, g_mlp, w_ff1, w_ff2,
                 g_ple, w_ple_gate, b_ple_gate, w_ple):
    B, S, _ = h.shape
    xn = rms_norm_2(h, g_mix)
    proj = xn @ w_in
    split_at = np.cumsum(IN_SIZES)[:-1].tolist()
    c_q, a_k, a_v, i_k, i_w, m_q, m_k, m_v, m_o, m_i, m_f = jnp.split(proj, split_at, axis=-1)

    c_q = rms_norm_2(c_q, g_cq)
    a_q = (c_q @ w_q_up).reshape(B, S, ATT_HEADS, HEAD_DIM)
    i_q = (c_q @ w_iq_up).reshape(B, S, IDX_HEADS, IDX_DIM)
    a_q = apply_partial_rope(rms_norm_2(a_q, g_qn), cos, sin)
    a_k = apply_partial_rope(rms_norm_2(a_k.reshape(B, S, ATT_KV_HEADS, HEAD_DIM), g_kn), cos, sin)
    a_v = a_v.reshape(B, S, ATT_KV_HEADS, HEAD_DIM)
    i_q = apply_partial_rope(i_q, cos, sin)
    i_k = apply_partial_rope(rms_norm_2(i_k, g_ik)[:, :, None, :], cos, sin)[:, :, 0, :]
    i_w = i_w * IDX_SCALE
    att = dsa_attention(a_q, a_k, a_v, i_q, i_k, i_w).reshape(B, S, ATT_W)

    qk = jax.nn.silu(causal_dwconv(jnp.concatenate([m_q, m_k], axis=-1), conv_w, conv_b))
    m_q, m_k = qk[..., :ML_W], qk[..., ML_W:]
    hm = mlstm_chunkwise(m_q.reshape(B, S, ML_HEADS, ML_DIM), m_k.reshape(B, S, ML_HEADS, ML_DIM),
                         m_v.reshape(B, S, ML_HEADS, ML_DIM), m_i + i_bias, m_f + f_bias)
    hm = (jax.nn.sigmoid(m_o) * rms_norm_2(hm, g_mh).reshape(B, S, ML_W))

    h = h + jnp.concatenate([att, hm], axis=-1) @ w_out

    u = rms_norm_2(h, g_mlp) @ w_ff1
    h = h + jnp.square(jax.nn.relu(u)) @ w_ff2

    gate = jax.nn.sigmoid(rms_norm_2(h, g_ple) @ w_ple_gate + b_ple_gate)
    return h + gate * (p_i @ w_ple)

def second_inputs(seed: int = 0) -> dict:
    key = jax.random.key(seed)
    ks = iter(jax.random.split(key, 32))
    f32 = jnp.float32

    def nrm(shape, scale):
        return jax.random.normal(next(ks), shape, f32) * scale

    def gain(shape):
        return 1.0 + nrm(shape, 0.02)

    L = DEPTH_2
    x = nrm((BATCH, SEQ, D_MODEL), 1.0)
    p = nrm((L, BATCH, SEQ, PLE_DIM), 1.0)
    offs = jax.random.randint(next(ks), (BATCH, 1), 0, 4096, dtype=jnp.int32)
    positions = jnp.arange(SEQ, dtype=jnp.int32)[None, :] + offs
    return {
        "x": x,
        "p": p,
        "positions": positions,
        "g_mix": gain((L, D_MODEL)),
        "w_in": nrm((L, D_MODEL, IN_W), D_MODEL ** -0.5),
        "g_cq": gain((L, Q_RANK)),
        "w_q_up": nrm((L, Q_RANK, ATT_W), Q_RANK ** -0.5),
        "w_iq_up": nrm((L, Q_RANK, IDX_HEADS * IDX_DIM), Q_RANK ** -0.5),
        "g_qn": gain((L, HEAD_DIM)),
        "g_kn": gain((L, HEAD_DIM)),
        "g_ik": gain((L, IDX_DIM)),
        "conv_w": nrm((L, CONV_W, 2 * ML_W), CONV_W ** -0.5),
        "conv_b": nrm((L, 2 * ML_W), 0.01),
        "i_bias": nrm((L, ML_HEADS), 0.1),
        "f_bias": jnp.linspace(3.0, 6.0, ML_HEADS, dtype=f32)[None, :] + nrm((L, ML_HEADS), 0.1),
        "g_mh": gain((L, ML_HEADS, ML_DIM)),
        "w_out": nrm((L, MIX_W, D_MODEL), MIX_W ** -0.5),
        "g_mlp": gain((L, D_MODEL)),
        "w_ff1": nrm((L, D_MODEL, D_FF), D_MODEL ** -0.5),
        "w_ff2": nrm((L, D_FF, D_MODEL), D_FF ** -0.5),
        "g_ple": gain((L, D_MODEL)),
        "w_ple_gate": nrm((L, D_MODEL, D_MODEL), D_MODEL ** -0.5),
        "b_ple_gate": nrm((L, D_MODEL), 0.01),
        "w_ple": nrm((L, PLE_DIM, D_MODEL), PLE_DIM ** -0.5),
    }

def second_block(x, p, positions, g_mix, w_in, g_cq, w_q_up, w_iq_up, g_qn, g_kn, g_ik,
              conv_w, conv_b, i_bias, f_bias, g_mh, w_out, g_mlp, w_ff1, w_ff2,
              g_ple, w_ple_gate, b_ple_gate, w_ple):
    cos, sin = rope_tables_2(positions)
    h = x
    for i in range(DEPTH_2):
        h = hybrid_layer(h, p[i], cos, sin, g_mix[i], w_in[i], g_cq[i], w_q_up[i], w_iq_up[i],
                         g_qn[i], g_kn[i], g_ik[i], conv_w[i], conv_b[i], i_bias[i], f_bias[i],
                         g_mh[i], w_out[i], g_mlp[i], w_ff1[i], w_ff2[i], g_ple[i],
                         w_ple_gate[i], b_ple_gate[i], w_ple[i])
    return h


def setup_inputs(seed=0):
    out = dict(first_inputs(seed))
    for name, value in second_inputs(seed + 1).items():
        if name != "x":
            out[name + "_2"] = value
    return out


def reference(
    x, p, g_mix, w_in, g_cq, w_uq, g_ckv, w_ukv, g_out_mla, g_out_dil, w_out, g_ffn, w_peer_q,
    peer_keys1, peer_keys2, peer_u, peer_v, g_ple, w_ple_gate, w_ple_proj, g_final, p_2,
    positions_2, g_mix_2, w_in_2, g_cq_2, w_q_up_2, w_iq_up_2, g_qn_2, g_kn_2, g_ik_2, conv_w_2,
    conv_b_2, i_bias_2, f_bias_2, g_mh_2, w_out_2, g_mlp_2, w_ff1_2, w_ff2_2, g_ple_2,
    w_ple_gate_2, b_ple_gate_2, w_ple_2,
):
    x = first_block(
        x, p, g_mix, w_in, g_cq, w_uq, g_ckv, w_ukv, g_out_mla, g_out_dil, w_out, g_ffn,
        w_peer_q, peer_keys1, peer_keys2, peer_u, peer_v, g_ple, w_ple_gate, w_ple_proj,
        g_final,
    )
    return second_block(
        x, p_2, positions_2, g_mix_2, w_in_2, g_cq_2, w_q_up_2, w_iq_up_2, g_qn_2, g_kn_2,
        g_ik_2, conv_w_2, conv_b_2, i_bias_2, f_bias_2, g_mh_2, w_out_2, g_mlp_2, w_ff1_2,
        w_ff2_2, g_ple_2, w_ple_gate_2, b_ple_gate_2, w_ple_2,
    )


_drawn_inputs = setup_inputs


def setup_inputs(seed=0):
    import zlib

    import numpy as np

    out = dict(_drawn_inputs(seed))
    spreads = {}
    factors = {'g_ple': 8.0,
     'g_mix_2': 8.0,
     'w_in_2': 3.166,
     'g_cq_2': 8.0,
     'w_q_up_2': 8.0,
     'w_iq_up_2': 8.0,
     'g_qn_2': 8.0,
     'g_kn_2': 8.0,
     'g_ik_2': 8.0,
     'conv_w_2': 8.0,
     'conv_b_2': 200.0,
     'i_bias_2': 200.0,
     'f_bias_2': 8.0,
     'g_mh_2': 8.0,
     'w_out_2': 3.197,
     'g_mlp_2': 8.0,
     'g_ple_2': 75.148,
     'w_ple_gate_2': 6.713,
     'b_ple_gate_2': 200.0}
    for name, (base, spread) in spreads.items():
        noise = np.random.default_rng([zlib.crc32(name.encode()), seed]).standard_normal(out[name].shape)
        drawn = base * np.exp(spread * noise) if base else spread * noise
        out[name] = __import__('jax').numpy.asarray(drawn.astype(out[name].dtype))
    for name, factor in factors.items():
        out[name] = (out[name] * factor).astype(out[name].dtype)
    return out
```

```python
from contextlib import ExitStack

import numpy as np

import concourse.bass as bass
from concourse import mybir

F32 = mybir.dt.float32
I32 = mybir.dt.int32
U32 = mybir.dt.uint32
ALU = mybir.AluOpType
ACT = mybir.ActivationFunctionType
AX = mybir.AxisListType

P128 = 128
T = 512
NT = T // P128
D = 1024
ND = D // P128
EPS = 1e-6
NEG = -1e30
TAKEN = -3e38
PLE = 256

QR, KVR, RR = 384, 256, 32
MH, NOPE, VD = 8, 64, 64
QK = NOPE + RR
IN1 = QR + KVR + RR + 3 * 512
NE, KEYS, PH, TOPK = 16384, 128, 8, 16
ETG = 16
IN2 = 2640
NSEL = 128
IDX_SCALE = (8 ** -0.5) * (64 ** -0.5)
DFF = 4096

GC = {}


def _cols(layout):
    at = 0
    for name, n in layout:
        GC[name] = at
        at += n
    return at


N_GAIN = _cols([("g_mix", 8), ("g_cq", 3), ("g_ckv", 2), ("g_out", 8), ("g_ffn", 8), ("g_ple", 8)]
               + [(f"{n}_{l}", k) for l in range(2) for n, k in
                  [("g_mix", 8), ("g_cq", 2), ("g_mh", 4), ("g_mlp", 8), ("g_ple", 8), ("conv_w", 32),
                   ("conv_b", 8)]])
RC = {"g_final": 0}
for _l in range(2):
    RC[f"g_qn_{_l}"] = 1024 + 208 * _l
    RC[f"g_kn_{_l}"] = 1024 + 208 * _l + 64
    RC[f"g_ik_{_l}"] = 1024 + 208 * _l + 128
    RC[f"if_bias_{_l}"] = 1024 + 208 * _l + 192
N_ROW = 1024 + 2 * 208
CC = {"ident": 0, "iota": 128, "before": 256, "upto": 768, "causal": 896, "head": 1408, "iota16": 1920,
      "cos_m": 1936, "sin_m": 2000, "cos_d": 2064, "sin_d": 2096, "inv": 2128}
N_CONST = 2136


def constants():
    c = np.zeros((P128, N_CONST), np.float32)
    i = np.arange(P128)
    c[:, 0:128] = np.eye(P128)
    c[:, 128:256] = i[None, :]
    c[:, 256:640] = 1.0
    c[:, 640:768] = i[None, :] < i[:, None]
    c[:, 768:896] = i[:, None] <= i[None, :]
    c[:, 1280:1408] = np.where(i[None, :] <= i[:, None], 0.0, NEG)
    for h in range(4):
        c[h, 1408 + 128 * h:1536 + 128 * h] = 1.0
    c[:, 1920:1936] = np.arange(16)
    pos = np.arange(T, dtype=np.float32)

    def tables(rot):
        inv = np.float32(500000.0) ** (-np.arange(0, rot, 2, dtype=np.float32) / np.float32(rot))
        ang = (pos[:, None] * inv[None, :]).astype(np.float64)
        return inv, [f(ang).astype(np.float32).reshape(NT, P128, -1).transpose(1, 0, 2).reshape(P128, -1)
                     for f in (np.cos, np.sin)]
    _, (c[:, 1936:2000], c[:, 2000:2064]) = tables(32)
    inv, (c[:, 2064:2096], c[:, 2096:2128]) = tables(16)
    c[:, 2128:2136] = inv[None, :]
    q, k = np.arange(T)[:, None], np.arange(T)[None, :]
    n = np.zeros((T, T))
    for window, dil in ((128, 1), (512, 4), (2048, 16)):
        n += ((q - k) % dil == 0) & (np.abs(q - k) <= window // 2)
    bias = np.where(n > 0, np.log(np.maximum(n, 1)) * 8.0, NEG).astype(np.float32)
    return c, bias


class Engine:

    def __init__(self, key, own):
        self.key, self.own, self.count, self.items, self.waited = key, own, 0, [], {}

    def __call__(self, fn, after=(), own=None, mark=True, dma=None):
        need = {}

        def add(x):
            if x is None:
                return
            if isinstance(x, list):
                for y in x:
                    add(y)
            else:
                need[x[0]] = max(need.get(x[0], 0), x[1])
        add(list(after) if isinstance(after, tuple) and not (after and isinstance(after[0], str)) else after)
        if (self.own if own is None else own) and self.count:
            add((self.key, self.count))
        waits = []
        for k, v in need.items():
            if v > 0 and self.waited.get(k, 0) < v:
                self.waited[k] = v
                waits.append((k, v))
        if dma is not None:
            self.items.append((fn, waits, (dma[0], 16)))
            return dma
        if mark:
            self.count += 1
        self.items.append((fn, waits, (self.key, 1) if mark else None))
        return (self.key, self.count) if mark else None

    def emit(self, eng, sems):
        for fn, waits, inc in self.items:
            for k, v in waits:
                eng.wait_ge(sems[k], v)
            ins = fn(eng)
            if inc:
                ins.then_inc(sems[inc[0]], inc[1])


class Ring:

    def __init__(self, bufs):
        self.bufs, self.at = bufs, 0
        self.freed = [[] for _ in bufs]

    def take(self):
        i = self.at % len(self.bufs)
        self.at += 1
        assert self.freed[i] is not None, "taken before it was given back"
        f, self.freed[i] = self.freed[i], None
        return i, self.bufs[i], f

    def free(self, i, toks):
        self.freed[i] = toks


class Banks:

    def __init__(self, banks):
        self.banks, self.freed, self.at = banks, [[] for _ in banks], {}

    def take(self, among=tuple(range(8))):
        n = self.at.get(among, 0)
        self.at[among] = n + 1
        i = among[n % len(among)]
        assert self.freed[i] is not None, "bank taken before it was given back"
        f, self.freed[i] = self.freed[i], None
        return i, self.banks[i], f

    def free(self, i, toks):
        self.freed[i] = toks


def build(nc, A, stop=None):
    with ExitStack() as ctx:
        def sb(name, words, dt=F32):
            return ctx.enter_context(nc.sbuf_tensor(name, [P128, words], dt))

        H = sb("h", NT * D)[:, :].rearrange("p (t d) -> p t d", t=NT)
        XT = sb("xnT", ND * T)[:, :].rearrange("p (c t) -> p c t", c=ND)
        WRING = 3
        wbuf = [sb(f"w{i}", 4096) for i in range(WRING)]
        con = sb("con", N_CONST)
        gain = sb("gain", N_GAIN)
        row = sb("row", 208)
        stat = sb("stat", 512)
        stat_rope = sb("rope2", 64)
        arena = sb("arena", 29500)
        banks = Banks([ctx.enter_context(nc.psum_tensor(f"bank{i}", [P128, 512], F32)) for i in range(8)])
        g_scratch = nc.dram_tensor("g_scratch", (KEYS, KEYS, T), F32, kind="Internal").ap()

        def ar(at, n):
            assert at + n <= 29500, (at, n)
            return arena[:, at:at + n]

        P, V, S, G, Q = (Engine(k, own) for k, own in
                         [("pe", False), ("dve", True), ("act", True), ("pool", True), ("sp", False)])
        sem_names = ["pe", "dve", "act", "pool", "sp"]
        dma_count = {}

        def dma(out, in_, sem, after=(), q=None):
            if sem not in dma_count:
                dma_count[sem] = 0
                sem_names.append(sem)
            dma_count[sem] += 16
            return (q or Q)(lambda e: e.dma_start(out, in_), after, dma=(sem, dma_count[sem]))

        ident = con[:, 0:128]

        def cst(name, n, p=P128):
            return con[0:p, CC[name]:CC[name] + n]

        t_h = dma(H, A["x"].rearrange("(t p) d -> p t d", p=P128), "h_in")
        t_con = dma(con[:, :], A["consts"], "con_in")
        t_gain = dma(gain[:, :], A["gains"], "gain_in")

        wring = Ring([w[:, :] for w in wbuf])

        def load_w(src, nk, n):
            i, buf, free = wring.take()
            dst = buf[:, 0:nk * n].rearrange("p (k n) -> p k n", k=nk)
            tok = dma(dst, src.rearrange("(k p) n -> p k n", p=P128), f"w{i}_in", after=free)
            return i, dst, tok

        state = {"turn": 0}

        def copy_out(dst, src, after):
            state["turn"] ^= 1
            if state["turn"]:
                return V(lambda e: e.tensor_copy(dst, src), after)
            return S(lambda e: e.activation(dst, src, ACT.Copy), after)

        def mm(out, lhsT, rhs, start, stop, after=(), mark=False):
            return P(lambda e: e.matmul(out, lhsT, rhs, start=start, stop=stop), after, mark=mark)

        def tp(out, in_, k, after=(), mark=False):
            return P(lambda e: e.transpose(out, in_, ident[0:k, 0:k]), after, mark=mark)

        def rstd_of(ss, width, out, tmp, after=()):
            a, b, c = tmp
            V(lambda e: e.tensor_scalar(a, ss, 1.0 / width, EPS, ALU.mult, ALU.add), after)
            t = (V.key, V.count)
            t = S(lambda e: e.activation(b, a, ACT.Sqrt), [t])
            V(lambda e: e.reciprocal(c, b), [t])
            V(lambda e: e.tensor_tensor(c, a, c, ALU.mult))
            V(lambda e: e.tensor_tensor(c, b, c, ALU.add))
            V(lambda e: e.tensor_scalar(c, c, 0.5, None, ALU.mult))
            return V(lambda e: e.reciprocal(out, c))

        st_ss, st_a, st_b, st_c, st_r = (stat[:, 64 * i:64 * i + 64] for i in range(5))
        st_mx, st_nm, st_sum = stat[:, 320:352], stat[:, 352:384], stat[:, 384:416]
        st_x = stat[:, 416:512]

        def norm_rows(srcs, width, junk, after):
            for t in range(NT):
                tok = S(lambda e, t=t: e.activation(junk[:, 0:width], srcs[t], ACT.Square,
                                                    accum_out=st_ss[:, t:t + 1]), after)
            return rstd_of(st_ss[:, 0:NT], width, st_r[:, 0:NT], (st_a[:, 0:NT], st_b[:, 0:NT], st_c[:, 0:NT]), [tok])

        def to_T(src_t, nd, dst, gname, after, free=(), scale=None, tmp=None):
            toks = []
            last_tp = [[], []]
            for t in range(NT):
                src = src_t[t]
                tok_x = after
                if scale is not None:
                    x = tmp[t % 2][:, 0:nd * P128]
                    tok_x = [V(lambda e, t=t, x=x, src=src: e.tensor_scalar(x, src, scale[:, t:t + 1], None, ALU.mult),
                               list(after) + last_tp[t % 2])]
                    src = x
                for c0 in range(0, nd, 4):
                    n = min(4, nd - c0)
                    b, bank, bf = banks.take()
                    for c in range(n):
                        tk = tp(bank[:, c * 128:(c + 1) * 128], src[:, (c0 + c) * 128:(c0 + c + 1) * 128], 128,
                                list(tok_x) + bf + [t_con], mark=(c == n - 1))
                    out = dst[:, c0:c0 + n, t * 128:(t + 1) * 128]
                    inn = bank[:, 0:n * 128].rearrange("p (c t) -> p c t", c=n)
                    if gname is None:
                        tk2 = copy_out(out, inn, [tk] + list(free))
                    else:
                        g = gain[:, GC[gname] + c0:GC[gname] + c0 + n].unsqueeze(2).to_broadcast([P128, n, 128])
                        tk2 = V(lambda e, out=out, inn=inn, g=g: e.tensor_tensor(out, inn, g, ALU.mult),
                                [tk, t_gain] + list(free))
                    banks.free(b, [tk2])
                    toks.append(tk2)
                last_tp[t % 2] = [tk]
            return toks

        def norm_T(srcs, nd, gname, dst, junk, tmp, after, free=()):
            r = norm_rows(srcs, nd * P128, junk, after)
            return to_T(srcs, nd, dst, gname, list(after) + [r], free, st_r, tmp)

        def lin(xT, nk, wt, n, evict, after, n0=0, bias=None):
            for t in range(NT):
                b, bank, bf = banks.take()
                for k in range(nk):
                    tk = mm(bank[:, 0:n], xT[:, k, t * 128:(t + 1) * 128], wt[:, k, n0:n0 + n], k == 0,
                            k == nk - 1 and bias is None, list(after) + bf,
                            mark=(k == nk - 1 and bias is None))
                if bias is not None:
                    tk = mm(bank[:, 0:n], con[0:1, CC["head"]:CC["head"] + 128], bias, False, True, after, mark=True)
                banks.free(b, evict(t, bank, tk))
            return tk

        def rope(x1, x2, o1, o2, c, s, tmp, after=()):
            a, b, cc, d = tmp
            V(lambda e: e.tensor_tensor(a, x1, c, ALU.mult), after)
            V(lambda e: e.tensor_tensor(b, x2, s, ALU.mult), own=False)
            V(lambda e: e.tensor_tensor(cc, x2, c, ALU.mult), own=False)
            V(lambda e: e.tensor_tensor(d, x1, s, ALU.mult), own=False)
            V(lambda e: e.tensor_tensor(o1, a, b, ALU.subtract))
            return V(lambda e: e.tensor_tensor(o2, cc, d, ALU.add))

        SC, OB = (0, 1, 2, 3, 4, 5), (6, 7)

        def attend(heads, dv, qT, kT, v, bias, scale, width, Pb, PTb, done, after, prep=None):
            prob, ptr = Ring(Pb), Ring(PTb)
            units = [(qt, h) for qt in range(NT) for h in range(heads)]
            st, obank = {}, {}

            def scores(u):
                qt, h = units[u]
                w = width(qt)
                b, bank, bf = banks.take(SC)
                ex = prep(h) if prep and qt == 0 else []
                tk = mm(bank[:, 0:w], qT(h, qt), kT(h, w), True, True, list(after) + bf + ex, mark=True)
                i, pr, pf = prob.take()
                par = u % 4
                mx, nm = st_mx[:, par:par + 1], st_nm[:, par:par + 1]
                bb = bias(qt, w)
                if bb is None:
                    V(lambda e: e.tensor_reduce(mx, bank[:, 0:w], AX.X, ALU.max), [tk])
                    src = bank[:, 0:w]
                else:
                    V(lambda e: e.tensor_tensor_reduce(pr[:, 0:w], bank[:, 0:w], bb, 1.0, -3e38, ALU.add, ALU.max,
                                                       mx), [tk] + pf + list(after))
                    src = pr[:, 0:w]
                t2 = V(lambda e: e.tensor_scalar(nm, mx, -scale, None, ALU.mult),
                       st.get(("exp", u - 4), []))
                sm = st_sum[:, (qt % 2) * 8 + h:(qt % 2) * 8 + h + 1]
                t3 = S(lambda e: e.activation(pr[:, 0:w], src, ACT.Exp, bias=nm, scale=scale, accum_out=sm),
                       [t2] + pf + st.get(("sum", qt - 2), []))
                st["exp", u] = [t3]
                banks.free(b, [t2, t3])
                st[u] = (i, pr, t3)

            def turn(u):
                qt, h = units[u]
                w = width(qt)
                i, pr, t3 = st[u]
                b, bank, bf = banks.take(SC)
                for c in range(w // 128):
                    tk = tp(bank[:, c * 128:(c + 1) * 128], pr[:, c * 128:(c + 1) * 128], 128, [t3] + bf,
                            mark=(c == w // 128 - 1))
                prob.free(i, [tk])
                j, pt, ptf = ptr.take()
                t4 = copy_out(pt[:, 0:w], bank[:, 0:w], [tk] + ptf)
                banks.free(b, [t4])
                st[u] = (j, pt, t4)

            def pv(u):
                qt, h = units[u]
                w = width(qt)
                j, pt, t4 = st[u]
                if h == 0:
                    obank[qt] = banks.take(OB)
                b, bank, bf = obank[qt]
                n = w // 128
                for c in range(n):
                    tk = mm(bank[:, h * dv:(h + 1) * dv], pt[:, c * 128:(c + 1) * 128], v(h, c), c == 0, c == n - 1,
                            [t4] + bf, mark=(c == n - 1))
                ptr.free(j, [tk])
                if h == heads - 1:
                    tok = done(qt, bank, tk)
                    banks.free(b, [tok])
                    st["sum", qt] = [tok]
                    st["end"] = tok

            n = len(units)
            for i in range(n + 3):
                if i < n:
                    scores(i)
                if 2 <= i < n + 2:
                    turn(i - 2)
                if i >= 3:
                    pv(i - 3)
            return st["end"]

        def scaled_out(dst, heads, dv):
            def done(qt, bank, tk):
                sm = st_sum[:, (qt % 2) * 8:(qt % 2) * 8 + heads]
                r = st_x[:, 0:heads]
                V(lambda e: e.reciprocal(r, sm), [tk, (S.key, S.count)])
                return V(lambda e: e.tensor_tensor(dst(qt), bank[:, 0:heads * dv].rearrange("p (h d) -> p h d", h=heads),
                                                   r.unsqueeze(2).to_broadcast([P128, heads, dv]), ALU.mult), [tk])
            return done

        def finish_with(src, after):
            t = dma(A["out"].rearrange("(t p) d -> p t d", p=P128), src, "out_st", after=after)
            Q(lambda e: e.nop(), [t])

        all_done = lambda: [(E.key, E.count) for E in (P, V, S, G) if E.count]

        junk = ar(28000, 1024)
        xtmp = [ar(0, 1024), ar(1024, 1024)]

        xt = norm_T([H[:, t, :] for t in range(NT)], ND, "g_mix", XT, junk, xtmp, [t_h])
        lat = ar(2048, 4 * 672).rearrange("p (t n) -> p t n", t=NT)
        qkvd = ar(4736, 4 * 1536).rearrange("p (t n) -> p t n", t=NT)

        def to_proj(c0, n):
            def ev(t, bank, tk):
                toks = []
                for lo, hi, dst, off in ((0, 672, lat, 0), (672, IN1, qkvd, 672)):
                    a, b = max(lo, c0), min(hi, c0 + n)
                    if a < b:
                        toks.append(copy_out(dst[:, t, a - off:b - off], bank[:, a - c0:b - c0], [tk] + toks))
                return toks
            return ev

        for c0 in range(0, IN1, 512):
            n = min(512, IN1 - c0)
            i, wt, tw = load_w(A["w_in"][:, c0:c0 + n], ND, n)
            t = lin(XT, ND, wt, n, to_proj(c0, n), xt + [tw])
            wring.free(i, [t])
        proj_done = [(V.key, V.count), (S.key, S.count)]
        cqT, ckvT = XT[:, 0:3, :], XT[:, 3:5, :]
        xfree = [(P.key, P.count)]
        a = norm_T([lat[:, t, 0:QR] for t in range(NT)], 3, "g_cq", cqT, junk, xtmp, proj_done, xfree)
        b_ = norm_T([lat[:, t, QR:QR + KVR] for t in range(NT)], 2, "g_ckv", ckvT, junk, xtmp,
                    [(P.key, P.count)], xfree)
        qtok = ar(10880, NT * 768).rearrange("p (t n) -> p t n", t=NT)
        ktok = ar(13952, NT * 768).rearrange("p (t n) -> p t n", t=NT)
        vtok = ar(17024, NT * 512).rearrange("p (t n) -> p t n", t=NT)
        i, wt, tw = load_w(A["w_uq"], 3, 768)
        for c in range(2):
            t = lin(cqT, 3, wt, 384, lambda t, bank, tk, c=c: [copy_out(qtok[:, t, c * 384:(c + 1) * 384],
                                                                       bank[:, 0:384], [tk])], a + [tw], n0=c * 384)
        wring.free(i, [t])
        i, wt, tw = load_w(A["w_ukv"], 2, 1024)

        def ev_kv(c):
            def ev(t, bank, tk):
                src = bank[:, :].rearrange("p (h x) -> p h x", h=4)
                kd = ktok[:, t, c * 384:(c + 1) * 384].rearrange("p (h x) -> p h x", h=4)[:, :, 0:64]
                vd = vtok[:, t, c * 256:(c + 1) * 256].rearrange("p (h x) -> p h x", h=4)
                t1 = V(lambda e: e.tensor_copy(kd, src[:, :, 0:64]), [tk])
                return [t1, S(lambda e: e.activation(vd, src[:, :, 64:128], ACT.Copy), [tk, t1])]
            return ev
        for c in range(2):
            t = lin(ckvT, 2, wt, 512, ev_kv(c), b_ + [tw], n0=c * 512)
        wring.free(i, [t])
        both = [(V.key, V.count), (S.key, S.count)]
        rtmp = [ar(19072 + 512 * j, 512) for j in range(4)]

        def cs(name, half, nh):
            v = con[:, CC[name]:CC[name] + NT * half].rearrange("p (t r) -> p t r", t=NT)
            return v.unsqueeze(2).to_broadcast([P128, NT, nh, half])

        def rv(x, nh, hd, lo, half):
            return x.rearrange("p t (h x) -> p t h x", h=nh)[:, :, :, lo:lo + half]

        def rt(nh, half):
            return [r[:, 0:NT * nh * half].rearrange("p (t h x) -> p t h x", t=NT, h=nh) for r in rtmp]
        q1, q2 = rv(qtok, 8, QK, 64, 16), rv(qtok, 8, QK, 80, 16)
        rope(q1, q2, q1, q2, cs("cos_m", 16, 8), cs("sin_m", 16, 8), rt(8, 16), both)
        k1, k2 = (lat[:, :, 640 + 16 * j:656 + 16 * j].unsqueeze(2) for j in range(2))
        rope(k1, k2, k1, k2, cs("cos_m", 16, 1), cs("sin_m", 16, 1), rt(1, 16))
        for t in range(NT):
            V(lambda e, t=t: e.tensor_copy(
                ktok[:, t, :].rearrange("p (h x) -> p h x", h=8)[:, :, 64:96],
                lat[:, t, 640:672].unsqueeze(1).to_broadcast([P128, 8, 32])))
        for off in (0, 512):
            x = qkvd[:, :, off:off + 512]
            x1, x2 = rv(x, 8, 64, 0, 8), rv(x, 8, 64, 8, 8)
            roped = rope(x1, x2, x1, x2, cs("cos_d", 8, 8), cs("sin_d", 8, 8), rt(8, 8))
        lat_free = (P.key, P.count)

        def heads_T(tok, nh, hd, dst, after, free):
            toks = []
            for j in range(nh):
                b, bank, bf = banks.take()
                for t in range(NT):
                    tk = tp(bank[0:hd, t * 128:(t + 1) * 128], tok[:, t, j * hd:(j + 1) * hd], 128,
                            list(after) + bf, mark=(t == NT - 1))
                tk2 = copy_out(dst[0:hd, j, :], bank[0:hd, :], [tk] + list(free))
                banks.free(b, [tk2])
                toks.append(tk2)
            return toks[-2:]

        mixed = ar(24640, 4096).rearrange("p (t n) -> p t n", t=NT)
        qT = XT
        tq = heads_T(qtok, 8, QK, qT, [roped], [lat_free])
        tk_ = heads_T(ktok, 8, QK, ar(19072, 4096).rearrange("p (h t) -> p h t", h=8), [roped], [roped])
        kT = ar(19072, 4096).rearrange("p (h t) -> p h t", h=8)
        used = (P.key, P.count)
        Pb = [ar(10880 + 512 * j, 512) for j in range(4)]
        PTb = [ar(12928 + 512 * j, 512) for j in range(3)]
        end = attend(8, 64, lambda h, qt: qT[0:QK, h, qt * 128:(qt + 1) * 128], lambda h, w: kT[0:QK, h, 0:w],
                     lambda h, c: vtok[:, c, h * 64:(h + 1) * 64], lambda qt, w: None, QK ** -0.5, lambda qt: T,
                     Pb, PTb, scaled_out(lambda qt: mixed[:, qt, 0:512].rearrange("p (h d) -> p h d", h=8), 8, 64),
                     tq + tk_ + [used])
        mla_end = [end, (P.key, P.count)]
        dbias = ar(17024, 2048).rearrange("p (t n) -> p t n", t=NT)
        tb = dma(dbias, A["dil_bias"].rearrange("(t p) k -> p t k", p=P128), "dbias_in", after=mla_end)
        qTd, kTd = XT[:, 0:4, :], XT[:, 4:8, :]
        tq = heads_T(qkvd[:, :, 0:512], 4, 128, qTd, [roped], mla_end)
        tk_ = heads_T(qkvd[:, :, 512:1024], 4, 128, kTd, [roped], mla_end)
        hp = lambda h: slice(64 * (h % 2), 64 * (h % 2) + 64)
        end = attend(8, 64, lambda h, qt: qTd[hp(h), h // 2, qt * 128:(qt + 1) * 128],
                     lambda h, w: kTd[hp(h), h // 2, 0:w],
                     lambda h, c: qkvd[:, c, 1024 + h * 64:1088 + h * 64], lambda qt, w: dbias[:, qt, 0:w], 0.125,
                     lambda qt: T, Pb, PTb,
                     scaled_out(lambda qt: mixed[:, qt, 512:1024].rearrange("p (h d) -> p h d", h=8), 8, 64),
                     tq + tk_ + [tb])
        att_end = [end, (P.key, P.count)]
        for half in range(2):
            mt = norm_T([mixed[:, t, half * 512:(half + 1) * 512] for t in range(NT)], 4, None,
                        XT[:, 4 * half:4 * half + 4, :], ar(4736, 1024), xtmp, att_end + [(P.key, P.count)], att_end)
            g = gain[:, GC["g_out"] + 4 * half:GC["g_out"] + 4 * half + 4].unsqueeze(2).to_broadcast([P128, 4, T])
            xs = XT[:, 4 * half:4 * half + 4, :]
            tm = V(lambda e, g=g, xs=xs: e.tensor_tensor(xs, xs, g, ALU.mult), mt)

        def add_h(c):
            def ev(t, bank, tk):
                dst = H[:, t, c * 512:(c + 1) * 512]
                return [V(lambda e: e.tensor_tensor(dst, bank[:, :], dst, ALU.add), [tk])]
            return ev
        for c in range(2):
            i, wt, tw = load_w(A["w_out"][:, c * 512:(c + 1) * 512], ND, 512)
            t = lin(XT, ND, wt, 512, add_h(c), [tm, tw])
            wring.free(i, [t])
        if stop == "attn1":
            finish_with(H, all_done())
            return emit_all(nc, ctx, sem_names, P, V, S, G, Q)

        xt = norm_T([H[:, t, :] for t in range(NT)], ND, "g_ffn", XT, junk, xtmp, all_done(), all_done())
        qpT = ar(2048, 4096).rearrange("p (h t) -> p h t", h=PH)
        kbd = ar(6144, 256)
        t_kbd = dma(kbd, A["peer_keys"], "kbd_in", after=all_done())
        qtoks = []
        for c in range(2):
            i, wt, tw = load_w(A["w_peer_q"][:, c * 512:(c + 1) * 512], ND, 512)
            for j in range(4):
                b, bank, bf = banks.take()
                for k in range(ND):
                    tk = mm(bank[:, :], wt[:, k, j * 128:(j + 1) * 128], XT[:, k, :], k == 0, k == ND - 1,
                            xt + bf + [tw], mark=(k == ND - 1))
                t2 = copy_out(qpT[:, 4 * c + j, :], bank[:, :], [tk])
                banks.free(b, [t2])
                qtoks.append(t2)
            wring.free(i, [tk])
        qtoks = qtoks[-2:]
        sc = ar(6400, 2048).rearrange("p (l k) -> p l k", l=16)
        s2 = ar(8448, 2048).rearrange("p (l k) -> p l k", l=16)
        v16 = ar(10496, 256).rearrange("p (l k) -> p l k", l=16)
        i16 = ar(10752, 256).bitcast(U32).rearrange("p (l k) -> p l k", l=16)
        i16f = ar(11008, 256).rearrange("p (l k) -> p l k", l=16)
        cand = ar(11264, 2048).rearrange("p (h c) -> p h c", h=8)
        cnd2 = ar(13312, 2048).rearrange("p (h c) -> p h c", h=8)
        top = ar(15360, 128).rearrange("p (h k) -> p h k", h=8)
        pos = ar(15488, 128).bitcast(U32).rearrange("p (h k) -> p h k", h=8)
        pj = [ar(15616 + 128 * j, 128).bitcast(U32) for j in range(2)]
        pf = [ar(15872 + 128 * j, 128) for j in range(2)]
        sel = [ar(16128 + 128 * j, 128) for j in range(3)]
        selT = [ar(16512 + 512 * j, 512) for j in range(3)]
        iota16 = con[:, CC["iota16"]:CC["iota16"] + 16].unsqueeze(1).to_broadcast([P128, 128, 16])

        def top16(vals, idx, src, work, after=()):
            V(lambda e: e.max(vals[:, 0:8], src), after)
            V(lambda e: e.max_index(idx[:, 0:8], vals[:, 0:8], src))
            V(lambda e: e.match_replace(work, vals[:, 0:8], src, TAKEN), own=False)
            V(lambda e: e.max(vals[:, 8:16], work))
            return V(lambda e: e.max_index(idx[:, 8:16], vals[:, 8:16], work))

        def choose(t):
            for hh in range(4):
                b, bank, bf = banks.take()
                for j in range(2):
                    tk = mm(bank[:, j * 256:(j + 1) * 256], qpT[:, 2 * hh + j, t * 128:(t + 1) * 128], kbd, True, True,
                            qtoks + [t_kbd] + bf, mark=(j == 1))
                t2 = S(lambda e, hh=hh, bank=bank: e.activation(
                    sc[:, 4 * hh:4 * hh + 4, :].rearrange("p l k -> p (l k)"), bank[:, :], ACT.Copy),
                    [tk, (V.key, V.count)])
                banks.free(b, [t2])
            for l in range(16):
                top16(v16[:, l, :], i16[:, l, :], sc[:, l, :], s2[:, l, :], [t2])
            V(lambda e: e.tensor_copy(i16f.rearrange("p l k -> p (l k)"), i16.rearrange("p l k -> p (l k)")))
            vv = v16.rearrange("p (h s) k -> p h s k", s=2)
            V(lambda e: e.tensor_tensor(cand.rearrange("p h (a b) -> p h a b", a=16),
                                        vv[:, :, 0, :].unsqueeze(3).to_broadcast([P128, 8, 16, 16]),
                                        vv[:, :, 1, :].unsqueeze(2).to_broadcast([P128, 8, 16, 16]), ALU.add))
            for h in range(8):
                top16(top[:, h, :], pos[:, h, :], cand[:, h, :], cnd2[:, h, :])
            posf = pos.rearrange("p h k -> p (h k)")
            V(lambda e: e.tensor_scalar(pj[0], posf, 4, None, ALU.logical_shift_right))
            V(lambda e: e.tensor_scalar(pj[1], posf, 15, None, ALU.bitwise_and))
            for j in range(2):
                V(lambda e, j=j: e.tensor_copy(pf[j], pj[j]))
                eq = s2.rearrange("p l k -> p (l k)").rearrange("p (a b) -> p a b", b=16)
                V(lambda e, j=j: e.tensor_tensor(eq, pf[j].unsqueeze(2).to_broadcast([P128, 128, 16]), iota16,
                                                 ALU.is_equal))
                eq4 = s2.rearrange("p l k -> p (l k)").rearrange("p (h a b) -> p h a b", h=8, b=16)
                iv = i16f.rearrange("p (h s) k -> p h s k", s=2)[:, :, j, :].unsqueeze(2).to_broadcast([P128, 8, 16, 16])
                V(lambda e, eq4=eq4, iv=iv: e.tensor_tensor(eq4, eq4, iv, ALU.mult))
                V(lambda e, j=j, eq=eq: e.tensor_reduce(sel[j], eq, AX.X, ALU.add), [(P.key, P.count)])
            gt = sel[2].rearrange("p (h k) -> p h k", h=8)
            t1 = V(lambda e: e.tensor_tensor(gt, top, top[:, :, 0:1].to_broadcast([P128, 8, 16]), ALU.subtract),
                   [(P.key, P.count)])
            t1 = S(lambda e: e.activation(gt, gt, ACT.Exp), [t1])
            V(lambda e: e.tensor_reduce(st_x[:, 8:16], gt, AX.X, ALU.add), [t1])
            V(lambda e: e.reciprocal(st_x[:, 8:16], st_x[:, 8:16]))
            t1 = V(lambda e: e.tensor_tensor(gt, gt, st_x[:, 8:16].unsqueeze(2).to_broadcast([P128, 8, 16]), ALU.mult))
            b, bank, bf = banks.take()
            for j in range(3):
                tk = tp(bank[:, j * 128:(j + 1) * 128], sel[j], 128, [t1] + bf, mark=(j == 2))
            for j in range(3):
                t2 = V(lambda e, j=j, t=t: e.tensor_copy(selT[j][:, t * 128:(t + 1) * 128],
                                                         bank[:, j * 128:(j + 1) * 128]), [tk])
            banks.free(b, [t2])
        for t in range(NT):
            choose(t)
        TB = 64
        gs = Ring([ar(18048, 8192)])
        ohr = Ring([(ar(2048 + 1024 * j, 512), ar(2560 + 1024 * j, 512)) for j in range(4)])
        iota = con[:, 128:256]
        stores = []
        for tb in range(T // TB):
            si, gbuf, gfree = gs.take()
            g3 = gbuf.rearrange("p (i t) -> p i t", t=TB)
            for q in range(TB // 4):
                oi, (oh2, oh1), ofree = ohr.take()
                for j in range(4):
                    tt = tb * TB + q * 4 + j
                    V(lambda e, tt=tt, j=j, oh2=oh2: e.tensor_scalar(
                        oh2[:, j * 128:(j + 1) * 128], iota, selT[1][:, tt:tt + 1], None, ALU.is_equal),
                      ofree, own=(j == 0 and q == 0))
                    tv = V(lambda e, tt=tt, j=j, oh1=oh1: e.tensor_scalar(
                        oh1[:, j * 128:(j + 1) * 128], iota, selT[0][:, tt:tt + 1], selT[2][:, tt:tt + 1],
                        ALU.is_equal, ALU.mult), ofree, own=False)
                b, bank, bf = banks.take()
                for j in range(4):
                    tk = mm(bank[:, j * 128:(j + 1) * 128], oh2[:, j * 128:(j + 1) * 128],
                            oh1[:, j * 128:(j + 1) * 128], True, True, [tv] + bf, mark=(j == 3))
                ohr.free(oi, [tk])
                out = g3[:, :, q * 4:q * 4 + 4].rearrange("p i t -> p t i")
                t2 = S(lambda e, out=out, bank=bank: e.activation(out, bank[:, :].rearrange("p (t i) -> p t i", t=4),
                                                                  ACT.Copy), [tk] + gfree, own=False)
                banks.free(b, [t2])
            ts = dma(g_scratch[:, :, tb * TB:(tb + 1) * TB].rearrange("a b t -> b a t"), g3, "g_st", after=[t2])
            gs.free(si, [ts])
            stores = [ts]
        wT = [ar(2048 + 8192 * j, 8192).rearrange("p (e t) -> p e t", e=ETG) for j in range(2)]
        act_b = Ring([ar(18432 + 512 * j, 512) for j in range(3)])
        gring = Ring([ar(19968 + 2048 * j, 2048) for j in range(3)])
        wT_free = [[], []]
        peer_begin = all_done() + stores
        ngroups = KEYS // ETG

        def up(g):
            toks = []
            for u in range(ETG // 4):
                e0 = g * ETG + 4 * u
                gi, gb, gf = gring.take()
                gv = gb.rearrange("p (i t) -> p i t", t=T)
                i, wt, tw = load_w(A["peer_uT"][:, e0 * 128:(e0 + 4) * 128], ND, 512)
                tg = dma(gv, g_scratch[e0:e0 + 4, :, :].rearrange("a b t -> b a t"), f"g{gi}_in",
                         after=gf + peer_begin)
                for j in range(4):
                    b, bank, bf = banks.take()
                    for k in range(ND):
                        tk = mm(bank[:, :], wt[:, k, j * 128:(j + 1) * 128], XT[:, k, :], k == 0, k == ND - 1,
                                bf + [tw], mark=(k == ND - 1))
                    ai, ab, af = act_b.take()
                    t1 = S(lambda e, ab=ab, bank=bank: e.activation(ab, bank[:, :], ACT.Gelu), [tk] + af + peer_begin,
                           own=False)
                    banks.free(b, [t1])
                    t2 = V(lambda e, ab=ab, gv=gv, j=j, u=u: e.tensor_tensor(
                        wT[g % 2][:, 4 * u + j, :], ab, gv[:, j, :], ALU.mult), [t1, tg] + wT_free[g % 2], own=False)
                    act_b.free(ai, [t2])
                    toks = [t2]
                wring.free(i, [tk])
                gring.free(gi, [t2])
            return toks

        def down(g, ready):
            for c in range(2):
                bb = [banks.take() for _ in range(4)]
                for half in range(2):
                    e0 = (g * ETG + 8 * half) * 128
                    i, wt, tw = load_w(A["peer_v"][e0:e0 + 1024, c * 512:(c + 1) * 512], 8, 512)
                    for e in range(8):
                        for t in range(NT):
                            tk = mm(bb[t][1][:, :], wT[g % 2][:, 8 * half + e, t * 128:(t + 1) * 128], wt[:, e, :],
                                    half == 0 and e == 0, half == 1 and e == 7,
                                    [tw] + ready + (bb[t][2] if half == 0 and e == 0 else []),
                                    mark=(e == 7 and t == 3))
                    wring.free(i, [tk])
                for t in range(NT):
                    dst = H[:, t, c * 512:(c + 1) * 512]
                    t2 = V(lambda e, t=t, dst=dst, bb=bb: e.tensor_tensor(dst, bb[t][1][:, :], dst, ALU.add), [tk],
                           own=False)
                    banks.free(bb[t][0], [t2])
            wT_free[g % 2] = [tk]

        nxt = up(0)
        for g in range(ngroups):
            ready = nxt
            if g + 1 < ngroups:
                nxt = up(g + 1)
            down(g, ready)
        if stop == "peer":
            finish_with(H, all_done())
            return emit_all(nc, ctx, sem_names, P, V, S, G, Q)

        def ple(gname, w_gate, w_proj, pT_src, bias_src, after):
            pT = ar(2048, 1024).rearrange("p (k t) -> p k t", k=2)
            br = ar(3072, 1024)
            t_p = dma(pT, pT_src.rearrange("(k p) t -> p k t", p=P128), "pT_in", after=after)
            if bias_src is not None:
                t_b = dma(br[0:1, :], bias_src, "bias_in", after=after)
            sg = Ring([ar(4096 + 512 * j, 512) for j in range(4)])
            xt = norm_T([H[:, t, :] for t in range(NT)], ND, gname, XT, junk, xtmp, after, after)
            for c in range(2):
                gates = {}
                i, wt, tw = load_w(w_gate[:, c * 512:(c + 1) * 512], ND, 512)

                def ev_gate(t, bank, tk):
                    si, buf, f = sg.take()
                    t1 = S(lambda e: e.activation(buf, bank[:, :], ACT.Sigmoid), [tk] + f + list(after))
                    gates[t] = (si, buf, t1)
                    return [t1]
                t_ = lin(XT, ND, wt, 512, ev_gate, xt + [tw] + ([t_b] if bias_src is not None else []),
                         bias=None if bias_src is None else br[0:1, c * 512:(c + 1) * 512])
                wring.free(i, [t_])
                i, wt, tw = load_w(w_proj[:, c * 512:(c + 1) * 512], 2, 512)

                def ev_proj(t, bank, tk):
                    si, buf, t1 = gates[t]
                    dst = H[:, t, c * 512:(c + 1) * 512]
                    t2 = V(lambda e: e.tensor_tensor(buf, bank[:, :], buf, ALU.mult), [tk, t1])
                    t3 = V(lambda e: e.tensor_tensor(dst, dst, buf, ALU.add))
                    sg.free(si, [t3])
                    return [t2]
                t_ = lin(pT, 2, wt, 512, ev_proj, [t_p, tw])
                wring.free(i, [t_])

        ple("g_ple", A["w_ple_gate"], A["w_ple_proj"], A["pT"], None, all_done())
        gf = ar(6144, 1024)
        t_gf = dma(gf, A["rows"][:, 0:1024], "gf_in", after=all_done())
        r = norm_rows([H[:, t, :] for t in range(NT)], D, junk, all_done())
        for t in range(NT):
            V(lambda e, t=t: e.scalar_tensor_tensor(H[:, t, :], H[:, t, :], st_r[:, t:t + 1], gf, ALU.mult, ALU.mult),
              [r, t_gf])
        if stop == "block1":
            finish_with(H, all_done())
            return emit_all(nc, ctx, sem_names, P, V, S, G, Q)

        pos_i = ar(2048, 4).bitcast(I32)
        cos2, sin2 = stat_rope[:, 0:32], stat_rope[:, 32:64]
        posf2, ang, turns, red, over = ar(2056, 4), ar(2064, 32), ar(2096, 32), ar(2128, 32), ar(2160, 32)
        begin = all_done()
        t_pos = dma(pos_i, A["pos"], "pos_in", after=begin)
        V(lambda e: e.tensor_copy(posf2, pos_i), [t_pos] + begin)
        V(lambda e: e.tensor_tensor(ang.rearrange("p (t r) -> p t r", t=NT),
                                    posf2.unsqueeze(2).to_broadcast([P128, NT, 8]),
                                    cst("inv", 8).unsqueeze(1).to_broadcast([P128, NT, 8]), ALU.mult))
        MAGIC = 12582912.0
        C1, C2 = 6.28125, 0.0019350051879882812
        C3 = 2 * np.pi - C1 - C2
        V(lambda e: e.tensor_scalar(turns, ang, float(1 / (2 * np.pi)), MAGIC, ALU.mult, ALU.add))
        V(lambda e: e.tensor_scalar(turns, turns, MAGIC, None, ALU.subtract))
        V(lambda e: e.scalar_tensor_tensor(red, turns, -C1, ang, ALU.mult, ALU.add))
        V(lambda e: e.scalar_tensor_tensor(red, turns, -C2, red, ALU.mult, ALU.add))
        V(lambda e: e.scalar_tensor_tensor(red, turns, float(-C3), red, ALU.mult, ALU.add))
        PI_LO = 3.1415925
        V(lambda e: e.tensor_scalar(ang, red, PI_LO, -PI_LO, ALU.min, ALU.max))
        V(lambda e: e.tensor_scalar(red, red, float(np.pi / 2), None, ALU.add))
        V(lambda e: e.tensor_scalar(over, red, float(np.pi), float(-2 * np.pi), ALU.is_gt, ALU.mult))
        V(lambda e: e.tensor_tensor(red, red, over, ALU.add))
        t_r = V(lambda e: e.tensor_scalar(red, red, PI_LO, -PI_LO, ALU.min, ALU.max))
        S(lambda e: e.activation(sin2, ang, ACT.Sin), [t_r])
        t_rope = S(lambda e: e.activation(cos2, red, ACT.Sin))

        def cs2(x, nh):
            return x.rearrange("p (t r) -> p t r", t=NT).unsqueeze(2).to_broadcast([P128, NT, nh, 8])

        mask = lambda qt: cst("causal", 512)[:, (3 - qt) * 128:512]
        before = lambda rt: cst("before", 512)[:, (3 - rt) * 128:512]
        ones = cst("before", 128)
        causal_w = lambda qt: (qt + 1) * 128

        def layer(l):
            begin = all_done()
            tok = ar(2048, NT * 592).rearrange("p (t n) -> p t n", t=NT)
            mv = ar(4416, 2048).rearrange("p (t n) -> p t n", t=NT)
            mo = ar(6464, 2048).rearrange("p (t n) -> p t n", t=NT)
            raw = ar(8512, 4128).rearrange("p (c n) -> p c n", c=8)
            qk = ar(12640, 4096).rearrange("p (c n) -> p c n", c=8)
            aq = ar(16736, 2048).rearrange("p (t n) -> p t n", t=NT)
            iq = ar(18784, 2048).rearrange("p (t n) -> p t n", t=NT)
            score = ar(16736, 2048).rearrange("p (t n) -> p t n", t=NT)
            sbias = ar(18784, 2048).rearrange("p (t n) -> p t n", t=NT)
            kT = ar(20832, 1024).rearrange("p (g n) -> p g n", g=2)
            ikT = ar(21856, 512)
            kdup = ar(22368, 1024).rearrange("p (t g u d) -> p t g u d", t=NT, g=2, u=2)
            ikdup = ar(23392, 512).rearrange("p (t u d) -> p t u d", t=NT, u=2)
            work = ar(23904, 512)
            Pb = [ar(24416 + 512 * j, 512) for j in range(4)]
            PTb = [ar(26464 + 512 * j, 512) for j in range(3)]
            iT = ar(28000, 512)
            mixed = ar(8512, 4096).rearrange("p (t n) -> p t n", t=NT)
            lfb = Ring([ar(896 * j, 896) for j in range(2)])
            small = ar(29024, 256)
            W = A["w_in_2"][l]
            t_row = dma(row[:, :], A["rows"][:, 1024 + 208 * l:1232 + 208 * l], "row_in", after=begin)
            xt = norm_T([H[:, t, :] for t in range(NT)], ND, f"g_mix_{l}", XT, junk, xtmp, begin, begin)
            i, wt, tw = load_w(W[:, 0:512], ND, 512)
            t = lin(XT, ND, wt, 512, lambda t, bank, tk: [copy_out(tok[:, t, 0:512], bank[:, :], [tk])], xt + [tw])
            wring.free(i, [t])
            i, buf, fr = wring.take()
            wt = buf[:, 0:640].rearrange("p (k n) -> p k n", k=ND)
            dma(wt[:, :, 0:72], W[:, 512:584].rearrange("(k p) n -> p k n", p=P128), f"w{i}_in", after=fr)
            tw = dma(wt[:, :, 72:80], W[:, 2632:2640].rearrange("(k p) n -> p k n", p=P128), f"w{i}_in", after=fr)
            t = lin(XT, ND, wt, 80, lambda t, bank, tk: [copy_out(tok[:, t, 512:592], bank[:, 0:80], [tk])], [tw])
            wring.free(i, [t])
            tok_done = [(V.key, V.count), (S.key, S.count)]
            t_z = V(lambda e: e.memset(raw[:, :, 0:3], 0.0))
            for c in range(2):
                i, wt, tw = load_w(W[:, 584 + 512 * c:1096 + 512 * c], ND, 512)
                for j in range(4):
                    b, bank, bf = banks.take()
                    for k in range(ND):
                        tk = mm(bank[:, :], wt[:, k, j * 128:(j + 1) * 128], XT[:, k, :], k == 0, k == ND - 1,
                                bf + [tw], mark=(k == ND - 1))
                    banks.free(b, [copy_out(raw[:, 4 * c + j, 3:515], bank[:, :], [tk])])
                wring.free(i, [tk])
            raw_done = [(V.key, V.count), (S.key, S.count)]
            i, wt, tw = load_w(W[:, 1608:2120], ND, 512)
            t = lin(XT, ND, wt, 512, lambda t, bank, tk: [copy_out(mv[:, t, :], bank[:, :], [tk])], [tw])
            wring.free(i, [t])
            i, wt, tw = load_w(W[:, 2120:2632], ND, 512)
            t_x = lin(XT, ND, wt, 512, lambda t, bank, tk: [S(lambda e: e.activation(
                mo[:, t, :], bank[:, :], ACT.Sigmoid), [tk])], [tw])
            wring.free(i, [t_x])
            cq = norm_T([tok[:, t, 0:256] for t in range(NT)], 2, f"g_cq_{l}", XT[:, 0:2, :], junk, xtmp,
                        tok_done, [t_x])
            for name, dst in (("w_q_up_2", aq), ("w_iq_up_2", iq)):
                i, wt, tw = load_w(A[name][l], 2, 512)
                t_q = lin(XT, 2, wt, 512, lambda t, bank, tk, dst=dst: [copy_out(dst[:, t, :], bank[:, :], [tk])],
                          cq + [tw])
                wring.free(i, [t_q])
            q_done = [(V.key, V.count), (S.key, S.count)]
            for c in range(8):
                for j in range(4):
                    g = gain[:, GC[f"conv_w_{l}"] + 8 * j + c:GC[f"conv_w_{l}"] + 8 * j + c + 1]
                    o, x = qk[:, c, :], raw[:, c, j:j + 512]
                    if j == 0:
                        V(lambda e, o=o, x=x, g=g: e.tensor_scalar(o, x, g, None, ALU.mult), raw_done)
                    else:
                        tv = V(lambda e, o=o, x=x, g=g: e.scalar_tensor_tensor(o, x, g, o, ALU.mult, ALU.add))
                bcol = gain[:, GC[f"conv_b_{l}"] + c:GC[f"conv_b_{l}"] + c + 1]
                t_qk = S(lambda e, o=o, bcol=bcol: e.activation(o, o, ACT.Silu, bias=bcol), [tv])

            def head_norm(x, nh, gname, after):
                sq = ar(24416 + 1024, NT * nh * 64).rearrange("p (t h d) -> p t h d", t=NT, h=nh)
                n = NT * nh
                V(lambda e: e.tensor_tensor(sq, x, x, ALU.mult), after)
                V(lambda e: e.tensor_reduce(st_ss[:, 0:n].rearrange("p (t h) -> p t h", t=NT), sq, AX.X, ALU.add))
                rstd_of(st_ss[:, 0:n], 64, st_r[:, 0:n], (st_a[:, 0:n], st_b[:, 0:n], st_c[:, 0:n]))
                r = st_r[:, 0:n].rearrange("p (t h) -> p t h", t=NT).unsqueeze(3).to_broadcast([P128, NT, nh, 64])
                V(lambda e: e.tensor_tensor(x, x, r, ALU.mult))
                g = row[:, RC[f"{gname}_0"] - 1024:RC[f"{gname}_0"] - 1024 + 64]
                g = g.unsqueeze(1).unsqueeze(1).to_broadcast([P128, NT, nh, 64])
                V(lambda e: e.tensor_tensor(x, x, g, ALU.mult), [t_row])

            def head_rope(x, nh, after=()):
                tm = [ar(24416 + 256 * j, 256)[:, 0:NT * nh * 8].rearrange("p (t h x) -> p t h x", t=NT, h=nh)
                      for j in range(4)]
                x1, x2 = x[:, :, :, 0:8], x[:, :, :, 8:16]
                return rope(x1, x2, x1, x2, cs2(cos2, nh), cs2(sin2, nh), tm, list(after) + [t_rope])
            x_iq = iq.rearrange("p t (h d) -> p t h d", h=8)
            x_ik = tok[:, :, 512:576].unsqueeze(2)
            x_aq = aq.rearrange("p t (h d) -> p t h d", h=8)
            x_ak = tok[:, :, 256:384].rearrange("p t (h d) -> p t h d", h=2)
            head_rope(x_iq, 8, q_done + tok_done)
            head_norm(x_ik, 1, "g_ik", [])
            head_rope(x_ik, 1)
            head_norm(x_aq, 8, "g_qn", [])
            head_rope(x_aq, 8)
            head_norm(x_ak, 2, "g_kn", [])
            head_rope(x_ak, 2)
            iw = tok[:, :, 576:584]
            V(lambda e: e.tensor_scalar(iw, iw, IDX_SCALE, None, ALU.mult))
            for u in range(2):
                V(lambda e, u=u: e.tensor_copy(ikdup[:, :, u, :], tok[:, :, 512:576]))
                prep = V(lambda e, u=u: e.tensor_copy(kdup[:, :, :, u, :], x_ak))
            xfree = [t_q]
            iqT, aqT = XT[:, 0:4, :], XT[:, 4:8, :]
            t1 = heads_T(iq, 4, 128, iqT, [prep], xfree)
            t2 = heads_T(ikdup.rearrange("p t u d -> p t (u d)"), 1, 128, ikT.unsqueeze(1), [prep], begin)
            t3 = heads_T(aq, 4, 128, aqT, [prep], xfree)
            t4 = heads_T(kdup.rearrange("p t g u d -> p t (g u d)"), 2, 128, kT, [prep], begin)
            turned = t1 + t2 + t3 + t4
            used = [(P.key, P.count)] + turned
            rel = Ring(Pb)
            for qt in range(NT):
                w = causal_w(qt)
                for h in range(8):
                    b, bank, bf = banks.take()
                    tk = mm(bank[:, 0:w], iqT[hp(h), h // 2, qt * 128:(qt + 1) * 128], ikT[hp(h), 0:w], True, True,
                            turned + bf, mark=True)
                    ri, rb, rf = rel.take()
                    t1 = S(lambda e, rb=rb, bank=bank, w=w: e.activation(rb[:, 0:w], bank[:, 0:w], ACT.Relu),
                           [tk] + rf + used, own=False)
                    banks.free(b, [t1])
                    sc_, wc = score[:, qt, 0:w], iw[:, qt, h:h + 1]
                    if h == 0:
                        t2 = V(lambda e, rb=rb, w=w, sc_=sc_, wc=wc: e.tensor_scalar(sc_, rb[:, 0:w], wc, None, ALU.mult),
                               [t1] + used)
                    else:
                        t2 = V(lambda e, rb=rb, w=w, sc_=sc_, wc=wc: e.scalar_tensor_tensor(
                            sc_, rb[:, 0:w], wc, sc_, ALU.mult, ALU.add), [t1])
                    rel.free(ri, [t2])
            gates = tok[:, :, 584:592]
            ifb = row[:, 192:200].unsqueeze(1).to_broadcast([P128, NT, 8])
            V(lambda e: e.tensor_tensor(gates, gates, ifb, ALU.add), [t_row])
            lf = small[:, 0:16].rearrange("p (t h) -> p t h", t=NT)
            ex = small[:, 16:32].rearrange("p (t h) -> p t h", t=NT)
            mn = small[:, 32:48].rearrange("p (t h) -> p t h", t=NT)
            cumF = small[:, 48:64].rearrange("p (t h) -> p t h", t=NT)
            S(lambda e: e.activation(ex, gates[:, :, 4:8], ACT.Abs), [(V.key, V.count)])
            S(lambda e: e.activation(ex, ex, ACT.Exp, scale=-1.0))
            t1 = S(lambda e: e.activation(ex, ex, ACT.Ln, bias=1.0))
            V(lambda e: e.tensor_scalar(mn, gates[:, :, 4:8], 0.0, None, ALU.min))
            t_lf = V(lambda e: e.tensor_tensor(lf, mn, ex, ALU.subtract), [t1])
            b, bank, bf = banks.take()
            for t in range(NT):
                tk = tp(bank[0:4, t * 128:(t + 1) * 128], gates[:, t, 0:4], 128, [t_lf] + bf, mark=(t == 3))
            t_iT = S(lambda e, bank=bank: e.activation(iT[0:4, :], bank[0:4, :], ACT.Copy), [tk])
            banks.free(b, [t_iT])
            b, bank, bf = banks.take()
            for qt in range(NT):
                for rt in range(qt + 1):
                    tk = mm(bank[:, 4 * qt:4 * qt + 4], cst("upto", 128) if rt == qt else ones, lf[:, rt, :],
                            rt == 0, rt == qt, [t_lf] + bf, mark=(rt == qt))
            t_F = V(lambda e, bank=bank: e.tensor_copy(cumF.rearrange("p t h -> p (t h)"), bank[:, 0:16]), [tk])
            banks.free(b, [t_F])

            V(lambda e: e.tensor_copy(sbias[:, 0, 0:128], mask(0)))
            for qt in range(1, NT):
                w = causal_w(qt)
                s_, wk = score[:, qt, 0:w], work[:, 0:w]
                dg = score[:, qt, w - 128:w]
                V(lambda e, dg=dg: e.tensor_tensor(dg, dg, mask(0), ALU.add))
                for r in range(NSEL // 8):
                    a_, b_ = (s_, wk) if r % 2 == 0 else (wk, s_)
                    V(lambda e, a_=a_: e.max(st_x[:, 0:8], a_))
                    V(lambda e, a_=a_, b_=b_: e.match_replace(b_, st_x[:, 0:8], a_, TAKEN))
                V(lambda e, qt=qt, w=w, s_=s_: e.tensor_scalar(sbias[:, qt, 0:w], s_, TAKEN / 2, NEG, ALU.is_gt,
                                                               ALU.mult))
            sel_done = (V.key, V.count)
            end = attend(8, 64, lambda h, qt: aqT[hp(h), h // 2, qt * 128:(qt + 1) * 128],
                         lambda h, w: kT[hp(h), h // 4, 0:w],
                         lambda h, c: tok[:, c, 384 + 64 * (h // 4):448 + 64 * (h // 4)],
                         lambda qt, w: sbias[:, qt, 0:w], 0.125, causal_w, Pb, PTb,
                         scaled_out(lambda qt: mixed[:, qt, 0:512].rearrange("p (h d) -> p h d", h=8), 8, 64),
                         [sel_done, (P.key, P.count), (S.key, S.count)])
            start = [end, (P.key, P.count), (S.key, S.count), t_qk, t_iT, t_F]
            mlstm_end = mlstm(qk, mv, lf, iT, cumF, lfb, Pb, PTb, small, mixed, start)
            x = mixed[:, :, 512:1024].rearrange("p t (h d) -> p t h d", h=4)
            sq = ar(24416, 2048).rearrange("p (t h d) -> p t h d", t=NT, h=4)
            V(lambda e: e.tensor_tensor(sq, x, x, ALU.mult), [mlstm_end, (P.key, P.count)])
            V(lambda e: e.tensor_reduce(st_ss[:, 0:16].rearrange("p (t h) -> p t h", t=NT), sq, AX.X, ALU.add))
            rstd_of(st_ss[:, 0:16], 128, st_r[:, 0:16], (st_a[:, 0:16], st_b[:, 0:16], st_c[:, 0:16]))
            r = st_r[:, 0:16].rearrange("p (t h) -> p t h", t=NT).unsqueeze(3).to_broadcast([P128, NT, 4, 128])
            V(lambda e: e.tensor_tensor(x, x, r, ALU.mult))
            tg = V(lambda e: e.tensor_tensor(mixed[:, :, 512:1024], mixed[:, :, 512:1024], mo, ALU.mult))
            pdone = [(P.key, P.count), tg]
            ma = to_T([mixed[:, t, 0:512] for t in range(NT)], 4, XT[:, 0:4, :], None, pdone, pdone)
            mb = to_T([mixed[:, t, 512:1024] for t in range(NT)], 4, XT[:, 4:8, :], f"g_mh_{l}", pdone, pdone)
            for c in range(2):
                i, wt, tw = load_w(A["w_out_2"][l][:, c * 512:(c + 1) * 512], ND, 512)
                t = lin(XT, ND, wt, 512, add_h(c), ma + mb + [tw])
                wring.free(i, [t])
            if stop == f"Lattn{l}":
                return True
            begin = all_done()
            xt = norm_T([H[:, t, :] for t in range(NT)], ND, f"g_mlp_{l}", XT, junk, xtmp, begin, begin)
            fT = ar(2048, 16384).rearrange("p (k t) -> p k t", k=32)
            for c in range(DFF // 512):
                i, wt, tw = load_w(A["w_ff1_2"][l][:, c * 512:(c + 1) * 512], ND, 512)
                for j in range(4):
                    b, bank, bf = banks.take()
                    for k in range(ND):
                        tk = mm(bank[:, :], wt[:, k, j * 128:(j + 1) * 128], XT[:, k, :], k == 0, k == ND - 1,
                                xt + bf + [tw], mark=(k == ND - 1))
                    f = fT[:, 4 * c + j, :]
                    t1 = S(lambda e, f=f, bank=bank: e.activation(f, bank[:, :], ACT.Relu), [tk] + begin, own=False)
                    banks.free(b, [t1])
                    t_f = V(lambda e, f=f: e.tensor_tensor(f, f, f, ALU.mult), [t1], own=False)
                wring.free(i, [tk])
            for c in range(2):
                bb = [banks.take() for _ in range(NT)]
                for kq in range(4):
                    i, wt, tw = load_w(A["w_ff2_2"][l][kq * 1024:(kq + 1) * 1024, c * 512:(c + 1) * 512], 8, 512)
                    for k in range(8):
                        for t in range(NT):
                            tk = mm(bb[t][1][:, :], fT[:, 8 * kq + k, t * 128:(t + 1) * 128], wt[:, k, :],
                                    kq == 0 and k == 0, kq == 3 and k == 7, [tw, t_f] + (bb[t][2] if kq + k == 0 else []),
                                    mark=(k == 7 and t == 3))
                    wring.free(i, [tk])
                for t in range(NT):
                    dst, bank = H[:, t, c * 512:(c + 1) * 512], bb[t][1]
                    t2 = V(lambda e, dst=dst, bank=bank: e.tensor_tensor(dst, bank[:, :], dst, ALU.add), [tk],
                           own=False)
                    banks.free(bb[t][0], [t2])
            if stop == f"Lff{l}":
                return True
            ple(f"g_ple_{l}", A["w_ple_gate_2"][l], A["w_ple_2"][l], A["p2T"][l], A["b_ple_gate_2"][l:l + 1, :],
                all_done())
            return stop == f"layer{l}"

        def mlstm(qk, mv, lf, iT, cumF, lfb, Pb, PTb, small, mixed, start):
            prob, ptr = Ring(Pb), Ring(PTb)
            lfm = {}

            def spread(h):
                i, buf, f = lfb.take()
                fr = list(f) + list(start)
                for rt in range(NT):
                    V(lambda e, rt=rt: e.tensor_scalar(buf[:, 384 + rt * 128:512 + rt * 128], cst("upto", 128),
                                                       lf[:, rt, h:h + 1], None, ALU.mult), fr, own=(rt == 0))
                    if rt < NT - 1:
                        V(lambda e, rt=rt: e.tensor_scalar(buf[:, rt * 128:(rt + 1) * 128], ones,
                                                           lf[:, rt, h:h + 1], None, ALU.mult), fr, own=False)
                lfm[h] = (i, buf, (V.key, V.count))

            units = [(h, qt) for h in range(4) for qt in range(NT)]
            st, ob = {}, {}
            mval = small[:, 64:80]
            nmv = small[:, 80:96]
            den = small[:, 96:112]
            em = small[:, 112:128]
            rin = small[:, 128:144]

            def scores(u):
                h, qt = units[u]
                w = causal_w(qt)
                if qt == 0:
                    spread(h)
                li, lb, lt = lfm[h]
                b, bank, bf = banks.take(SC)
                for rt in range(qt, -1, -1):
                    lhs = lb[:, 384 + rt * 128:512 + rt * 128] if rt == qt else lb[:, rt * 128:(rt + 1) * 128]
                    mm(bank[:, 0:(rt + 1) * 128], lhs, before(rt), rt == qt, False, [lt] + list(start) + bf)
                tk = mm(bank[:, 0:w], con[0:4, CC["head"] + 128 * h:CC["head"] + 128 * h + 128], iT[0:4, 0:w], False,
                        True, mark=True)
                if qt == NT - 1:
                    lfb.free(li, [tk])
                b2, bank2, bf2 = banks.take(SC)
                tk2 = mm(bank2[:, 0:w], qk[:, h, qt * 128:(qt + 1) * 128], qk[:, 4 + h, 0:w], True, True, bf2,
                         mark=True)
                i, pr, pf = prob.take()
                c = 4 * h + qt
                m, nm = mval[:, c:c + 1], nmv[:, c:c + 1]
                V(lambda e: e.tensor_tensor_reduce(pr[:, 0:w], bank[:, 0:w], mask(qt), 1.0, -3e38, ALU.add, ALU.max, m),
                  [tk] + pf + list(start))
                t1 = (V.key, V.count)
                V(lambda e: e.tensor_tensor(m, m, cumF[:, qt, h:h + 1], ALU.max))
                t2 = V(lambda e: e.tensor_scalar(nm, m, -1.0, None, ALU.mult))
                banks.free(b, [t1])
                t3 = S(lambda e: e.activation(pr[:, 0:w], pr[:, 0:w], ACT.Exp, bias=nm), [t2])
                st[u] = (i, pr, t3, b2, bank2, tk2)

            def turn(u):
                h, qt = units[u]
                w = causal_w(qt)
                i, pr, t3, b2, bank2, tk2 = st[u]
                dn = den[:, 4 * h + qt:4 * h + qt + 1]
                t4 = V(lambda e: e.tensor_tensor_reduce(pr[:, 0:w], bank2[:, 0:w], pr[:, 0:w], 128 ** -0.5, 0.0,
                                                        ALU.mult, ALU.add, dn), [t3, tk2])
                banks.free(b2, [t4])
                b, bank, bf = banks.take(SC)
                for c in range(w // 128):
                    tk = tp(bank[:, c * 128:(c + 1) * 128], pr[:, c * 128:(c + 1) * 128], 128, [t4] + bf,
                            mark=(c == w // 128 - 1))
                prob.free(i, [tk])
                j, pt, ptf = ptr.take()
                t5 = copy_out(pt[:, 0:w], bank[:, 0:w], [tk] + ptf)
                banks.free(b, [t5])
                st[u] = (j, pt, t5)

            def pv(u):
                h, qt = units[u]
                j, pt, t5 = st[u]
                if qt == 0:
                    ob[h] = banks.take(OB)
                b, bank, bf = ob[h]
                for c in range(qt + 1):
                    tk = mm(bank[:, qt * 128:(qt + 1) * 128], pt[:, c * 128:(c + 1) * 128],
                            mv[:, c, h * 128:(h + 1) * 128], c == 0, c == qt, [t5] + bf, mark=(c == qt))
                ptr.free(j, [tk])
                if qt == NT - 1:
                    s_ = slice(4 * h, 4 * h + 4)
                    S(lambda e: e.activation(em[:, s_], nmv[:, s_], ACT.Exp), [tk])
                    t6 = S(lambda e: e.activation(rin[:, s_], den[:, s_], ACT.Abs))
                    V(lambda e: e.tensor_tensor(rin[:, s_], rin[:, s_], em[:, s_], ALU.max), [t6])
                    V(lambda e: e.reciprocal(rin[:, s_], rin[:, s_]))
                    t7 = V(lambda e: e.tensor_tensor(
                        mixed[:, :, 512 + h * 128:640 + h * 128], bank[:, :].rearrange("p (t d) -> p t d", t=NT),
                        rin[:, s_].unsqueeze(2).to_broadcast([P128, NT, 128]), ALU.mult))
                    banks.free(b, [t7])
                    st["end"] = t7

            n = len(units)
            for i in range(n + 2):
                if i < n:
                    scores(i)
                if 1 <= i < n + 1:
                    turn(i - 1)
                if i >= 2:
                    pv(i - 2)
            return st["end"]

        for l in range(2):
            if layer(l):
                break
        finish_with(H, all_done())
        return emit_all(nc, ctx, sem_names, P, V, S, G, Q)


def emit_all(nc, ctx, sem_names, P, V, S, G, Q):
    sems = {n: ctx.enter_context(nc.semaphore(f"s_{n}")) for n in sem_names}
    block = ctx.enter_context(nc.Block())

    @block.sync
    def _(e):
        Q.emit(e, sems)

    @block.tensor
    def _(e):
        P.emit(e, sems)

    @block.vector
    def _(e):
        V.emit(e, sems)

    @block.scalar
    def _(e):
        S.emit(e, sems)

    @block.gpsimd
    def _(e):
        G.emit(e, sems)


def host_arrays(i):
    def col(v):
        return np.asarray(v, np.float32).reshape(-1, P128).T
    parts = [col(i["g_mix"][0]), col(i["g_cq"][0]), col(i["g_ckv"][0]),
             np.concatenate([col(i["g_out_mla"][0]), col(i["g_out_dil"][0])], 1), col(i["g_ffn"][0]),
             col(i["g_ple"][0])]
    rows = [np.broadcast_to(i["g_final"][None, :], (P128, D))]
    for l in range(2):
        parts += [col(i["g_mix_2"][l]), col(i["g_cq_2"][l]), col(i["g_mh_2"][l].reshape(-1)), col(i["g_mlp_2"][l]),
                  col(i["g_ple_2"][l]), np.concatenate([col(i["conv_w_2"][l, j]) for j in range(4)], 1),
                  col(i["conv_b_2"][l])]
        r = np.concatenate([i["g_qn_2"][l], i["g_kn_2"][l], i["g_ik_2"][l], i["i_bias_2"][l], i["f_bias_2"][l],
                            np.zeros(8, np.float32)])
        rows.append(np.broadcast_to(r[None, :], (P128, 208)))
    kbd = np.zeros((P128, 256), np.float32)
    kbd[0:64, 0:128] = i["peer_keys1"][0].T
    kbd[64:128, 128:256] = i["peer_keys2"][0].T
    consts, dil = constants()
    c = np.ascontiguousarray
    return {
        "x": i["x"][0], "consts": consts, "dil_bias": dil, "gains": c(np.concatenate(parts, 1)),
        "rows": c(np.concatenate(rows, 1)), "w_in": i["w_in"][0], "w_uq": i["w_uq"][0], "w_ukv": i["w_ukv"][0],
        "w_out": i["w_out"][0], "w_peer_q": i["w_peer_q"][0], "peer_keys": kbd,
        "peer_uT": c(i["peer_u"][0].T), "peer_v": i["peer_v"][0], "w_ple_gate": i["w_ple_gate"][0],
        "w_ple_proj": i["w_ple_proj"][0], "pT": c(i["p"][0, 0].T),
        "pos": c(i["positions_2"][0].reshape(NT, P128).T),
        "p2T": c(i["p_2"][:, 0].transpose(0, 2, 1)), "w_in_2": i["w_in_2"], "w_q_up_2": i["w_q_up_2"],
        "w_iq_up_2": i["w_iq_up_2"], "w_out_2": i["w_out_2"], "w_ff1_2": i["w_ff1_2"], "w_ff2_2": i["w_ff2_2"],
        "w_ple_gate_2": i["w_ple_gate_2"], "b_ple_gate_2": i["b_ple_gate_2"], "w_ple_2": i["w_ple_2"],
    }


def kernel(**inputs):
    import concourse.bacc as bacc
    from concourse.bass_utils import run_bass_kernel_spmd

    nc = bacc.Bacc("TRN2", target_bir_lowering=False, num_devices=1)
    arrays, aps = {}, {}
    for name, a in host_arrays({k: np.asarray(v) for k, v in inputs.items()}).items():
        a = np.ascontiguousarray(a)
        arrays[name + "_dram"] = a
        aps[name] = nc.dram_tensor(name + "_dram", a.shape, mybir.dt.from_np(a.dtype), kind="ExternalInput").ap()
    out = nc.dram_tensor("out_dram", (T, D), F32, kind="ExternalOutput").ap()
    aps["out"] = out
    build(nc, aps)
    r = run_bass_kernel_spmd(nc, [arrays], core_ids=[0])
    return r.results[0]["out_dram"].reshape(1, T, D)
```

```python
from contextlib import ExitStack

import numpy as np

import concourse.bass as bass
from concourse import mybir

F32 = mybir.dt.float32
F32R = mybir.dt.float32r
I32 = mybir.dt.int32
U32 = mybir.dt.uint32
ALU = mybir.AluOpType
ACT = mybir.ActivationFunctionType
AX = mybir.AxisListType

P128 = 128
T = 512
NT = T // P128
D = 1024
ND = D // P128
EPS = 1e-6
NEG = -1e30
TAKEN = -3e38
PLE = 256

AHEAD_CHOOSE, AHEAD_GATES = 24, 4
TB = 32
AREA, AREA_SMALL = 25300, 8800

QR, KVR, RR = 384, 256, 32
MH, NOPE, VD = 8, 64, 64
QK = NOPE + RR
IN1 = QR + KVR + RR + 3 * 512
NE, KEYS, PH, TOPK = 16384, 128, 8, 16
ETG = 8
IN2 = 2640
NSEL = 128
IDX_SCALE = (8 ** -0.5) * (64 ** -0.5)
DFF = 4096

GC = {}


def _cols(layout):
    at = 0
    for name, n in layout:
        GC[name] = at
        at += n
    GC["g_out2"] = GC["g_out"] + 4 if "g_out" in GC else 0
    return at


N_GAIN = _cols([("g_mix", 8), ("g_cq", 3), ("g_ckv", 2), ("g_out", 8), ("g_ffn", 8), ("g_ple", 8)]
               + [(f"{n}_{l}", k) for l in range(2) for n, k in
                  [("g_mix", 8), ("g_cq", 2), ("g_mh", 4), ("g_mlp", 8), ("g_ple", 8), ("conv_w", 32),
                   ("conv_b", 8)]])
RC = {"g_final": 0}
for _l in range(2):
    RC[f"g_qn_{_l}"] = 1024 + 208 * _l
    RC[f"g_kn_{_l}"] = 1024 + 208 * _l + 64
    RC[f"g_ik_{_l}"] = 1024 + 208 * _l + 128
    RC[f"if_bias_{_l}"] = 1024 + 208 * _l + 192
N_ROW = 1024 + 2 * 208
CC = {"ident": 0, "iota": 128, "before": 256, "upto": 768, "causal": 896, "head": 1408, "iota16": 1920,
      "cos_m": 1936, "sin_m": 2000, "cos_d": 2064, "sin_d": 2096, "inv": 2128}
N_CONST = 2136


def constants():
    c = np.zeros((P128, N_CONST), np.float32)
    i = np.arange(P128)
    c[:, 0:128] = np.eye(P128)
    c[:, 128:256] = i[None, :]
    c[:, 256:640] = 1.0
    c[:, 640:768] = i[None, :] < i[:, None]
    c[:, 768:896] = i[:, None] <= i[None, :]
    c[:, 1280:1408] = np.where(i[None, :] <= i[:, None], 0.0, NEG)
    for h in range(4):
        c[h, 1408 + 128 * h:1536 + 128 * h] = 1.0
    c[:, 1920:1936] = np.arange(16)
    pos = np.arange(T, dtype=np.float32)

    def tables(rot):
        inv = np.float32(500000.0) ** (-np.arange(0, rot, 2, dtype=np.float32) / np.float32(rot))
        ang = (pos[:, None] * inv[None, :]).astype(np.float64)
        return inv, [f(ang).astype(np.float32).reshape(NT, P128, -1).transpose(1, 0, 2).reshape(P128, -1)
                     for f in (np.cos, np.sin)]
    _, (c[:, 1936:2000], c[:, 2000:2064]) = tables(32)
    inv, (c[:, 2064:2096], c[:, 2096:2128]) = tables(16)
    c[:, 2128:2136] = inv[None, :]
    q, k = np.arange(T)[:, None], np.arange(T)[None, :]
    n = np.zeros((T, T))
    for window, dil in ((128, 1), (512, 4), (2048, 16)):
        n += ((q - k) % dil == 0) & (np.abs(q - k) <= window // 2)
    bias = np.where(n > 0, np.log(np.maximum(n, 1)) * 8.0, NEG).astype(np.float32)
    return c, bias


def weight_plan(A):
    plan = []

    def add(name, W, c0, n, rows=None):
        r0, r1 = rows or (0, W.shape[0])
        for k in range(r0, r1, 512):
            m = min(512, r1 - k)
            plan.append((name, W[k:k + m, c0:c0 + n], m // P128, n))
    for c0 in range(0, IN1, 512):
        add("w_in", A["w_in"], c0, min(512, IN1 - c0))
    for c in range(2):
        add("w_uq", A["w_uq"], 384 * c, 384)
    for c in range(2):
        add("w_ukv", A["w_ukv"], 512 * c, 512)
    for name in ("w_out", "w_peer_q"):
        for c in range(2):
            add(name, A[name], 512 * c, 512)

    def up(g):
        for u in range(ETG // 4):
            add("peer_uT", A["peer_uT"], (g * ETG + 4 * u) * 128, 512)
    ngroups = KEYS // ETG
    for g in range(0, ngroups, 2):
        up(g)
    for g in range(ngroups):
        if g + 1 < ngroups and (g + 1) % 2:
            up(g + 1)
        for c in range(2):
            add("peer_v", A["peer_v"], 512 * c, 512, (g * ETG * 128, (g + 1) * ETG * 128))
    for c in range(2):
        add("w_gate", A["w_ple_gate"], 512 * c, 512)
        add("w_proj", A["w_ple_proj"], 512 * c, 512)
    for l in range(2):
        W = A["w_in_2"][l]
        add("w_in_2", W, 0, 512)
        for k in range(2):
            plan.append(("w_in_2 b", [(0, 72, W[512 * k:512 * k + 512, 512:584]),
                                      (72, 80, W[512 * k:512 * k + 512, 2632:2640])], 4, 80))
        for c in range(4):
            add("w_in_2", W, 584 + 512 * c, 512)
        add("w_q_up_2", A["w_q_up_2"][l], 0, 512)
        add("w_iq_up_2", A["w_iq_up_2"][l], 0, 512)
        for c in range(2):
            add("w_out_2", A["w_out_2"][l], 512 * c, 512)
        for q in range(DFF // 1024):
            for c in range(2):
                add("w_ff1_2", A["w_ff1_2"][l], 1024 * q + 512 * c, 512)
            for c in range(2):
                add("w_ff2_2", A["w_ff2_2"][l], 512 * c, 512, (1024 * q, 1024 * (q + 1)))
        for c in range(2):
            add("w_gate", A["w_ple_gate_2"][l], 512 * c, 512)
            add("w_proj", A["w_ple_2"][l], 512 * c, 512)
    return plan


class Engine:

    def __init__(self, key, own):
        self.key, self.own, self.count, self.items, self.waited = key, own, 0, [], {}

    def __call__(self, fn, after=(), own=None, mark=True, dma=None):
        need = {}

        def add(x):
            if x is None:
                return
            if isinstance(x, list):
                for y in x:
                    add(y)
            else:
                need[x[0]] = max(need.get(x[0], 0), x[1])
        add(list(after) if isinstance(after, tuple) and not (after and isinstance(after[0], str)) else after)
        if (self.own if own is None else own) and self.count:
            add((self.key, self.count))
        waits = []
        for k, v in need.items():
            if v > 0 and self.waited.get(k, 0) < v:
                self.waited[k] = v
                waits.append((k, v))
        if dma is not None:
            self.items.append((fn, waits, (dma[0], 16)))
            return dma
        if mark:
            self.count += 1
        self.items.append((fn, waits, (self.key, 1) if mark else None))
        return (self.key, self.count) if mark else None

    def emit(self, eng, sems):
        for fn, waits, inc in self.items:
            for k, v in waits:
                eng.wait_ge(sems[k], v)
            ins = fn(eng)
            if inc:
                ins.then_inc(sems[inc[0]], inc[1])


class Ring:

    def __init__(self, bufs):
        self.bufs, self.at = bufs, 0
        self.freed = [[] for _ in bufs]

    def take(self):
        i = self.at % len(self.bufs)
        self.at += 1
        assert self.freed[i] is not None, "taken before it was given back"
        f, self.freed[i] = self.freed[i], None
        return i, self.bufs[i], f

    def free(self, i, toks):
        self.freed[i] = toks


class Banks:

    def __init__(self, banks):
        self.banks, self.freed, self.at = banks, [[] for _ in banks], {}

    def take(self, among=tuple(range(8))):
        n = self.at.get(among, 0)
        self.at[among] = n + 1
        i = among[n % len(among)]
        assert self.freed[i] is not None, "bank taken before it was given back"
        f, self.freed[i] = self.freed[i], None
        return i, self.banks[i], f

    def free(self, i, toks):
        self.freed[i] = toks


def build(nc, A, stop=None):
    with ExitStack() as ctx:
        def sb(name, words, dt=F32):
            return ctx.enter_context(nc.sbuf_tensor(name, [P128, words], dt))

        H = sb("h", NT * D)[:, :].rearrange("p (t d) -> p t d", t=NT)
        X = tuple(sb(n, ND * T, F32R)[:, :].rearrange("p (c t) -> p c t", c=ND) for n in ("x_hi", "x_lo"))
        wraw = [sb(f"w_raw{i}", 2048) for i in range(2)]
        wspl = [(sb(f"w_hi{i}", 2048, F32R), sb(f"w_lo{i}", 2048, F32R)) for i in range(2)]
        con = sb("con", N_CONST)
        gain = sb("gain", N_GAIN)
        row = sb("row", 208)
        stat = sb("stat", 512)
        stat_rope = sb("rope2", 64)
        scope, arena = [], []

        def end_phase():
            while scope:
                scope.pop().__exit__(None, None, None)
        ctx.callback(end_phase)

        def phase(split):
            end_phase()
            arena.clear()

            def new(name, words, dt):
                c = nc.sbuf_tensor(f"{name}_{len(phases)}", [P128, words], dt)
                scope.append(c)
                return c.__enter__()
            phases.append(split)
            out = None
            if split:
                out = [tuple(new(f"f_{p}{i}", 4096, F32R)[:, :].rearrange("p (e t) -> p e t", e=8)
                             for p in ("hi", "lo")) for i in range(2)]
            arena.append(new("area", AREA_SMALL if split else AREA, F32))
            return out
        phases = []
        phase(False)
        banks = Banks([ctx.enter_context(nc.psum_tensor(f"bank{i}", [P128, 512], F32)) for i in range(8)])
        a_scratch = nc.dram_tensor("a_scratch", (KEYS // 2, KEYS, T), F32, kind="Internal").ap()
        g_scratch = nc.dram_tensor("g_scratch", (T // TB, KEYS, KEYS, TB), F32, kind="Internal").ap()

        def ar(at, n):
            return arena[0][:, at:at + n]

        P, V, S, G, Q = (Engine(k, own) for k, own in
                         [("pe", False), ("dve", True), ("act", True), ("pool", True), ("sp", False)])
        sem_names = ["pe", "dve", "act", "pool", "sp"]
        dma_count = {}

        def dma(out, in_, sem, after=(), q=None):
            if sem not in dma_count:
                dma_count[sem] = 0
                sem_names.append(sem)
            dma_count[sem] += 16
            return (q or Q)(lambda e: e.dma_start(out, in_), after, dma=(sem, dma_count[sem]))

        ident = con[:, 0:128]

        def cst(name, n, p=P128):
            return con[0:p, CC[name]:CC[name] + n]

        t_h = dma(H, A["x"].rearrange("(t p) d -> p t d", p=P128), "h_in")
        t_con = dma(con[:, :], A["consts"], "con_in")
        t_gain = dma(gain[:, :], A["gains"], "gain_in")

        raw_ring = Ring([w[:, :] for w in wraw])
        spl_ring = Ring([(a[:, :], b[:, :]) for a, b in wspl])
        plan = weight_plan(A)
        fetched = []

        def fetch():
            if not plan:
                return
            name, src, nk, n = plan.pop(0)
            ri, raw, rfree = raw_ring.take()
            si, (hi, lo), sfree = spl_ring.take()
            r3 = raw[:, 0:nk * n].rearrange("p (k n) -> p k n", k=nk)
            for a, b, s_ in (src if isinstance(src, list) else [(0, n, src)]):
                tw = dma(r3[:, :, a:b], s_.rearrange("(k p) n -> p k n", p=P128), f"w_raw{ri}_in", after=rfree)
            h_, l_, r_ = hi[:, 0:nk * n], lo[:, 0:nk * n], raw[:, 0:nk * n]
            th = S(lambda e: e.activation(h_, r_, ACT.Copy), [tw] + sfree, own=False)
            tl = G(lambda e: e.tensor_tensor(l_, r_, h_.bitcast(F32), ALU.subtract), [tw, th] + sfree, own=False)
            raw_ring.free(ri, [th, tl])
            fetched.append((name, si, h_.rearrange("p (k n) -> p k n", k=nk), l_.rearrange("p (k n) -> p k n", k=nk),
                            nk, [th, tl]))

        def take_w(name):
            if not fetched:
                fetch()
            got = fetched.pop(0)
            assert got[0] == name, (got[0], name)
            return got[1:]

        def give_w(si, toks):
            spl_ring.free(si, toks)
            fetch()

        state = {"turn": 0}

        def copy_out(dst, src, after):
            state["turn"] ^= 1
            if state["turn"]:
                return V(lambda e: e.tensor_copy(dst, src), after)
            return S(lambda e: e.activation(dst, src, ACT.Copy), after)

        def mm(out, lhsT, rhs, start, stop, after=(), mark=False):
            return P(lambda e: e.matmul(out, lhsT, rhs, start=start, stop=stop), after, mark=mark)

        def tp(out, in_, k, after=(), mark=False):
            return P(lambda e: e.transpose(out, in_, ident[0:k, 0:k]), after, mark=mark)

        def rstd_of(ss, width, out, tmp, after=()):
            a, b, c = tmp
            V(lambda e: e.tensor_scalar(a, ss, 1.0 / width, EPS, ALU.mult, ALU.add), after)
            t = (V.key, V.count)
            t = S(lambda e: e.activation(b, a, ACT.Sqrt), [t])
            V(lambda e: e.reciprocal(c, b), [t])
            V(lambda e: e.tensor_tensor(c, a, c, ALU.mult))
            V(lambda e: e.tensor_tensor(c, b, c, ALU.add))
            V(lambda e: e.tensor_scalar(c, c, 0.5, None, ALU.mult))
            return V(lambda e: e.reciprocal(out, c))

        st_ss, st_a, st_b, st_c, st_r = (stat[:, 64 * i:64 * i + 64] for i in range(5))
        st_mx, st_nm, st_sum = stat[:, 320:352], stat[:, 352:384], stat[:, 384:416]
        st_x = stat[:, 416:512]

        def norm_rows(srcs, width, junk, after):
            after = list(after) + last_x
            for t in range(NT):
                tok = S(lambda e, t=t: e.activation(junk[:, 0:width], srcs[t], ACT.Square,
                                                    accum_out=st_ss[:, t:t + 1]), after)
            return rstd_of(st_ss[:, 0:NT], width, st_r[:, 0:NT], (st_a[:, 0:NT], st_b[:, 0:NT], st_c[:, 0:NT]), [tok])

        last_x = []
        xfull = Ring([2048, 2560])

        def to_T(src_t, nd, dst, c_at, gname, after, free=(), scale=None):
            toks = []
            last_tp = [[], []]
            for t in range(NT):
                src = src_t[t]
                tok_x = after
                if scale is not None:
                    x = ar(1024 * (t % 2), nd * P128)
                    tok_x = [V(lambda e, t=t, x=x, src=src: e.tensor_scalar(x, src, scale[:, t:t + 1], None, ALU.mult),
                               list(after) + last_tp[t % 2])]
                    src = x
                for c0 in range(0, nd, 4):
                    n = min(4, nd - c0)
                    b, bank, bf = banks.take()
                    for c in range(n):
                        tk = tp(bank[:, c * 128:(c + 1) * 128], src[:, (c0 + c) * 128:(c0 + c + 1) * 128], 128,
                                list(tok_x) + bf + [t_con], mark=(c == n - 1))
                    hi, lo = (d[:, c_at + c0:c_at + c0 + n, t * 128:(t + 1) * 128] for d in dst)
                    inn = bank[:, 0:n * 128].rearrange("p (c t) -> p c t", c=n)
                    fi, fat, ff = xfull.take()
                    full = ar(fat, n * 128).rearrange("p (c t) -> p c t", c=n)
                    if gname is None:
                        t1 = V(lambda e, full=full, inn=inn: e.tensor_copy(full, inn), [tk] + ff + list(after))
                    else:
                        g = gain[:, GC[gname] + c0:GC[gname] + c0 + n].unsqueeze(2).to_broadcast([P128, n, 128])
                        t1 = V(lambda e, full=full, inn=inn, g=g: e.tensor_tensor(full, inn, g, ALU.mult),
                               [tk, t_gain] + ff + list(after))
                    banks.free(b, [t1])
                    t2 = S(lambda e, full=full, hi=hi: e.activation(hi, full, ACT.Copy), [t1] + list(free), own=False)
                    t3 = V(lambda e, full=full, hi=hi, lo=lo: e.tensor_tensor(lo, full, hi.bitcast(F32), ALU.subtract),
                           [t2] + list(free))
                    xfull.free(fi, [t3])
                    toks += [t2, t3]
                last_tp[t % 2] = [tk]
            last_x[:] = last_tp[0] + last_tp[1] + toks[-4:]
            return toks[-2:]

        def norm_T(srcs, nd, gname, after, free=(), c_at=0, gout=None):
            r = norm_rows(srcs, nd * P128, ar(0, 1024), after)
            return to_T(srcs, nd, X, c_at, gname, list(after) + [r], free, st_r)

        def gemm4(*args, **kw):
            for tk in gemm4_steps(*args, **kw):
                pass
            return tk

        def gemm4_steps(name, ntiles, n, x, tokens_out, evict, after, bias=None, k0=0, among=tuple(range(8))):
            bb = [banks.take(among) for _ in range(4)]
            for i in range(ntiles):
                si, wh, wl, nk, tw = take_w(name)
                for g in range(4):
                    b, bank, bf = bb[g]
                    for k in range(nk):
                        xs = [p[:, k0 + k, :] for p in x]
                        if tokens_out:
                            st_ = [p[:, g * 128:(g + 1) * 128] for p in xs]
                            mv_ = [wh[:, k, 0:n], wl[:, k, 0:n]]
                            out = bank[:, 0:n]
                        else:
                            st_ = [wh[:, k, g * 128:(g + 1) * 128], wl[:, k, g * 128:(g + 1) * 128]]
                            mv_, out = xs, bank[:, :]
                        for a_, b_ in ((0, 1), (0, 0), (1, 0)):
                            first = i == 0 and k == 0 and (a_, b_) == (0, 1)
                            last = i == ntiles - 1 and k == nk - 1 and a_ == 1
                            tk = mm(out, st_[a_], mv_[b_], first, last and bias is None,
                                    (list(after) + bf if first else []) + tw, mark=(k == nk - 1 and a_ == 1))
                    if i == ntiles - 1:
                        if bias is not None:
                            tk = mm(out, con[0:1, CC["head"]:CC["head"] + 128], bias, False, True, after, mark=True)
                        banks.free(b, evict(g, bank, tk))
                    if g == 3:
                        give_w(si, [tk])
                    yield tk
                k0 += nk

        def rope(x1, x2, o1, o2, c, s, tmp, after=()):
            a, b, cc, d = tmp
            V(lambda e: e.tensor_tensor(a, x1, c, ALU.mult), after)
            V(lambda e: e.tensor_tensor(b, x2, s, ALU.mult), own=False)
            V(lambda e: e.tensor_tensor(cc, x2, c, ALU.mult), own=False)
            V(lambda e: e.tensor_tensor(d, x1, s, ALU.mult), own=False)
            V(lambda e: e.tensor_tensor(o1, a, b, ALU.subtract))
            return V(lambda e: e.tensor_tensor(o2, cc, d, ALU.add))

        SC, OB = (0, 1, 2, 3, 4, 5), (6, 7)

        def attend(heads, dv, prep, v, bias, scale, width, Pb, PTb, done, after):
            prob, ptr = Ring(Pb), Ring(PTb)
            units = [(h, qt) for h in range(heads) for qt in range(NT)]
            st, obank, qk_of = {}, {}, {0: prep(0)}

            def scores(u):
                h, qt = units[u]
                w = width(qt)
                q_, k_, tqk = qk_of[h]
                b, bank, bf = banks.take(SC)
                tk = mm(bank[:, 0:w], q_[:, qt * 128:(qt + 1) * 128], k_[:, 0:w], True, True,
                        list(after) + bf + tqk, mark=True)
                if qt == 1 and h + 1 < heads:
                    qk_of[h + 1] = prep(h + 1)
                i, pr, pf = prob.take()
                par = u % 4
                mx, nm = st_mx[:, par:par + 1], st_nm[:, par:par + 1]
                bb = bias(qt, w)
                if bb is None:
                    V(lambda e: e.tensor_reduce(mx, bank[:, 0:w], AX.X, ALU.max), [tk])
                    src = bank[:, 0:w]
                else:
                    V(lambda e: e.tensor_tensor_reduce(pr[:, 0:w], bank[:, 0:w], bb, 1.0, -3e38, ALU.add, ALU.max,
                                                       mx), [tk] + pf + list(after))
                    src = pr[:, 0:w]
                t2 = V(lambda e: e.tensor_scalar(nm, mx, -scale, None, ALU.mult),
                       st.get(("exp", u - 4), []))
                at = (h % 2) * 8 + qt
                sm = st_sum[:, at:at + 1]
                t3 = S(lambda e: e.activation(pr[:, 0:w], src, ACT.Exp, bias=nm, scale=scale, accum_out=sm),
                       [t2] + pf + st.get(("sum", h - 2), []))
                st["exp", u] = [t3]
                banks.free(b, [t2, t3])
                st[u] = (i, pr, t3)

            def turn(u):
                h, qt = units[u]
                w = width(qt)
                i, pr, t3 = st[u]
                b, bank, bf = banks.take(SC)
                for c in range(w // 128):
                    tk = tp(bank[:, c * 128:(c + 1) * 128], pr[:, c * 128:(c + 1) * 128], 128, [t3] + bf,
                            mark=(c == w // 128 - 1))
                prob.free(i, [tk])
                j, pt, ptf = ptr.take()
                t4 = copy_out(pt[:, 0:w], bank[:, 0:w], [tk] + ptf)
                banks.free(b, [t4])
                st[u] = (j, pt, t4)

            def pv(u):
                h, qt = units[u]
                w = width(qt)
                j, pt, t4 = st[u]
                if qt == 0:
                    obank[h] = banks.take(OB)
                b, bank, bf = obank[h]
                n = w // 128
                for c in range(n):
                    tk = mm(bank[:, qt * dv:(qt + 1) * dv], pt[:, c * 128:(c + 1) * 128], v(h, c), c == 0, c == n - 1,
                            [t4] + bf, mark=(c == n - 1))
                ptr.free(j, [tk])
                if qt == NT - 1:
                    tok = done(h, bank, tk)
                    banks.free(b, [tok])
                    st["sum", h] = [tok]
                    st["end"] = tok

            n = len(units)
            for i in range(n + 3):
                if i < n:
                    scores(i)
                if 2 <= i < n + 2:
                    turn(i - 2)
                if i >= 3:
                    pv(i - 3)
            return st["end"]

        def scaled_out(dst, dv):
            def done(h, bank, tk):
                at = (h % 2) * 8
                r = st_x[:, 0:NT]
                V(lambda e: e.reciprocal(r, st_sum[:, at:at + NT]), [tk, (S.key, S.count)])
                return V(lambda e: e.tensor_tensor(dst(h), bank[:, 0:NT * dv].rearrange("p (t d) -> p t d", t=NT),
                                                   r.unsqueeze(2).to_broadcast([P128, NT, dv]), ALU.mult), [tk])
            return done

        def head_T(srcs, dst, after, free):
            n = srcs[0].shape[-1]
            b, bank, bf = banks.take(SC)
            for t in range(NT):
                tk = tp(bank[0:n, t * 128:(t + 1) * 128], srcs[t], 128, list(after) + bf, mark=(t == NT - 1))
            t2 = copy_out(dst[0:n, :], bank[0:n, :], [tk] + list(free))
            banks.free(b, [t2])
            return [t2]

        def soft_bufs(at):
            return [ar(at + 512 * j, 512) for j in range(4)], [ar(at + 2048 + 512 * j, 512) for j in range(3)]

        def finish_with(src, after):
            t = dma(A["out"].rearrange("(t p) d -> p t d", p=P128), src, "out_st", after=after)
            Q(lambda e: e.nop(), [t])

        all_done = lambda: [(E.key, E.count) for E in (P, V, S, G) if E.count]

        fetch()
        fetch()
        xt = norm_T([H[:, t, :] for t in range(NT)], ND, "g_mix", [t_h])
        lat = ar(3072, 4 * 672).rearrange("p (t n) -> p t n", t=NT)
        qkvd = ar(6656, 4 * 1536).rearrange("p (t n) -> p t n", t=NT)

        def to_proj(c0, n):
            def ev(t, bank, tk):
                toks = []
                for lo, hi, dst, off in ((0, 672, lat, 0), (672, IN1, qkvd, 672)):
                    a, b = max(lo, c0), min(hi, c0 + n)
                    if a < b:
                        toks.append(copy_out(dst[:, t, a - off:b - off], bank[:, a - c0:b - c0], [tk] + toks))
                return toks
            return ev

        for c0 in range(0, IN1, 512):
            n = min(512, IN1 - c0)
            t_in = gemm4("w_in", 2, n, X, True, to_proj(c0, n), xt)
        proj_done = [(V.key, V.count), (S.key, S.count)]
        a = norm_T([lat[:, t, 0:QR] for t in range(NT)], 3, "g_cq", proj_done, [t_in])
        b_ = norm_T([lat[:, t, QR:QR + KVR] for t in range(NT)], 2, "g_ckv", proj_done, [t_in], c_at=3)
        qtok = ar(12800, NT * 768).rearrange("p (t n) -> p t n", t=NT)
        ktok = ar(15872, NT * 768).rearrange("p (t n) -> p t n", t=NT)
        vtok = ar(18944, NT * 512).rearrange("p (t n) -> p t n", t=NT)
        for c in range(2):
            gemm4("w_uq", 1, 384, X, True, lambda t, bank, tk, c=c: [
                copy_out(qtok[:, t, c * 384:(c + 1) * 384], bank[:, 0:384], [tk])], a)

        def ev_kv(c):
            def ev(t, bank, tk):
                src = bank[:, :].rearrange("p (h x) -> p h x", h=4)
                kd = ktok[:, t, c * 384:(c + 1) * 384].rearrange("p (h x) -> p h x", h=4)[:, :, 0:64]
                vd = vtok[:, t, c * 256:(c + 1) * 256].rearrange("p (h x) -> p h x", h=4)
                t1 = V(lambda e: e.tensor_copy(kd, src[:, :, 0:64]), [tk])
                return [t1, S(lambda e: e.activation(vd, src[:, :, 64:128], ACT.Copy), [tk, t1])]
            return ev
        for c in range(2):
            gemm4("w_ukv", 1, 512, X, True, ev_kv(c), b_, k0=3)
        both = [(V.key, V.count), (S.key, S.count)]
        rtmp = [ar(20992 + 512 * j, 512) for j in range(4)]

        def cs(name, half, nh):
            v = con[:, CC[name]:CC[name] + NT * half].rearrange("p (t r) -> p t r", t=NT)
            return v.unsqueeze(2).to_broadcast([P128, NT, nh, half])

        def rv(x, nh, hd, lo, half):
            return x.rearrange("p t (h x) -> p t h x", h=nh)[:, :, :, lo:lo + half]

        def rt(nh, half):
            return [r[:, 0:NT * nh * half].rearrange("p (t h x) -> p t h x", t=NT, h=nh) for r in rtmp]
        q1, q2 = rv(qtok, 8, QK, 64, 16), rv(qtok, 8, QK, 80, 16)
        rope(q1, q2, q1, q2, cs("cos_m", 16, 8), cs("sin_m", 16, 8), rt(8, 16), both)
        k1, k2 = (lat[:, :, 640 + 16 * j:656 + 16 * j].unsqueeze(2) for j in range(2))
        rope(k1, k2, k1, k2, cs("cos_m", 16, 1), cs("sin_m", 16, 1), rt(1, 16))
        for t in range(NT):
            roped = V(lambda e, t=t: e.tensor_copy(
                ktok[:, t, :].rearrange("p (h x) -> p h x", h=8)[:, :, 64:96],
                lat[:, t, 640:672].unsqueeze(1).to_broadcast([P128, 8, 32])))
        for off in (0, 512):
            x = qkvd[:, :, off:off + 512]
            x1, x2 = rv(x, 8, 64, 0, 8), rv(x, 8, 64, 8, 8)
            roped_d = rope(x1, x2, x1, x2, cs("cos_d", 8, 8), cs("sin_d", 8, 8), rt(8, 8))
        mixed = ar(20992, 4096).rearrange("p (t n) -> p t n", t=NT)
        Pb, PTb = soft_bufs(3072)
        heads_at = [(ar(1024 * j, 512), ar(1024 * j + 512, 512)) for j in range(2)]

        def prep_m(h):
            qd, kd = heads_at[h % 2]
            before_ = [(P.key, P.count)]
            ta = head_T([qtok[:, t, h * QK:(h + 1) * QK] for t in range(NT)], qd, [roped], before_)
            tb_ = head_T([ktok[:, t, h * QK:(h + 1) * QK] for t in range(NT)], kd, [roped], before_)
            return qd[0:QK, :], kd[0:QK, :], ta + tb_
        end = attend(8, 64, prep_m, lambda h, c: vtok[:, c, h * 64:(h + 1) * 64], lambda qt, w: None,
                     QK ** -0.5, lambda qt: T, Pb, PTb, scaled_out(lambda h: mixed[:, :, h * 64:(h + 1) * 64], 64),
                     [roped_d])
        mla_end = [end, (P.key, P.count)]
        dbias = ar(12800, 2048).rearrange("p (t n) -> p t n", t=NT)
        tb = dma(dbias, A["dil_bias"].rearrange("(t p) k -> p t k", p=P128), "dbias_in", after=mla_end)
        pair = {}

        def prep_pairs(q_src, k_src, slots, after):
            def prep(h):
                if h % 2 == 0:
                    qd, kd = slots[h // 2 % 2]
                    before_ = [(P.key, P.count)]
                    ta = head_T(q_src(h // 2), qd, after, before_)
                    tb_ = head_T(k_src(h // 2), kd, after, before_) if k_src else []
                    pair[0] = (qd, kd, ta + tb_)
                qd, kd, tt = pair[0]
                lo = 64 * (h % 2)
                return qd[lo:lo + 64, :], kd[lo:lo + 64, :], tt
            return prep
        end = attend(8, 64, prep_pairs(lambda j: [qkvd[:, t, j * 128:(j + 1) * 128] for t in range(NT)],
                                       lambda j: [qkvd[:, t, 512 + j * 128:640 + j * 128] for t in range(NT)],
                                       heads_at, mla_end),
                     lambda h, c: qkvd[:, c, 1024 + h * 64:1088 + h * 64], lambda qt, w: dbias[:, qt, 0:w], 0.125,
                     lambda qt: T, Pb, PTb, scaled_out(lambda h: mixed[:, :, 512 + h * 64:576 + h * 64], 64),
                     mla_end + [tb])
        att_end = [end, (P.key, P.count)]
        for half in range(2):
            tm = norm_T([mixed[:, t, half * 512:(half + 1) * 512] for t in range(NT)], 4,
                        "g_out" if half == 0 else "g_out2", att_end, att_end, c_at=4 * half)

        def add_h(c):
            def ev(t, bank, tk):
                dst = H[:, t, c * 512:(c + 1) * 512]
                return [V(lambda e: e.tensor_tensor(dst, bank[:, :], dst, ALU.add), [tk])]
            return ev
        for c in range(2):
            gemm4("w_out", 2, 512, X, True, add_h(c), tm)
        if stop == "attn1":
            finish_with(H, all_done())
            return emit_all(nc, ctx, sem_names, P, V, S, G, Q)

        xt = norm_T([H[:, t, :] for t in range(NT)], ND, "g_ffn", all_done(), all_done())
        qpT = ar(3072, 4096).rearrange("p (h t) -> p h t", h=PH)
        kbd = ar(7168, 256)
        t_kbd = dma(kbd, A["peer_keys"], "kbd_in", after=all_done())
        for c in range(2):
            gemm4("w_peer_q", 2, 512, X, False, lambda g, bank, tk, c=c: [
                copy_out(qpT[:, 4 * c + g, :], bank[:, :], [tk])], xt)
        qtoks = [(V.key, V.count), (S.key, S.count)]
        sc = ar(7424, 2048).rearrange("p (l k) -> p l k", l=16)
        s2 = ar(9472, 2048).rearrange("p (l k) -> p l k", l=16)
        v16 = ar(11520, 256).rearrange("p (l k) -> p l k", l=16)
        i16 = ar(11776, 256).bitcast(U32).rearrange("p (l k) -> p l k", l=16)
        i16f = ar(12032, 256).rearrange("p (l k) -> p l k", l=16)
        cand = ar(7424, 2048).rearrange("p (h c) -> p h c", h=8)
        cnd2 = ar(9472, 2048).rearrange("p (h c) -> p h c", h=8)
        top = ar(12288, 128).rearrange("p (h k) -> p h k", h=8)
        pos = ar(12416, 128).bitcast(U32).rearrange("p (h k) -> p h k", h=8)
        pj = [ar(12544 + 128 * j, 128).bitcast(U32) for j in range(2)]
        pf = [ar(12800 + 128 * j, 128) for j in range(2)]
        sel = [ar(13056 + 128 * j, 128) for j in range(3)]
        selT = [ar(13440 + 512 * j, 512) for j in range(3)]
        iota16 = con[:, CC["iota16"]:CC["iota16"] + 16].unsqueeze(1).to_broadcast([P128, 128, 16])

        def top16(lists):
            t1 = [V(lambda e, v=v, s=s: e.max(v[:, 0:8], s), w, own=False) for v, i, s, k, w in lists]
            for (v, i, s, k, w), t in zip(lists, t1):
                V(lambda e, v=v, s=s, i=i: e.max_index(i[:, 0:8], v[:, 0:8], s), [t], own=False)
            t2 = [V(lambda e, v=v, s=s, k=k: e.match_replace(k, v[:, 0:8], s, TAKEN), [t], own=False)
                  for (v, i, s, k, w), t in zip(lists, t1)]
            t3 = [V(lambda e, v=v, k=k: e.max(v[:, 8:16], k), [t], own=False)
                  for (v, i, s, k, w), t in zip(lists, t2)]
            for (v, i, s, k, w), t in zip(lists, t3):
                V(lambda e, v=v, k=k, i=i: e.max_index(i[:, 8:16], v[:, 8:16], k), [t], own=False)

        def key_scores(t):
            for hh in range(4):
                b, bank, bf = banks.take((4, 5, 6, 7))
                for j in range(2):
                    tk = mm(bank[:, j * 256:(j + 1) * 256], qpT[:, 2 * hh + j, t * 128:(t + 1) * 128], kbd, True, True,
                            qtoks + [t_kbd] + bf, mark=(j == 1))
                t2 = S(lambda e, hh=hh, bank=bank: e.activation(
                    sc[:, 4 * hh:4 * hh + 4, :].rearrange("p l k -> p (l k)"), bank[:, :], ACT.Copy),
                    [tk] + chosen)
                banks.free(b, [t2])
            return t2

        chosen = []

        def choose(t, t2):
            top16([(v16[:, l, :], i16[:, l, :], sc[:, l, :], s2[:, l, :], [t2, (V.key, V.count)])
                   for l in range(16)])
            V(lambda e: e.tensor_copy(i16f.rearrange("p l k -> p (l k)"), i16.rearrange("p l k -> p (l k)")))
            vv = v16.rearrange("p (h s) k -> p h s k", s=2)
            V(lambda e: e.tensor_tensor(cand.rearrange("p h (a b) -> p h a b", a=16),
                                        vv[:, :, 0, :].unsqueeze(3).to_broadcast([P128, 8, 16, 16]),
                                        vv[:, :, 1, :].unsqueeze(2).to_broadcast([P128, 8, 16, 16]), ALU.add))
            tc_ = (V.key, V.count)
            top16([(top[:, h, :], pos[:, h, :], cand[:, h, :], cnd2[:, h, :], [tc_]) for h in range(8)])
            chosen[:] = [(V.key, V.count)]
            posf = pos.rearrange("p h k -> p (h k)")
            V(lambda e: e.tensor_scalar(pj[0], posf, 4, None, ALU.logical_shift_right))
            V(lambda e: e.tensor_scalar(pj[1], posf, 15, None, ALU.bitwise_and))
            for j in range(2):
                V(lambda e, j=j: e.tensor_copy(pf[j], pj[j]))
                eq = s2.rearrange("p l k -> p (l k)").rearrange("p (a b) -> p a b", b=16)
                V(lambda e, j=j: e.tensor_tensor(eq, pf[j].unsqueeze(2).to_broadcast([P128, 128, 16]), iota16,
                                                 ALU.is_equal))
                eq4 = s2.rearrange("p l k -> p (l k)").rearrange("p (h a b) -> p h a b", h=8, b=16)
                iv = i16f.rearrange("p (h s) k -> p h s k", s=2)[:, :, j, :].unsqueeze(2).to_broadcast([P128, 8, 16, 16])
                V(lambda e, eq4=eq4, iv=iv: e.tensor_tensor(eq4, eq4, iv, ALU.mult))
                V(lambda e, j=j, eq=eq: e.tensor_reduce(sel[j], eq, AX.X, ALU.add), sel_free)
            gt = sel[2].rearrange("p (h k) -> p h k", h=8)
            t1 = V(lambda e: e.tensor_tensor(gt, top, top[:, :, 0:1].to_broadcast([P128, 8, 16]), ALU.subtract),
                   sel_free)
            t1 = S(lambda e: e.activation(gt, gt, ACT.Exp), [t1])
            V(lambda e: e.tensor_reduce(st_x[:, 8:16], gt, AX.X, ALU.add), [t1])
            V(lambda e: e.reciprocal(st_x[:, 8:16], st_x[:, 8:16]))
            return V(lambda e: e.tensor_tensor(gt, gt, st_x[:, 8:16].unsqueeze(2).to_broadcast([P128, 8, 16]),
                                               ALU.mult))

        sel_free = []

        def turn_choice(t, t1):
            b, bank, bf = banks.take((4, 5, 6, 7))
            for j in range(3):
                tk = tp(bank[:, j * 128:(j + 1) * 128], sel[j], 128, [t1] + bf, mark=(j == 2))
            for j in range(3):
                t2 = V(lambda e, j=j, t=t: e.tensor_copy(selT[j][:, t * 128:(t + 1) * 128],
                                                         bank[:, j * 128:(j + 1) * 128]), [tk])
            banks.free(b, [t2])
            sel_free[:] = [tk]
            return t2

        gs = Ring([ar(17024 + 4096 * j, 4096) for j in range(2)])
        ohr = Ring([(ar(at, 512), ar(at + 512, 512)) for at in (2048, 14976, 16000)])
        iota4 = con[:, 128:256].unsqueeze(1).to_broadcast([P128, 4, 128])
        g_stores = {}

        def dense_gates(t, ready, background):
            for tb in range(P128 // TB * t, P128 // TB * (t + 1)):
                si, gbuf, gfree = gs.take()
                g3 = gbuf.rearrange("p (i t) -> p i t", t=TB)
                for q in range(TB // 4):
                    oi, (oh2, oh1), ofree = ohr.take()
                    tt = tb * TB + q * 4

                    def of(j, tt=tt):
                        return selT[j][:, tt:tt + 4].unsqueeze(2).to_broadcast([P128, 4, 128])
                    o2, o1 = (o.rearrange("p (t i) -> p t i", t=4) for o in (oh2, oh1))
                    ta = V(lambda e, o1=o1, a=of(0): e.tensor_tensor(o1, iota4, a, ALU.is_equal), [ready] + ofree,
                           own=False)
                    tv = V(lambda e, o2=o2, a=of(1): e.tensor_tensor(o2, iota4, a, ALU.is_equal), ofree, own=False)
                    tg = G(lambda e, o1=o1, a=of(2): e.tensor_tensor(o1, o1, a, ALU.mult), [ta, ready], own=False)
                    b, bank, bf = banks.take((4, 5, 6, 7))
                    for j in range(4):
                        tk = mm(bank[:, j * 128:(j + 1) * 128], oh2[:, j * 128:(j + 1) * 128],
                                oh1[:, j * 128:(j + 1) * 128], True, True, [tv, tg] + bf, mark=(j == 3))
                    ohr.free(oi, [tk])
                    out = g3[:, :, q * 4:q * 4 + 4].rearrange("p i t -> p t i")
                    t2 = S(lambda e, out=out, bank=bank: e.activation(
                        out, bank[:, :].rearrange("p (t i) -> p t i", t=4), ACT.Copy), [tk] + gfree, own=False)
                    banks.free(b, [t2])
                    background(q)
                ts = dma(g_scratch[tb], g3, f"g_st{si}", after=[t2])
                gs.free(si, [ts])
                g_stores[si] = ts

        ngroups = KEYS // ETG
        pre_begin = xt + last_x + [(P.key, P.count), (S.key, S.count), (V.key, V.count)]
        pre_b = Ring([ar(512 * j, 512) for j in range(4)])
        pre_stores = {}

        def ahead():
            for g in range(0, ngroups, 2):
                for u in range(ETG // 4):
                    e0 = g // 2 * ETG + 4 * u

                    def ev(j, bank, tk, e0=e0):
                        ai, ab, af = pre_b.take()
                        t1 = S(lambda e: e.activation(ab, bank[:, :], ACT.Gelu), [tk] + af + pre_begin, own=False)
                        ts = dma(a_scratch[e0 + j], ab, f"a_st{ai}", after=[t1])
                        pre_b.free(ai, [ts])
                        pre_stores[ai] = ts
                        return [t1]
                    yield from gemm4_steps("peer_uT", 2, 512, X, False, ev, [], among=(0, 1, 2, 3))
        work_ahead = ahead()

        def steps(n):
            for _ in range(n):
                next(work_ahead, None)
        tsc = key_scores(0)
        for t in range(NT):
            tch = choose(t, tsc)
            steps(AHEAD_CHOOSE)
            tt_ = turn_choice(t, tch)
            if t + 1 < NT:
                tsc = key_scores(t + 1)
            dense_gates(t, tt_, lambda q: steps(1) if q % AHEAD_GATES == AHEAD_GATES - 1 else None)
        steps(10 ** 6)
        stores = list(g_stores.values()) + list(pre_stores.values())
        peer_begin = all_done() + stores
        F_ = phase(True)
        act_b = Ring([ar(2048 + 512 * j, 512) for j in range(3)])
        gring = Ring([ar(3584 + 2048 * j, 2048) for j in range(2)])
        aring = Ring([ar(1024 * j, 1024) for j in range(2)])
        f_free = [[], []]

        def split_f(full, hi, lo, after, free):
            t1 = S(lambda e: e.activation(hi, full, ACT.Copy), list(after) + list(free), own=False)
            return t1, G(lambda e: e.tensor_tensor(lo, full, hi.bitcast(F32), ALU.subtract), [t1] + list(free),
                         own=False)

        def up(g):
            toks = []
            for u in range(ETG // 4):
                e0 = g * ETG + 4 * u
                gi, gb, gf = gring.take()
                gv = gb.rearrange("p (b i t) -> p b i t", i=4, t=TB)
                tg = dma(gv, g_scratch[:, :, e0:e0 + 4, :].rearrange("b p i t -> p b i t"), f"g{gi}_in",
                         after=gf + peer_begin)

                def ev(j, bank, tk, u=u, gv=gv, tg=tg):
                    ai, ab, af = act_b.take()
                    t1 = S(lambda e: e.activation(ab, bank[:, :], ACT.Gelu), [tk] + af + peer_begin, own=False)
                    a3 = ab.rearrange("p (b t) -> p b t", t=TB)
                    t2 = V(lambda e: e.tensor_tensor(a3, a3, gv[:, :, j, :], ALU.mult), [t1, tg], own=False)
                    fh, fl = (f[:, 4 * u + j, :] for f in F_[g % 2])
                    t3, t4 = split_f(ab, fh, fl, [t2], f_free[g % 2])
                    act_b.free(ai, [t4])
                    toks[:] = [t3, t4, t2]
                    return [t1]
                if g % 2:
                    gemm4("peer_uT", 2, 512, X, False, ev, [])
                else:
                    for j in range(0, 4, 2):
                        ai, ab, af = aring.take()
                        a2 = ab.rearrange("p (e t) -> p e t", e=2)
                        at = g // 2 * ETG + 4 * u + j
                        ta = dma(a2, a_scratch[at:at + 2].rearrange("e p t -> p e t"), f"a{ai}_in",
                                 after=af + peer_begin)
                        for i in range(2):
                            a3 = a2[:, i, :].rearrange("p (b t) -> p b t", t=TB)
                            t2 = V(lambda e, a3=a3, gv=gv, c=j + i: e.tensor_tensor(a3, a3, gv[:, :, c, :], ALU.mult),
                                   [ta, tg], own=False)
                        fh, fl = (f[:, 4 * u + j:4 * u + j + 2, :] for f in F_[g % 2])
                        t3, t4 = split_f(a2, fh, fl, [t2], f_free[g % 2])
                        aring.free(ai, [t4])
                        toks[:] = [t3, t4, t2]
                gring.free(gi, [toks[2]])
            return toks[0:2]

        def down(g, ready):
            for c in range(2):
                def ev(t, bank, tk, c=c):
                    dst = H[:, t, c * 512:(c + 1) * 512]
                    return [V(lambda e: e.tensor_tensor(dst, bank[:, :], dst, ALU.add), [tk], own=False)]
                tk = gemm4("peer_v", 2, 512, F_[g % 2], True, ev, ready)
            f_free[g % 2] = [tk]

        nxt = up(0)
        for g in range(ngroups):
            ready = nxt
            if g + 1 < ngroups:
                nxt = up(g + 1)
            down(g, ready)
        if stop == "peer":
            finish_with(H, all_done())
            return emit_all(nc, ctx, sem_names, P, V, S, G, Q)

        def ple(gname, pT_src, bias_src, after):
            pT = ar(3072, 1024)
            br = ar(4096, 1024)
            t_p = dma(pT.rearrange("p (k t) -> p k t", k=2), pT_src.rearrange("(k p) t -> p k t", p=P128), "pT_in",
                      after=after)
            ps = tuple(f[:, 0:2, :] for f in F_[0])
            split = split_f(pT.rearrange("p (k t) -> p k t", k=2), ps[0], ps[1], [t_p], after)
            if bias_src is not None:
                t_b = dma(br[0:1, :], bias_src, "bias_in", after=after)
            sg = Ring([ar(5120 + 512 * j, 512) for j in range(4)])
            xt = norm_T([H[:, t, :] for t in range(NT)], ND, gname, after, after)
            for c in range(2):
                gates = {}

                def ev_gate(t, bank, tk):
                    si, buf, f = sg.take()
                    t1 = S(lambda e: e.activation(buf, bank[:, :], ACT.Sigmoid), [tk] + f + list(after))
                    gates[t] = (si, buf, t1)
                    return [t1]
                gemm4("w_gate", 2, 512, X, True, ev_gate, xt + ([t_b] if bias_src is not None else []),
                      bias=None if bias_src is None else br[0:1, c * 512:(c + 1) * 512])

                def ev_proj(t, bank, tk, c=c):
                    si, buf, t1 = gates[t]
                    dst = H[:, t, c * 512:(c + 1) * 512]
                    t2 = V(lambda e: e.tensor_tensor(buf, bank[:, :], buf, ALU.mult), [tk, t1])
                    t3 = V(lambda e: e.tensor_tensor(dst, dst, buf, ALU.add))
                    sg.free(si, [t3])
                    return [t2]
                gemm4("w_proj", 1, 512, ps, True, ev_proj, list(split))

        ple("g_ple", A["pT"], None, all_done())
        gf = ar(7168, 1024)
        t_gf = dma(gf, A["rows"][:, 0:1024], "gf_in", after=all_done())
        r = norm_rows([H[:, t, :] for t in range(NT)], D, ar(0, 1024), all_done())
        for t in range(NT):
            V(lambda e, t=t: e.scalar_tensor_tensor(H[:, t, :], H[:, t, :], st_r[:, t:t + 1], gf, ALU.mult, ALU.mult),
              [r, t_gf])
        if stop == "block1":
            finish_with(H, all_done())
            return emit_all(nc, ctx, sem_names, P, V, S, G, Q)

        cos2, sin2 = stat_rope[:, 0:32], stat_rope[:, 32:64]
        pos_i = ar(3072, 4).bitcast(I32)
        posf2, ang, turns, red, over = (ar(3104 + 32 * j, n) for j, n in enumerate((4, 32, 32, 32, 32)))
        begin = all_done()
        t_pos = dma(pos_i, A["pos"], "pos_in", after=begin)
        V(lambda e: e.tensor_copy(posf2, pos_i), [t_pos] + begin)
        V(lambda e: e.tensor_tensor(ang.rearrange("p (t r) -> p t r", t=NT),
                                    posf2.unsqueeze(2).to_broadcast([P128, NT, 8]),
                                    cst("inv", 8).unsqueeze(1).to_broadcast([P128, NT, 8]), ALU.mult))
        MAGIC = 12582912.0
        C1, C2 = 6.28125, 0.0019350051879882812
        C3 = 2 * np.pi - C1 - C2
        V(lambda e: e.tensor_scalar(turns, ang, float(1 / (2 * np.pi)), MAGIC, ALU.mult, ALU.add))
        V(lambda e: e.tensor_scalar(turns, turns, MAGIC, None, ALU.subtract))
        V(lambda e: e.scalar_tensor_tensor(red, turns, -C1, ang, ALU.mult, ALU.add))
        V(lambda e: e.scalar_tensor_tensor(red, turns, -C2, red, ALU.mult, ALU.add))
        V(lambda e: e.scalar_tensor_tensor(red, turns, float(-C3), red, ALU.mult, ALU.add))
        PI_LO = 3.1415925
        V(lambda e: e.tensor_scalar(ang, red, PI_LO, -PI_LO, ALU.min, ALU.max))
        V(lambda e: e.tensor_scalar(red, red, float(np.pi / 2), None, ALU.add))
        V(lambda e: e.tensor_scalar(over, red, float(np.pi), float(-2 * np.pi), ALU.is_gt, ALU.mult))
        V(lambda e: e.tensor_tensor(red, red, over, ALU.add))
        t_r = V(lambda e: e.tensor_scalar(red, red, PI_LO, -PI_LO, ALU.min, ALU.max))
        S(lambda e: e.activation(sin2, ang, ACT.Sin), [t_r])
        t_rope = S(lambda e: e.activation(cos2, red, ACT.Sin))

        def cs2(x, nh):
            return x.rearrange("p (t r) -> p t r", t=NT).unsqueeze(2).to_broadcast([P128, NT, nh, 8])

        mask = lambda qt: cst("causal", 512)[:, (3 - qt) * 128:512]
        before = lambda rt: cst("before", 512)[:, (3 - rt) * 128:512]
        ones = cst("before", 128)
        causal_w = lambda qt: (qt + 1) * 128

        def layer(l):
            nonlocal F_
            phase(False)
            begin = all_done()
            tok = ar(3072, NT * 592).rearrange("p (t n) -> p t n", t=NT)
            mv = ar(5440, 2048).rearrange("p (t n) -> p t n", t=NT)
            mo = ar(7488, 2048).rearrange("p (t n) -> p t n", t=NT)
            qk = ar(9536, 4096).rearrange("p (c n) -> p c n", c=8)
            raws = Ring([ar(13632 + 516 * j, 516) for j in range(3)])
            iT = ar(13632, 512)
            aq = ar(15180, 2048).rearrange("p (t n) -> p t n", t=NT)
            lfb = Ring([ar(15180 + 896 * j, 896) for j in range(2)])
            iq = ar(17228, 2048).rearrange("p (t n) -> p t n", t=NT)
            sbias = ar(17228, 2048).rearrange("p (t n) -> p t n", t=NT)
            hm = ar(17228, 2048).rearrange("p (t n) -> p t n", t=NT)
            score = ar(19276, 2048).rearrange("p (t n) -> p t n", t=NT)
            att = ar(19276, 2048).rearrange("p (t n) -> p t n", t=NT)
            kdup = ar(19276, 1024).rearrange("p (t g u d) -> p t g u d", t=NT, g=2, u=2)
            ikdup = ar(20300, 512).rearrange("p (t u d) -> p t u d", t=NT, u=2)
            Pb, PTb = soft_bufs(21324)
            qslots = [ar(512 * j, 512) for j in range(2)]
            kT = ar(1024, 1024).rearrange("p (g n) -> p g n", g=2)
            ikT = ar(2048, 512)
            work = ar(2560, 512)
            small = ar(24908, 256)
            t_row = dma(row[:, :], A["rows"][:, 1024 + 208 * l:1232 + 208 * l], "row_in", after=begin)
            xt = norm_T([H[:, t, :] for t in range(NT)], ND, f"g_mix_{l}", begin, begin)
            gemm4("w_in_2", 2, 512, X, True, lambda t, bank, tk: [copy_out(tok[:, t, 0:512], bank[:, :], [tk])], xt)
            gemm4("w_in_2 b", 2, 80, X, True, lambda t, bank, tk: [copy_out(tok[:, t, 512:592], bank[:, 0:80], [tk])],
                  xt)
            tok_done = [(V.key, V.count), (S.key, S.count)]
            for c in range(2):
                def ev_conv(g, bank, tk, c=c):
                    ch = 4 * c + g
                    ri, rw, rf = raws.take()
                    V(lambda e: e.memset(rw[:, 0:3], 0.0), rf + begin)
                    t1 = S(lambda e: e.activation(rw[:, 3:515], bank[:, :], ACT.Copy), [tk] + rf + begin)
                    o = qk[:, ch, :]
                    for j in range(4):
                        at = GC[f"conv_w_{l}"] + 8 * j + ch
                        g_, x_ = gain[:, at:at + 1], rw[:, j:j + 512]
                        if j == 0:
                            V(lambda e, x_=x_, g_=g_: e.tensor_scalar(o, x_, g_, None, ALU.mult), [t1])
                        else:
                            t2 = V(lambda e, x_=x_, g_=g_: e.scalar_tensor_tensor(o, x_, g_, o, ALU.mult, ALU.add))
                    at = GC[f"conv_b_{l}"] + ch
                    conv_out.append((o, gain[:, at:at + 1], t2))
                    raws.free(ri, [t2])
                    return [t1]
                conv_out = []
                gemm4("w_in_2", 2, 512, X, False, ev_conv, [])
                for o, bcol, t2 in conv_out:
                    t_qk = S(lambda e, o=o, bcol=bcol: e.activation(o, o, ACT.Silu, bias=bcol), [t2])
            gemm4("w_in_2", 2, 512, X, True, lambda t, bank, tk: [copy_out(mv[:, t, :], bank[:, :], [tk])], [])
            t_x = gemm4("w_in_2", 2, 512, X, True, lambda t, bank, tk: [S(lambda e: e.activation(
                mo[:, t, :], bank[:, :], ACT.Sigmoid), [tk])], [])
            cq = norm_T([tok[:, t, 0:256] for t in range(NT)], 2, f"g_cq_{l}", tok_done, [t_x])
            for name, dst in (("w_q_up_2", aq), ("w_iq_up_2", iq)):
                t_q = gemm4(name, 1, 512, X, True, lambda t, bank, tk, dst=dst: [
                    copy_out(dst[:, t, :], bank[:, :], [tk])], cq)
            q_done = [(V.key, V.count), (S.key, S.count)]

            def head_norm(x, nh, gname, after):
                sq = ar(21324 + 1024, NT * nh * 64).rearrange("p (t h d) -> p t h d", t=NT, h=nh)
                n = NT * nh
                V(lambda e: e.tensor_tensor(sq, x, x, ALU.mult), after)
                V(lambda e: e.tensor_reduce(st_ss[:, 0:n].rearrange("p (t h) -> p t h", t=NT), sq, AX.X, ALU.add))
                rstd_of(st_ss[:, 0:n], 64, st_r[:, 0:n], (st_a[:, 0:n], st_b[:, 0:n], st_c[:, 0:n]))
                r = st_r[:, 0:n].rearrange("p (t h) -> p t h", t=NT).unsqueeze(3).to_broadcast([P128, NT, nh, 64])
                V(lambda e: e.tensor_tensor(x, x, r, ALU.mult))
                g = row[:, RC[f"{gname}_0"] - 1024:RC[f"{gname}_0"] - 1024 + 64]
                g = g.unsqueeze(1).unsqueeze(1).to_broadcast([P128, NT, nh, 64])
                V(lambda e: e.tensor_tensor(x, x, g, ALU.mult), [t_row])

            def head_rope(x, nh, after=()):
                tm = [ar(21324 + 256 * j, 256)[:, 0:NT * nh * 8].rearrange("p (t h x) -> p t h x", t=NT, h=nh)
                      for j in range(4)]
                x1, x2 = x[:, :, :, 0:8], x[:, :, :, 8:16]
                return rope(x1, x2, x1, x2, cs2(cos2, nh), cs2(sin2, nh), tm, list(after) + [t_rope])
            x_iq = iq.rearrange("p t (h d) -> p t h d", h=8)
            x_ik = tok[:, :, 512:576].unsqueeze(2)
            x_aq = aq.rearrange("p t (h d) -> p t h d", h=8)
            x_ak = tok[:, :, 256:384].rearrange("p t (h d) -> p t h d", h=2)
            head_rope(x_iq, 8, q_done + tok_done)
            head_norm(x_ik, 1, "g_ik", [])
            head_rope(x_ik, 1)
            head_norm(x_aq, 8, "g_qn", [])
            head_rope(x_aq, 8)
            head_norm(x_ak, 2, "g_kn", [])
            head_rope(x_ak, 2)
            iw = tok[:, :, 576:584]
            V(lambda e: e.tensor_scalar(iw, iw, IDX_SCALE, None, ALU.mult))
            for u in range(2):
                V(lambda e, u=u: e.tensor_copy(ikdup[:, :, u, :], tok[:, :, 512:576]))
                prep = V(lambda e, u=u: e.tensor_copy(kdup[:, :, :, u, :], x_ak))
            tmp_free = [(P.key, P.count)] + last_x
            tk_i = head_T([ikdup[:, t].rearrange("p u d -> p (u d)") for t in range(NT)], ikT, [prep], tmp_free)
            for g in range(2):
                tk_a = head_T([kdup[:, t, g].rearrange("p u d -> p (u d)") for t in range(NT)], kT[:, g, :], [prep],
                              tmp_free)
                tk_i += tk_a
            turned = tk_i + [(P.key, P.count)]
            rel = Ring(Pb)
            for h in range(8):
                if h % 2 == 0:
                    qd = qslots[h // 2 % 2]
                    tq = head_T([iq[:, t, h * 64:h * 64 + 128] for t in range(NT)], qd, [prep], turned + [(P.key, P.count)])
                lo = 64 * (h % 2)
                for qt in range(NT):
                    w = causal_w(qt)
                    b, bank, bf = banks.take()
                    tk = mm(bank[:, 0:w], qd[lo:lo + 64, qt * 128:(qt + 1) * 128], ikT[lo:lo + 64, 0:w], True, True,
                            turned + tq + bf, mark=True)
                    ri, rb, rf = rel.take()
                    t1 = S(lambda e, rb=rb, bank=bank, w=w: e.activation(rb[:, 0:w], bank[:, 0:w], ACT.Relu),
                           [tk] + rf + turned, own=False)
                    banks.free(b, [t1])
                    sc_, wc = score[:, qt, 0:w], iw[:, qt, h:h + 1]
                    if h == 0:
                        t2 = V(lambda e, rb=rb, w=w, sc_=sc_, wc=wc: e.tensor_scalar(sc_, rb[:, 0:w], wc, None, ALU.mult),
                               [t1] + turned)
                    else:
                        t2 = V(lambda e, rb=rb, w=w, sc_=sc_, wc=wc: e.scalar_tensor_tensor(
                            sc_, rb[:, 0:w], wc, sc_, ALU.mult, ALU.add), [t1])
                    rel.free(ri, [t2])
            gates = tok[:, :, 584:592]
            ifb = row[:, 192:200].unsqueeze(1).to_broadcast([P128, NT, 8])
            V(lambda e: e.tensor_tensor(gates, gates, ifb, ALU.add), [t_row])
            lf = small[:, 0:16].rearrange("p (t h) -> p t h", t=NT)
            ex = small[:, 16:32].rearrange("p (t h) -> p t h", t=NT)
            mn = small[:, 32:48].rearrange("p (t h) -> p t h", t=NT)
            cumF = small[:, 48:64].rearrange("p (t h) -> p t h", t=NT)
            S(lambda e: e.activation(ex, gates[:, :, 4:8], ACT.Abs), [(V.key, V.count)])
            S(lambda e: e.activation(ex, ex, ACT.Exp, scale=-1.0))
            t1 = S(lambda e: e.activation(ex, ex, ACT.Ln, bias=1.0))
            V(lambda e: e.tensor_scalar(mn, gates[:, :, 4:8], 0.0, None, ALU.min))
            t_lf = V(lambda e: e.tensor_tensor(lf, mn, ex, ALU.subtract), [t1])
            b, bank, bf = banks.take()
            for t in range(NT):
                tk = tp(bank[0:4, t * 128:(t + 1) * 128], gates[:, t, 0:4], 128, [t_lf] + bf, mark=(t == 3))
            t_iT = S(lambda e, bank=bank: e.activation(iT[0:4, :], bank[0:4, :], ACT.Copy), [tk])
            banks.free(b, [t_iT])
            b, bank, bf = banks.take()
            for qt in range(NT):
                for rt in range(qt + 1):
                    tk = mm(bank[:, 4 * qt:4 * qt + 4], cst("upto", 128) if rt == qt else ones, lf[:, rt, :],
                            rt == 0, rt == qt, [t_lf] + bf, mark=(rt == qt))
            t_F = V(lambda e, bank=bank: e.tensor_copy(cumF.rearrange("p t h -> p (t h)"), bank[:, 0:16]), [tk])
            banks.free(b, [t_F])

            V(lambda e: e.tensor_copy(sbias[:, 0, 0:128], mask(0)), [(P.key, P.count)])
            for qt in range(1, NT):
                w = causal_w(qt)
                s_, wk = score[:, qt, 0:w], work[:, 0:w]
                dg = score[:, qt, w - 128:w]
                V(lambda e, dg=dg: e.tensor_tensor(dg, dg, mask(0), ALU.add))
                for r in range(NSEL // 8):
                    a_, b_ = (s_, wk) if r % 2 == 0 else (wk, s_)
                    V(lambda e, a_=a_: e.max(st_x[:, 0:8], a_))
                    V(lambda e, a_=a_, b_=b_: e.match_replace(b_, st_x[:, 0:8], a_, TAKEN))
                V(lambda e, qt=qt, w=w, s_=s_: e.tensor_scalar(sbias[:, qt, 0:w], s_, TAKEN / 2, NEG, ALU.is_gt,
                                                               ALU.mult))
            sel_done = (V.key, V.count)
            def prep_a(h):
                if h % 2 == 0:
                    qd = qslots[h // 2 % 2]
                    pair[0] = (qd, head_T([aq[:, t, h * 64:h * 64 + 128] for t in range(NT)], qd, [prep],
                                          [(P.key, P.count)]))
                qd, tt = pair[0]
                lo = 64 * (h % 2)
                return qd[lo:lo + 64, :], kT[lo:lo + 64, h // 4, :], tt
            end = attend(8, 64, prep_a, lambda h, c: tok[:, c, 384 + 64 * (h // 4):448 + 64 * (h // 4)],
                         lambda qt, w: sbias[:, qt, 0:w], 0.125, causal_w, Pb, PTb,
                         scaled_out(lambda h: att[:, :, h * 64:(h + 1) * 64], 64),
                         [sel_done, (P.key, P.count), (S.key, S.count)])
            start = [end, (P.key, P.count), (S.key, S.count), t_qk, t_iT, t_F]
            mlstm_end = mlstm(qk, mv, lf, iT, cumF, lfb, Pb, PTb, small, hm, start)
            x = hm.rearrange("p t (h d) -> p t h d", h=4)
            sq = ar(21324, 2048).rearrange("p (t h d) -> p t h d", t=NT, h=4)
            V(lambda e: e.tensor_tensor(sq, x, x, ALU.mult), [mlstm_end, (P.key, P.count)])
            V(lambda e: e.tensor_reduce(st_ss[:, 0:16].rearrange("p (t h) -> p t h", t=NT), sq, AX.X, ALU.add))
            rstd_of(st_ss[:, 0:16], 128, st_r[:, 0:16], (st_a[:, 0:16], st_b[:, 0:16], st_c[:, 0:16]))
            r = st_r[:, 0:16].rearrange("p (t h) -> p t h", t=NT).unsqueeze(3).to_broadcast([P128, NT, 4, 128])
            V(lambda e: e.tensor_tensor(x, x, r, ALU.mult))
            tg = V(lambda e: e.tensor_tensor(hm, hm, mo, ALU.mult))
            pdone = [(P.key, P.count), tg]
            to_T([att[:, t, :] for t in range(NT)], 4, X, 0, None, pdone, pdone)
            mb = to_T([hm[:, t, :] for t in range(NT)], 4, X, 4, f"g_mh_{l}", pdone, pdone)
            for c in range(2):
                gemm4("w_out_2", 2, 512, X, True, add_h(c), mb)
            if stop == f"Lattn{l}":
                return True
            F_ = phase(True)
            begin = all_done()
            xt = norm_T([H[:, t, :] for t in range(NT)], ND, f"g_mlp_{l}", begin, begin)
            relu_b = Ring([ar(3072 + 512 * j, 512) for j in range(4)])
            mid_free = [begin, begin]
            for q in range(DFF // 1024):
                mid = F_[q % 2]
                done_ = []
                for c in range(2):
                    def ev_relu(g, bank, tk, c=c):
                        bi, fb, ff = relu_b.take()
                        t1 = S(lambda e: e.activation(fb, bank[:, :], ACT.Relu), [tk] + ff + begin, own=False)
                        t2 = V(lambda e: e.tensor_tensor(fb, fb, fb, ALU.mult), [t1], own=False)
                        fh, fl = (f[:, 4 * c + g, :] for f in mid)
                        t3, t4 = split_f(fb, fh, fl, [t2], mid_free[q % 2])
                        relu_b.free(bi, [t4])
                        done_[:] = [t3, t4]
                        return [t1]
                    gemm4("w_ff1_2", 2, 512, X, False, ev_relu, xt)
                for c in range(2):
                    tk = gemm4("w_ff2_2", 2, 512, mid, True, add_h(c), done_)
                mid_free[q % 2] = [tk]
            if stop == f"Lff{l}":
                return True
            ple(f"g_ple_{l}", A["p2T"][l], A["b_ple_gate_2"][l:l + 1, :], all_done())
            return stop == f"layer{l}"

        def mlstm(qk, mv, lf, iT, cumF, lfb, Pb, PTb, small, hm, start):
            prob, ptr = Ring(Pb), Ring(PTb)
            lfm = {}

            def spread(h):
                i, buf, f = lfb.take()
                fr = list(f) + list(start)
                for rt in range(NT):
                    V(lambda e, rt=rt: e.tensor_scalar(buf[:, 384 + rt * 128:512 + rt * 128], cst("upto", 128),
                                                       lf[:, rt, h:h + 1], None, ALU.mult), fr, own=(rt == 0))
                    if rt < NT - 1:
                        V(lambda e, rt=rt: e.tensor_scalar(buf[:, rt * 128:(rt + 1) * 128], ones,
                                                           lf[:, rt, h:h + 1], None, ALU.mult), fr, own=False)
                lfm[h] = (i, buf, (V.key, V.count))

            units = [(h, qt) for h in range(4) for qt in range(NT)]
            st, ob = {}, {}
            mval = small[:, 64:80]
            nmv = small[:, 80:96]
            den = small[:, 96:112]
            em = small[:, 112:128]
            rin = small[:, 128:144]

            def scores(u):
                h, qt = units[u]
                w = causal_w(qt)
                if qt == 0:
                    spread(h)
                li, lb, lt = lfm[h]
                b, bank, bf = banks.take(SC)
                for rt in range(qt, -1, -1):
                    lhs = lb[:, 384 + rt * 128:512 + rt * 128] if rt == qt else lb[:, rt * 128:(rt + 1) * 128]
                    mm(bank[:, 0:(rt + 1) * 128], lhs, before(rt), rt == qt, False, [lt] + list(start) + bf)
                tk = mm(bank[:, 0:w], con[0:4, CC["head"] + 128 * h:CC["head"] + 128 * h + 128], iT[0:4, 0:w], False,
                        True, mark=True)
                if qt == NT - 1:
                    lfb.free(li, [tk])
                b2, bank2, bf2 = banks.take(SC)
                tk2 = mm(bank2[:, 0:w], qk[:, h, qt * 128:(qt + 1) * 128], qk[:, 4 + h, 0:w], True, True, bf2,
                         mark=True)
                i, pr, pf = prob.take()
                c = 4 * h + qt
                m, nm = mval[:, c:c + 1], nmv[:, c:c + 1]
                V(lambda e: e.tensor_tensor_reduce(pr[:, 0:w], bank[:, 0:w], mask(qt), 1.0, -3e38, ALU.add, ALU.max, m),
                  [tk] + pf + list(start))
                t1 = (V.key, V.count)
                V(lambda e: e.tensor_tensor(m, m, cumF[:, qt, h:h + 1], ALU.max))
                t2 = V(lambda e: e.tensor_scalar(nm, m, -1.0, None, ALU.mult))
                banks.free(b, [t1])
                t3 = S(lambda e: e.activation(pr[:, 0:w], pr[:, 0:w], ACT.Exp, bias=nm), [t2])
                st[u] = (i, pr, t3, b2, bank2, tk2)

            def turn(u):
                h, qt = units[u]
                w = causal_w(qt)
                i, pr, t3, b2, bank2, tk2 = st[u]
                dn = den[:, 4 * h + qt:4 * h + qt + 1]
                t4 = V(lambda e: e.tensor_tensor_reduce(pr[:, 0:w], bank2[:, 0:w], pr[:, 0:w], 128 ** -0.5, 0.0,
                                                        ALU.mult, ALU.add, dn), [t3, tk2])
                banks.free(b2, [t4])
                b, bank, bf = banks.take(SC)
                for c in range(w // 128):
                    tk = tp(bank[:, c * 128:(c + 1) * 128], pr[:, c * 128:(c + 1) * 128], 128, [t4] + bf,
                            mark=(c == w // 128 - 1))
                prob.free(i, [tk])
                j, pt, ptf = ptr.take()
                t5 = copy_out(pt[:, 0:w], bank[:, 0:w], [tk] + ptf)
                banks.free(b, [t5])
                st[u] = (j, pt, t5)

            def pv(u):
                h, qt = units[u]
                j, pt, t5 = st[u]
                if qt == 0:
                    ob[h] = banks.take(OB)
                b, bank, bf = ob[h]
                for c in range(qt + 1):
                    tk = mm(bank[:, qt * 128:(qt + 1) * 128], pt[:, c * 128:(c + 1) * 128],
                            mv[:, c, h * 128:(h + 1) * 128], c == 0, c == qt, [t5] + bf, mark=(c == qt))
                ptr.free(j, [tk])
                if qt == NT - 1:
                    s_ = slice(4 * h, 4 * h + 4)
                    S(lambda e: e.activation(em[:, s_], nmv[:, s_], ACT.Exp), [tk])
                    t6 = S(lambda e: e.activation(rin[:, s_], den[:, s_], ACT.Abs))
                    V(lambda e: e.tensor_tensor(rin[:, s_], rin[:, s_], em[:, s_], ALU.max), [t6])
                    V(lambda e: e.reciprocal(rin[:, s_], rin[:, s_]))
                    t7 = V(lambda e: e.tensor_tensor(
                        hm[:, :, h * 128:(h + 1) * 128], bank[:, :].rearrange("p (t d) -> p t d", t=NT),
                        rin[:, s_].unsqueeze(2).to_broadcast([P128, NT, 128]), ALU.mult))
                    banks.free(b, [t7])
                    st["end"] = t7

            n = len(units)
            for i in range(n + 2):
                if i < n:
                    scores(i)
                if 1 <= i < n + 1:
                    turn(i - 1)
                if i >= 2:
                    pv(i - 2)
            return st["end"]

        for l in range(2):
            if layer(l):
                break
        finish_with(H, all_done())
        return emit_all(nc, ctx, sem_names, P, V, S, G, Q)


def emit_all(nc, ctx, sem_names, P, V, S, G, Q):
    sems = {n: ctx.enter_context(nc.semaphore(f"s_{n}")) for n in sem_names}
    block = ctx.enter_context(nc.Block())

    @block.sync
    def _(e):
        Q.emit(e, sems)

    @block.tensor
    def _(e):
        P.emit(e, sems)

    @block.vector
    def _(e):
        V.emit(e, sems)

    @block.scalar
    def _(e):
        S.emit(e, sems)

    @block.gpsimd
    def _(e):
        G.emit(e, sems)


def host_arrays(i):
    def col(v):
        return np.asarray(v, np.float32).reshape(-1, P128).T
    parts = [col(i["g_mix"][0]), col(i["g_cq"][0]), col(i["g_ckv"][0]),
             np.concatenate([col(i["g_out_mla"][0]), col(i["g_out_dil"][0])], 1), col(i["g_ffn"][0]),
             col(i["g_ple"][0])]
    rows = [np.broadcast_to(i["g_final"][None, :], (P128, D))]
    for l in range(2):
        parts += [col(i["g_mix_2"][l]), col(i["g_cq_2"][l]), col(i["g_mh_2"][l].reshape(-1)), col(i["g_mlp_2"][l]),
                  col(i["g_ple_2"][l]), np.concatenate([col(i["conv_w_2"][l, j]) for j in range(4)], 1),
                  col(i["conv_b_2"][l])]
        r = np.concatenate([i["g_qn_2"][l], i["g_kn_2"][l], i["g_ik_2"][l], i["i_bias_2"][l], i["f_bias_2"][l],
                            np.zeros(8, np.float32)])
        rows.append(np.broadcast_to(r[None, :], (P128, 208)))
    kbd = np.zeros((P128, 256), np.float32)
    kbd[0:64, 0:128] = i["peer_keys1"][0].T
    kbd[64:128, 128:256] = i["peer_keys2"][0].T
    consts, dil = constants()
    c = np.ascontiguousarray
    return {
        "x": i["x"][0], "consts": consts, "dil_bias": dil, "gains": c(np.concatenate(parts, 1)),
        "rows": c(np.concatenate(rows, 1)), "w_in": i["w_in"][0], "w_uq": i["w_uq"][0], "w_ukv": i["w_ukv"][0],
        "w_out": i["w_out"][0], "w_peer_q": i["w_peer_q"][0], "peer_keys": kbd,
        "peer_uT": c(i["peer_u"][0].T), "peer_v": i["peer_v"][0], "w_ple_gate": i["w_ple_gate"][0],
        "w_ple_proj": i["w_ple_proj"][0], "pT": c(i["p"][0, 0].T),
        "pos": c(i["positions_2"][0].reshape(NT, P128).T),
        "p2T": c(i["p_2"][:, 0].transpose(0, 2, 1)), "w_in_2": i["w_in_2"], "w_q_up_2": i["w_q_up_2"],
        "w_iq_up_2": i["w_iq_up_2"], "w_out_2": i["w_out_2"], "w_ff1_2": i["w_ff1_2"], "w_ff2_2": i["w_ff2_2"],
        "w_ple_gate_2": i["w_ple_gate_2"], "b_ple_gate_2": i["b_ple_gate_2"], "w_ple_2": i["w_ple_2"],
    }


def kernel(**inputs):
    import concourse.bacc as bacc
    from concourse.bass_utils import run_bass_kernel_spmd

    nc = bacc.Bacc("TRN2", target_bir_lowering=False, num_devices=1)
    arrays, aps = {}, {}
    for name, a in host_arrays({k: np.asarray(v) for k, v in inputs.items()}).items():
        a = np.ascontiguousarray(a)
        arrays[name + "_dram"] = a
        aps[name] = nc.dram_tensor(name + "_dram", a.shape, mybir.dt.from_np(a.dtype), kind="ExternalInput").ap()
    out = nc.dram_tensor("out_dram", (T, D), F32, kind="ExternalOutput").ap()
    aps["out"] = out
    build(nc, aps)
    r = run_bass_kernel_spmd(nc, [arrays], core_ids=[0])
    return r.results[0]["out_dram"].reshape(1, T, D)
```

```python
from contextlib import ExitStack

import numpy as np

import concourse.bass as bass
from concourse import mybir

F32 = mybir.dt.float32
F32R = mybir.dt.float32r
I32 = mybir.dt.int32
U32 = mybir.dt.uint32
ALU = mybir.AluOpType
ACT = mybir.ActivationFunctionType
AX = mybir.AxisListType

P128 = 128
T = 512
NT = T // P128
D = 1024
ND = D // P128
EPS = 1e-6
NEG = -1e30
TAKEN = -3e38
PLE = 256

AHEAD_FIRST = 20
CHOICE_STEPS = 4
TB = 32
AREA, AREA_SMALL = 25300, 8800
TMP = 3072
TOP_1, TOP_2 = 20992, 21324

QR, KVR, RR = 384, 256, 32
MH, NOPE, VD = 8, 64, 64
QK = NOPE + RR
IN1 = QR + KVR + RR + 3 * 512
NE, KEYS, PH, TOPK = 16384, 128, 8, 16
ETG = 8
IN2 = 2640
NSEL = 128
IDX_SCALE = (8 ** -0.5) * (64 ** -0.5)
DFF = 4096

GC = {}


def _cols(layout):
    at = 0
    for name, n in layout:
        GC[name] = at
        at += n
    GC["g_out2"] = GC["g_out"] + 4 if "g_out" in GC else 0
    return at


N_GAIN = _cols([("g_mix", 8), ("g_cq", 3), ("g_ckv", 2), ("g_out", 8), ("g_ffn", 8), ("g_ple", 8)]
               + [(f"{n}_{l}", k) for l in range(2) for n, k in
                  [("g_mix", 8), ("g_cq", 2), ("g_mh", 4), ("g_mlp", 8), ("g_ple", 8), ("conv_w", 32),
                   ("conv_b", 8)]])
RC = {"g_final": 0}
for _l in range(2):
    RC[f"g_qn_{_l}"] = 1024 + 208 * _l
    RC[f"g_kn_{_l}"] = 1024 + 208 * _l + 64
    RC[f"g_ik_{_l}"] = 1024 + 208 * _l + 128
    RC[f"if_bias_{_l}"] = 1024 + 208 * _l + 192
N_ROW = 1024 + 2 * 208
CC = {"ident": 0, "iota": 128, "before": 256, "upto": 768, "causal": 896, "head": 1408, "iota16": 1920,
      "cos_m": 1936, "sin_m": 2000, "cos_d": 2064, "sin_d": 2096, "inv": 2128}
N_CONST = 2136


def constants():
    c = np.zeros((P128, N_CONST), np.float32)
    i = np.arange(P128)
    c[:, 0:128] = np.eye(P128)
    c[:, 128:256] = i[None, :]
    c[:, 256:640] = 1.0
    c[:, 640:768] = i[None, :] < i[:, None]
    c[:, 768:896] = i[:, None] <= i[None, :]
    c[:, 1280:1408] = np.where(i[None, :] <= i[:, None], 0.0, NEG)
    for h in range(4):
        c[h, 1408 + 128 * h:1536 + 128 * h] = 1.0
    c[:, 1920:1936] = np.arange(16)
    pos = np.arange(T, dtype=np.float32)

    def tables(rot):
        inv = np.float32(500000.0) ** (-np.arange(0, rot, 2, dtype=np.float32) / np.float32(rot))
        ang = (pos[:, None] * inv[None, :]).astype(np.float64)
        return inv, [f(ang).astype(np.float32).reshape(NT, P128, -1).transpose(1, 0, 2).reshape(P128, -1)
                     for f in (np.cos, np.sin)]
    _, (c[:, 1936:2000], c[:, 2000:2064]) = tables(32)
    inv, (c[:, 2064:2096], c[:, 2096:2128]) = tables(16)
    c[:, 2128:2136] = inv[None, :]
    q, k = np.arange(T)[:, None], np.arange(T)[None, :]
    n = np.zeros((T, T))
    for window, dil in ((128, 1), (512, 4), (2048, 16)):
        n += ((q - k) % dil == 0) & (np.abs(q - k) <= window // 2)
    bias = np.where(n > 0, np.log(np.maximum(n, 1)) * 8.0, NEG).astype(np.float32)
    return c, bias


def weight_plan(A):
    plan = []

    def add(name, W, c0, n, rows=None):
        r0, r1 = rows or (0, W.shape[0])
        for k in range(r0, r1, 512):
            m = min(512, r1 - k)
            plan.append((name, W[k:k + m, c0:c0 + n], m // P128, n))
    for c0 in range(0, IN1, 512):
        add("w_in", A["w_in"], c0, min(512, IN1 - c0))
        for c in range(2 if c0 == 512 else 0):
            add("w_uq", A["w_uq"], 384 * c, 384)
    for c in range(2):
        add("w_ukv", A["w_ukv"], 512 * c, 512)
    for name in ("w_out", "w_peer_q"):
        for c in range(2):
            add(name, A[name], 512 * c, 512)

    def up(g):
        for u in range(ETG // 4):
            add("peer_uT", A["peer_uT"], (g * ETG + 4 * u) * 128, 512)
    ngroups = KEYS // ETG
    for g in range(0, ngroups, 2):
        up(g)
    for g in range(ngroups):
        if g + 1 < ngroups and (g + 1) % 2:
            up(g + 1)
        for c in range(2):
            add("peer_v", A["peer_v"], 512 * c, 512, (g * ETG * 128, (g + 1) * ETG * 128))
    for c in range(2):
        add("w_gate", A["w_ple_gate"], 512 * c, 512)
        add("w_proj", A["w_ple_proj"], 512 * c, 512)
    for l in range(2):
        W = A["w_in_2"][l]
        add("w_in_2", W, 0, 512)
        for k in range(2):
            plan.append(("w_in_2 b", [(0, 72, W[512 * k:512 * k + 512, 512:584]),
                                      (72, 80, W[512 * k:512 * k + 512, 2632:2640])], 4, 80))
        add("w_q_up_2", A["w_q_up_2"][l], 0, 512)
        add("w_iq_up_2", A["w_iq_up_2"][l], 0, 512)
        for c in range(4):
            add("w_in_2", W, 584 + 512 * c, 512)
        for c in range(2):
            add("w_out_2", A["w_out_2"][l], 512 * c, 512)
        for q in range(-1, DFF // 1024):
            for c in range(2 if q + 1 < DFF // 1024 else 0):
                add("w_ff1_2", A["w_ff1_2"][l], 1024 * (q + 1) + 512 * c, 512)
            for c in range(2 if q >= 0 else 0):
                add("w_ff2_2", A["w_ff2_2"][l], 512 * c, 512, (1024 * q, 1024 * (q + 1)))
        for c in range(2):
            add("w_gate", A["w_ple_gate_2"][l], 512 * c, 512)
            add("w_proj", A["w_ple_2"][l], 512 * c, 512)
    return plan


class Engine:

    def __init__(self, key, own):
        self.key, self.own, self.count, self.items, self.waited = key, own, 0, [], {}

    def __call__(self, fn, after=(), own=None, mark=True, dma=None):
        need = {}

        def add(x):
            if x is None:
                return
            if isinstance(x, list):
                for y in x:
                    add(y)
            else:
                need[x[0]] = max(need.get(x[0], 0), x[1])
        add(list(after) if isinstance(after, tuple) and not (after and isinstance(after[0], str)) else after)
        if (self.own if own is None else own) and self.count:
            add((self.key, self.count))
        waits = []
        for k, v in need.items():
            if v > 0 and self.waited.get(k, 0) < v:
                self.waited[k] = v
                waits.append((k, v))
        if dma is not None:
            self.items.append((fn, waits, (dma[0], 16)))
            return dma
        if mark:
            self.count += 1
        self.items.append((fn, waits, (self.key, 1) if mark else None))
        return (self.key, self.count) if mark else None

    def emit(self, eng, sems):
        for fn, waits, inc in self.items:
            for k, v in waits:
                eng.wait_ge(sems[k], v)
            ins = fn(eng)
            if inc:
                ins.then_inc(sems[inc[0]], inc[1])


class Ring:

    def __init__(self, bufs):
        self.bufs, self.at = bufs, 0
        self.freed = [[] for _ in bufs]

    def take(self):
        i = self.at % len(self.bufs)
        self.at += 1
        assert self.freed[i] is not None, "taken before it was given back"
        f, self.freed[i] = self.freed[i], None
        return i, self.bufs[i], f

    def free(self, i, toks):
        self.freed[i] = toks


class Tiles(list):
    pass


class Banks:

    def __init__(self, banks):
        self.banks, self.freed, self.at = banks, [[] for _ in banks], {}

    def take(self, among=tuple(range(8))):
        n = self.at.get(among, 0)
        self.at[among] = n + 1
        i = among[n % len(among)]
        assert self.freed[i] is not None, "bank taken before it was given back"
        f, self.freed[i] = self.freed[i], None
        return i, self.banks[i], f

    def free(self, i, toks):
        self.freed[i] = toks


def build(nc, A, stop=None):
    with ExitStack() as ctx:
        def sb(name, words, dt=F32):
            return ctx.enter_context(nc.sbuf_tensor(name, [P128, words], dt))

        H = sb("h", NT * D)[:, :].rearrange("p (t d) -> p t d", t=NT)
        X = tuple(sb(n, ND * T, F32R)[:, :].rearrange("p (c t) -> p c t", c=ND) for n in ("x_hi", "x_lo"))
        wraw = [sb(f"w_raw{i}", 2048) for i in range(2)]
        wspl = [(sb(f"w_hi{i}", 2048, F32R), sb(f"w_lo{i}", 2048, F32R)) for i in range(2)]
        con = sb("con", N_CONST)
        gain = sb("gain", N_GAIN)
        row = sb("row", 208)
        stat = sb("stat", 512)
        stat_rope = sb("rope2", 64)
        tmp = sb("tmp", TMP)
        scope, arena = [], []

        def end_phase():
            while scope:
                scope.pop().__exit__(None, None, None)
        ctx.callback(end_phase)

        def new(name, words, dt):
            c = nc.sbuf_tensor(f"{name}_{phases[0]}", [P128, words], dt)
            scope.append(c)
            return c.__enter__()

        def phase(split, top=None):
            end_phase()
            arena.clear()
            phases[0] += 1
            out = None
            if split:
                out = [tuple(new(f"f_{p}{i}", 4096, F32R)[:, :].rearrange("p (e t) -> p e t", e=8)
                             for p in ("hi", "lo")) for i in range(2)]
                arena.append(new("area", AREA_SMALL - TMP, F32))
            else:
                top_at[:] = [top or AREA]
                arena.append(new("area", top_at[0] - TMP, F32))
                if top:
                    arena.append(new("area_top", AREA - top, F32))
            return out

        def top_for_cq(on, nd=2):
            scope.pop().__exit__(None, None, None)
            if not on:
                scope.pop().__exit__(None, None, None)
                arena.append(new("area_top2", AREA - top_at[0], F32))
                return None
            arena.pop()
            return tuple(new(f"cq_{p}", nd * T, F32R)[:, :].rearrange("p (c t) -> p c t", c=nd) for p in ("hi", "lo"))
        phases, top_at = [0], []
        phase(False, TOP_1)
        banks = Banks([ctx.enter_context(nc.psum_tensor(f"bank{i}", [P128, 512], F32)) for i in range(8)])
        a_scratch = nc.dram_tensor("a_scratch", (KEYS // 2, KEYS, T), F32, kind="Internal").ap()
        g_scratch = nc.dram_tensor("g_scratch", (T // TB, KEYS, KEYS, TB), F32, kind="Internal").ap()

        def ar(at, n):
            if at < TMP:
                assert at + n <= TMP
                return tmp[:, at:at + n]
            if at >= top_at[0] and len(arena) == 2:
                return arena[1][:, at - top_at[0]:at - top_at[0] + n]
            return arena[0][:, at - TMP:at - TMP + n]

        P, V, S, G, Q = (Engine(k, own) for k, own in
                         [("pe", False), ("dve", True), ("act", True), ("pool", True), ("sp", False)])
        sem_names = ["pe", "dve", "act", "pool", "sp"]
        dma_count = {}

        def dma(out, in_, sem, after=(), q=None):
            if sem not in dma_count:
                dma_count[sem] = 0
                sem_names.append(sem)
            dma_count[sem] += 16
            return (q or Q)(lambda e: e.dma_start(out, in_), after, dma=(sem, dma_count[sem]))

        ident = con[:, 0:128]

        def cst(name, n, p=P128):
            return con[0:p, CC[name]:CC[name] + n]

        def load_h(t):
            return dma(H[:, t, :], A["x"][t * P128:(t + 1) * P128], f"h{t}_in")
        t_h = [load_h(0)]
        t_ident = dma(con[:, 0:P128], A["consts"][:, 0:P128], "ident_in")
        t_gain = dma(gain[:, :], A["gains"], "gain_in")

        raw_ring = Ring([w[:, :] for w in wraw])
        spl_ring = Ring([(a[:, :], b[:, :]) for a, b in wspl])
        plan = weight_plan(A)
        fetched = []

        def fetch():
            if not plan:
                return
            name, src, nk, n = plan.pop(0)
            ri, raw, rfree = raw_ring.take()
            si, (hi, lo), sfree = spl_ring.take()
            r3 = raw[:, 0:nk * n].rearrange("p (k n) -> p k n", k=nk)
            for a, b, s_ in (src if isinstance(src, list) else [(0, n, src)]):
                tw = dma(r3[:, :, a:b], s_.rearrange("(k p) n -> p k n", p=P128), f"w_raw{ri}_in", after=rfree)
            h_, l_, r_ = hi[:, 0:nk * n], lo[:, 0:nk * n], raw[:, 0:nk * n]
            th = S(lambda e: e.activation(h_, r_, ACT.Copy), [tw] + sfree, own=False)
            tl = G(lambda e: e.tensor_tensor(l_, r_, h_.bitcast(F32), ALU.subtract), [tw, th] + sfree, own=False)
            raw_ring.free(ri, [th, tl])
            fetched.append((name, si, h_.rearrange("p (k n) -> p k n", k=nk), l_.rearrange("p (k n) -> p k n", k=nk),
                            nk, [th, tl]))

        def take_w(name):
            if not fetched:
                fetch()
            got = fetched.pop(0)
            assert got[0] == name, (got[0], name)
            return got[1:]

        def give_w(si, toks):
            spl_ring.free(si, toks)
            fetch()

        held = []

        def release():
            while held:
                give_w(*held.pop(0))

        state = {"turn": 0}

        def copy_out(dst, src, after):
            state["turn"] ^= 1
            if state["turn"]:
                return V(lambda e: e.tensor_copy(dst, src), after)
            return S(lambda e: e.activation(dst, src, ACT.Copy), after)

        def mm(out, lhsT, rhs, start, stop, after=(), mark=False):
            return P(lambda e: e.matmul(out, lhsT, rhs, start=start, stop=stop), after, mark=mark)

        def tp(out, in_, k, after=(), mark=False):
            return P(lambda e: e.transpose(out, in_, ident[0:k, 0:k]), after, mark=mark)

        def rstd_of(ss, width, out, tmp, after=()):
            a, b, c = tmp
            V(lambda e: e.tensor_scalar(a, ss, 1.0 / width, EPS, ALU.mult, ALU.add), after)
            t = (V.key, V.count)
            t = S(lambda e: e.activation(b, a, ACT.Sqrt), [t])
            V(lambda e: e.reciprocal(c, b), [t])
            V(lambda e: e.tensor_tensor(c, a, c, ALU.mult))
            V(lambda e: e.tensor_tensor(c, b, c, ALU.add))
            V(lambda e: e.tensor_scalar(c, c, 0.5, None, ALU.mult))
            return V(lambda e: e.reciprocal(out, c))

        st_ss, st_a, st_b, st_c, st_r = (stat[:, 64 * i:64 * i + 64] for i in range(5))
        st_mx, st_nm, st_sum = stat[:, 320:352], stat[:, 352:384], stat[:, 384:416]
        st_x = stat[:, 416:512]

        last_x = []
        xs = Ring([0, 1024])
        xfull = Ring([2048, 2560])
        norms = [0]

        class Rows:

            def __init__(self, srcs, nd, gname, c_at=0, dst=None, norm=True, early=(),
                         among=tuple(range(8))):
                self.srcs, self.nd, self.gname, self.c_at, self.dst, self.norm = srcs, nd, gname, c_at, dst or X, norm
                self.early, self.x, self.toks, self.pending = list(early), {}, Tiles([[] for _ in range(NT)]), []
                self.among = among
                norms[0] += 1
                self.col = 40 + 4 * (norms[0] % 6)

            def square(self, t, after):
                if not self.norm:
                    self.x[t] = (None, self.srcs[t], list(after) + self.early)
                    return
                xi, at, xf = xs.take()
                x, ss = ar(at, self.nd * P128), st_ss[:, self.col + t:self.col + t + 1]
                t1 = S(lambda e: e.activation(x, self.srcs[t], ACT.Square, accum_out=ss), [after, self.early, xf])
                self.x[t] = (xi, x, [t1])

            def scale(self, t):
                if not self.norm:
                    return
                xi, x, t1 = self.x[t]
                ss, a, b, c, r = (st[:, self.col + t:self.col + t + 1] for st in (st_ss, st_a, st_b, st_c, st_r))
                tr = rstd_of(ss, self.nd * P128, r, (a, b, c), t1)
                t2 = S(lambda e: e.activation(x, self.srcs[t], ACT.Copy, scale=r), [tr])
                self.x[t] = (xi, x, [t2])
                if t == NT - 1:
                    release()

            def turn(self, t):
                xi, x, ready = self.x[t]
                for c0 in range(0, self.nd, 4):
                    n = min(4, self.nd - c0)
                    b, bank, bf = banks.take(self.among)
                    for c in range(n):
                        tk = tp(bank[:, c * 128:(c + 1) * 128], x[:, (c0 + c) * 128:(c0 + c + 1) * 128], 128,
                                [ready, bf, t_ident], mark=(c == n - 1))
                    hi, lo = (d[:, self.c_at + c0:self.c_at + c0 + n, t * 128:(t + 1) * 128] for d in self.dst)
                    inn = bank[:, 0:n * 128].rearrange("p (c t) -> p c t", c=n)
                    fi, fat, ff = xfull.take()
                    full = ar(fat, n * 128).rearrange("p (c t) -> p c t", c=n)
                    if self.gname is None:
                        t1 = V(lambda e, full=full, inn=inn: e.tensor_copy(full, inn), [tk, ff, self.early], own=False)
                    else:
                        at = GC[self.gname] + c0
                        g = gain[:, at:at + n].unsqueeze(2).to_broadcast([P128, n, 128])
                        t1 = V(lambda e, full=full, inn=inn, g=g: e.tensor_tensor(full, inn, g, ALU.mult),
                               [tk, t_gain, ff, self.early], own=False)
                    banks.free(b, [t1])
                    t2 = S(lambda e, full=full, hi=hi: e.activation(hi, full, ACT.Copy), [t1], own=False)
                    self.rest()
                    self.pending = [(t, fi, full, hi, lo, t2)]
                    xfull.free(fi, None)
                if xi is not None:
                    xs.free(xi, [tk])
                last_x[:] = [tk]

            def rest(self):
                for t, fi, full, hi, lo, t2 in self.pending:
                    t3 = V(lambda e: e.tensor_tensor(lo, full, hi.bitcast(F32), ALU.subtract), [t2], own=False)
                    xfull.free(fi, [t3])
                    self.toks[t] = [t2, t3]
                    last_x[1:] = [t2, t3]

            def advance(self, t, after):
                if t >= 1:
                    self.scale(t - 1)
                if t >= 2:
                    self.turn(t - 2)
                self.square(t, after)

            def finish(self, scaled=False):
                if not scaled:
                    self.scale(NT - 1)
                self.turn(NT - 2)
                self.turn(NT - 1)
                self.rest()
                return self.toks

            def all(self, after):
                for t in range(NT):
                    self.advance(t, after)
                return self.finish()

        def tiles(x):
            return [x[:, t, :] for t in range(NT)]

        def gemm4(*args, **kw):
            for tk in gemm4_steps(*args, **kw):
                pass
            return tk

        def gemm4_behind(rows, name, ntiles, n, evict, **kw):
            product = gemm4_steps(name, ntiles, n, rows.dst, True, evict, rows.toks, **kw)
            rows.scale(NT - 1)
            next(product)
            rows.turn(NT - 2)
            next(product)
            rows.turn(NT - 1)
            next(product)
            rows.rest()
            for tk in product:
                pass
            return tk

        def gemm4_steps(name, ntiles, n, x, tokens_out, evict, after, bias=None, bias_after=(), k0=0,
                        among=tuple(range(8)), hold=False):
            bb = [banks.take(among) for _ in range(4)]
            for i in range(ntiles):
                si, wh, wl, nk, tw = take_w(name)
                for g in range(4):
                    b, bank, bf = bb[g]
                    for k in range(nk):
                        xs = [p[:, k0 + k, :] for p in x]
                        if tokens_out:
                            st_ = [p[:, g * 128:(g + 1) * 128] for p in xs]
                            mv_ = [wh[:, k, 0:n], wl[:, k, 0:n]]
                            out = bank[:, 0:n]
                        else:
                            st_ = [wh[:, k, g * 128:(g + 1) * 128], wl[:, k, g * 128:(g + 1) * 128]]
                            mv_, out = xs, bank[:, :]
                        now = after.get(i, []) if isinstance(after, dict) else after if i == 0 else []
                        now = list(now[g] if tokens_out and isinstance(now, Tiles) else now)
                        for a_, b_ in ((0, 1), (0, 0), (1, 0)):
                            first = i == 0 and k == 0 and (a_, b_) == (0, 1)
                            last = i == ntiles - 1 and k == nk - 1 and a_ == 1
                            tk = mm(out, st_[a_], mv_[b_], first, last and bias is None,
                                    (now if k == 0 else []) + (bf if first else []) + tw,
                                    mark=(k == nk - 1 and a_ == 1))
                    if i == ntiles - 1:
                        if bias is not None:
                            tk = mm(out, con[0:1, CC["head"]:CC["head"] + 128], bias, False, True, bias_after, mark=True)
                        banks.free(b, evict(g, bank, tk))
                    if g == 3 and hold and i == ntiles - 1:
                        held.append((si, [tk]))
                    elif g == 3:
                        give_w(si, [tk])
                    yield tk
                k0 += nk

        def rope(x1, x2, o1, o2, c, s, tmp, after=()):
            a, b, cc, d = tmp
            V(lambda e: e.tensor_tensor(a, x1, c, ALU.mult), after)
            V(lambda e: e.tensor_tensor(b, x2, s, ALU.mult), own=False)
            V(lambda e: e.tensor_tensor(cc, x2, c, ALU.mult), own=False)
            V(lambda e: e.tensor_tensor(d, x1, s, ALU.mult), own=False)
            V(lambda e: e.tensor_tensor(o1, a, b, ALU.subtract))
            return V(lambda e: e.tensor_tensor(o2, cc, d, ALU.add))

        SC, OB = (0, 1, 2, 3, 4, 5), (6, 7)

        def attend(heads, dv, prep, v, bias, width, Pb, PTb, done, after):
            prob, ptr = Ring(Pb), Ring(PTb)
            units = [(h, qt) for h in range(heads) for qt in range(NT)]
            st, obank, qk_of = {}, {}, {0: prep(0)}

            def scores(u):
                h, qt = units[u]
                w = width(qt)
                q_, k_, tqk = qk_of[h]
                b, bank, bf = banks.take(SC)
                tk = mm(bank[:, 0:w], q_[:, qt * 128:(qt + 1) * 128], k_[:, 0:w], True, True,
                        list(after) + bf + tqk, mark=True)
                if qt == 1 and h + 1 < heads:
                    qk_of[h + 1] = prep(h + 1)
                i, pr, pf = prob.take()
                par = u % 4
                mx, nm = st_mx[:, par:par + 1], st_nm[:, par:par + 1]
                bb, t_bias, scale = bias(h, qt, w)
                if bb is None:
                    V(lambda e: e.tensor_reduce(mx, bank[:, 0:w], AX.X, ALU.max), [tk])
                    src = bank[:, 0:w]
                else:
                    V(lambda e: e.tensor_tensor_reduce(pr[:, 0:w], bank[:, 0:w], bb, 1.0, -3e38, ALU.add, ALU.max,
                                                       mx), [tk] + pf + list(after) + t_bias)
                    src = pr[:, 0:w]
                t2 = V(lambda e: e.tensor_scalar(nm, mx, -scale, None, ALU.mult),
                       st.get(("exp", u - 4), []))
                at = (h % 2) * 8 + qt
                sm = st_sum[:, at:at + 1]
                t3 = S(lambda e: e.activation(pr[:, 0:w], src, ACT.Exp, bias=nm, scale=scale, accum_out=sm),
                       [t2] + pf + st.get(("sum", h - 2), []))
                st["exp", u] = [t3]
                banks.free(b, [t2, t3])
                st[u] = (i, pr, t3)

            def turn(u):
                h, qt = units[u]
                w = width(qt)
                i, pr, t3 = st[u]
                b, bank, bf = banks.take(SC)
                for c in range(w // 128):
                    tk = tp(bank[:, c * 128:(c + 1) * 128], pr[:, c * 128:(c + 1) * 128], 128, [t3] + bf,
                            mark=(c == w // 128 - 1))
                prob.free(i, [tk])
                j, pt, ptf = ptr.take()
                t4 = copy_out(pt[:, 0:w], bank[:, 0:w], [tk] + ptf)
                banks.free(b, [t4])
                st[u] = (j, pt, t4)

            def pv(u):
                h, qt = units[u]
                w = width(qt)
                j, pt, t4 = st[u]
                if qt == 0:
                    obank[h] = banks.take(OB)
                b, bank, bf = obank[h]
                n = w // 128
                for c in range(n):
                    tk = mm(bank[:, qt * dv:(qt + 1) * dv], pt[:, c * 128:(c + 1) * 128], v(h, c), c == 0, c == n - 1,
                            [t4] + bf, mark=(c == n - 1))
                ptr.free(j, [tk])
                if qt == NT - 1:
                    tok = done(h, bank, tk)
                    banks.free(b, [tok])
                    st["sum", h] = [tok]
                    st["end"] = tok

            n = len(units)
            for i in range(n + 4):
                if i < n:
                    scores(i)
                if 2 <= i < n + 2:
                    turn(i - 2)
                if i >= 4:
                    pv(i - 4)
            return st["end"]

        def scaled_out(dst, dv):
            def done(h, bank, tk):
                at = (h % 2) * 8
                r = st_x[:, 0:NT]
                V(lambda e: e.reciprocal(r, st_sum[:, at:at + NT]), [tk, (S.key, S.count)])
                return V(lambda e: e.tensor_tensor(dst(h), bank[:, 0:NT * dv].rearrange("p (t d) -> p t d", t=NT),
                                                   r.unsqueeze(2).to_broadcast([P128, NT, dv]), ALU.mult), [tk])
            return done

        def head_T(srcs, dst, after, free):
            n = srcs[0].shape[-1]
            b, bank, bf = banks.take(SC)
            for t in range(NT):
                tk = tp(bank[0:n, t * 128:(t + 1) * 128], srcs[t], 128, list(after) + bf, mark=(t == NT - 1))
            t2 = copy_out(dst[0:n, :], bank[0:n, :], [tk] + list(free))
            banks.free(b, [t2])
            return [t2]

        def soft_bufs(at):
            return [ar(at + 512 * j, 512) for j in range(4)], [ar(at + 2048 + 512 * j, 512) for j in range(3)]

        def finish_with(src, after):
            t = dma(A["out"].rearrange("(t p) d -> p t d", p=P128), src, "out_st", after=after)
            Q(lambda e: e.nop(), [t])

        all_done = lambda: [(E.key, E.count) for E in (P, V, S, G) if E.count]

        t_h.append(load_h(1))
        fetch()
        t_h += [load_h(2), load_h(3)]
        fetch()
        t_con = dma(con[:, P128:N_CONST], A["consts"][:, P128:N_CONST], "con_in")
        nrm = Rows(tiles(H), ND, "g_mix")
        for t in range(NT):
            nrm.advance(t, [t_h[t]])
        lat = ar(3072, 4 * 672).rearrange("p (t n) -> p t n", t=NT)
        qkvd = ar(6656, 4 * 1536).rearrange("p (t n) -> p t n", t=NT)

        cq_split = top_for_cq(True, 3)
        rows_q = Rows([lat[:, t, 0:QR] for t in range(NT)], 3, "g_cq", dst=cq_split)
        rows_kv = Rows([lat[:, t, QR:QR + KVR] for t in range(NT)], 2, "g_ckv", c_at=3)

        def to_proj(c0, n, lat_ready):
            def ev(t, bank, tk):
                toks = []
                for lo, hi, dst, off in ((0, 672, lat, 0), (672, IN1, qkvd, 672)):
                    a, b = max(lo, c0), min(hi, c0 + n)
                    if a < b:
                        toks.append(copy_out(dst[:, t, a - off:b - off], bank[:, a - c0:b - c0], [tk] + toks))
                if c0 == 0:
                    rows_q.advance(t, toks)
                if c0 + n == IN1:
                    rows_kv.advance(t, lat_ready)
                return toks
            return ev
        qtok = ar(12800, NT * 768).rearrange("p (t n) -> p t n", t=NT)
        ktok = ar(15872, NT * 768).rearrange("p (t n) -> p t n", t=NT)
        vtok = ar(18944, NT * 512).rearrange("p (t n) -> p t n", t=NT)

        def cs(name, half, nh):
            v = con[:, CC[name]:CC[name] + NT * half].rearrange("p (t r) -> p t r", t=NT)
            return v.unsqueeze(2).to_broadcast([P128, NT, nh, half])

        def rv(x, nh, hd, lo, half):
            return x.rearrange("p t (h x) -> p t h x", h=nh)[:, :, :, lo:lo + half]

        def rt(nh, half):
            return [r[:, 0:NT * nh * half].rearrange("p (t h x) -> p t h x", t=NT, h=nh) for r in rtmp()]

        def rtmp():
            return [ar(20992 + 512 * j, 512) for j in range(4)]

        for c0 in range(0, IN1, 512):
            n = min(512, IN1 - c0)
            to = to_proj(c0, n, [(V.key, V.count), (S.key, S.count)])
            if c0 == 0:
                gemm4_behind(nrm, "w_in", 2, n, to, hold=True)
                rows_q.scale(NT - 1)
            elif c0 == 512:
                product = gemm4_steps("w_in", 2, n, X, True, to, [])
                next(product)
                a = rows_q.finish(scaled=True)
                for _ in product:
                    pass
                for c in range(2):
                    gemm4("w_uq", 1, 384, cq_split, True, lambda t, bank, tk, c=c: [
                        copy_out(qtok[:, t, c * 384:(c + 1) * 384], bank[:, 0:384], [tk])], a)
                top_for_cq(False)
                q1, q2 = rv(qtok, 8, QK, 64, 16), rv(qtok, 8, QK, 80, 16)
                rope(q1, q2, q1, q2, cs("cos_m", 16, 8), cs("sin_m", 16, 8), rt(8, 16), [(V.key, V.count), (S.key, S.count), t_con])
                k1, k2 = (lat[:, :, 640 + 16 * j:656 + 16 * j].unsqueeze(2) for j in range(2))
                rope(k1, k2, k1, k2, cs("cos_m", 16, 1), cs("sin_m", 16, 1), rt(1, 16))
                for t in range(NT):
                    roped = V(lambda e, t=t: e.tensor_copy(
                        ktok[:, t, :].rearrange("p (h x) -> p h x", h=8)[:, :, 64:96],
                        lat[:, t, 640:672].unsqueeze(1).to_broadcast([P128, 8, 32])))
            else:
                gemm4("w_in", 2, n, X, True, to, [], hold=c0 + n == IN1)

        def ev_kv(c):
            def ev(t, bank, tk):
                src = bank[:, :].rearrange("p (h x) -> p h x", h=4)
                kd = ktok[:, t, c * 384:(c + 1) * 384].rearrange("p (h x) -> p h x", h=4)[:, :, 0:64]
                vd = vtok[:, t, c * 256:(c + 1) * 256].rearrange("p (h x) -> p h x", h=4)
                t1 = V(lambda e: e.tensor_copy(kd, src[:, :, 0:64]), [tk])
                return [t1, S(lambda e: e.activation(vd, src[:, :, 64:128], ACT.Copy), [tk, t1])]
            return ev
        gemm4_behind(rows_kv, "w_ukv", 1, 512, ev_kv(0), k0=3)
        gemm4("w_ukv", 1, 512, X, True, ev_kv(1), [], k0=3)
        both = [(V.key, V.count), (S.key, S.count)]
        kv_there = list(both)
        for off in (0, 512):
            x = qkvd[:, :, off:off + 512]
            x1, x2 = rv(x, 8, 64, 0, 8), rv(x, 8, 64, 8, 8)
            roped_d = rope(x1, x2, x1, x2, cs("cos_d", 8, 8), cs("sin_d", 8, 8), rt(8, 8))
        mixed = ar(20992, 4096).rearrange("p (t n) -> p t n", t=NT)
        Pb, PTb = soft_bufs(3072)
        heads_at = [(ar(1024 * j, 512), ar(1024 * j + 512, 512)) for j in range(2)]

        def prep_m(h):
            qd, kd = heads_at[h % 2]
            before_ = [(P.key, P.count)]
            ta = head_T([qtok[:, t, h * QK:(h + 1) * QK] for t in range(NT)], qd, [roped] + kv_there, before_)
            tb_ = head_T([ktok[:, t, h * QK:(h + 1) * QK] for t in range(NT)], kd, [roped] + kv_there, before_)
            return qd[0:QK, :], kd[0:QK, :], ta + tb_
        dbias = ar(12800, 2048).rearrange("p (t n) -> p t n", t=NT)
        tm, t_dbias, mla_end, pair = {}, [], [], {}

        def prep_pairs(q_src, k_src, slots, after):
            def prep(h):
                if h % 2 == 0:
                    qd, kd = slots[h // 2 % 2]
                    before_ = [(P.key, P.count)]
                    ta = head_T(q_src(h // 2), qd, after, before_)
                    tb_ = head_T(k_src(h // 2), kd, after, before_) if k_src else []
                    pair[0] = (qd, kd, ta + tb_)
                qd, kd, tt = pair[0]
                lo = 64 * (h % 2)
                return qd[lo:lo + 64, :], kd[lo:lo + 64, :], tt
            return prep
        slots_d = [(ar(15872 + 1024 * j, 512), ar(15872 + 1024 * j + 512, 512)) for j in range(2)]
        prep_d = prep_pairs(lambda j: [qkvd[:, t, j * 128:(j + 1) * 128] for t in range(NT)],
                            lambda j: [qkvd[:, t, 512 + j * 128:640 + j * 128] for t in range(NT)], slots_d, [roped_d])
        half = [Rows([mixed[:, t, 512 * j:512 * j + 512] for t in range(NT)], 4, g, c_at=4 * j, among=a)
                for j, g, a in ((0, "g_out", SC), (1, "g_out2", tuple(range(8))))]
        out = scaled_out(lambda h: mixed[:, :, h * 64:(h + 1) * 64], 64)

        def prep_both(h):
            if h < MH:
                return prep_m(h)
            if h == MH:
                t_dbias[:] = [dma(dbias, A["dil_bias"].rearrange("(t p) k -> p t k", p=P128), "dbias_in",
                                  after=[(P.key, P.count)])]
            return prep_d(h - MH)

        def v_both(h, c):
            return vtok[:, c, h * 64:(h + 1) * 64] if h < MH else qkvd[:, c, 512 + h * 64:576 + h * 64]

        def bias_both(h, qt, w):
            return (None, [], QK ** -0.5) if h < MH else (dbias[:, qt, 0:w], t_dbias, 0.125)

        def done_both(h, bank, tk):
            t1 = out(h, bank, tk)
            if h == MH - 1:
                mla_end[:] = [t1]
            elif MH <= h < MH + NT:
                half[0].advance(h - MH, mla_end)
            elif h == MH + NT:
                half[0].scale(NT - 1)
                half[0].turn(NT - 2)
            elif h == MH + NT + 1:
                half[0].turn(NT - 1)
                half[0].rest()
                tm[0] = half[0].toks
            return t1
        end = attend(16, 64, prep_both, v_both, bias_both, lambda qt: T, Pb, PTb, done_both, [])
        att_end = [end, (P.key, P.count)]
        def add_h(c, rows=None):
            def ev(t, bank, tk):
                dst = H[:, t, c * 512:(c + 1) * 512]
                t1 = V(lambda e: e.tensor_tensor(dst, bank[:, :], dst, ALU.add), [tk])
                if c == 1 and rows is not None:
                    rows.advance(t, [t1])
                return [t1]
            return ev
        product = gemm4_steps("w_out", 2, 512, X, True, add_h(0), tm)
        for t in range(NT):
            next(product)
            half[1].advance(t, att_end)
        tm[1] = half[1].finish()
        for _ in product:
            pass
        before_last = all_done()
        rows_ffn = Rows(tiles(H), ND, "g_ffn")
        gemm4("w_out", 2, 512, X, True, add_h(1, rows_ffn), tm, hold=True)
        xt = rows_ffn.finish()
        if stop == "attn1":
            finish_with(H, all_done())
            return emit_all(nc, ctx, sem_names, P, V, S, G, Q)

        phase(False)
        qpT = ar(3072, 4096).rearrange("p (h t) -> p h t", h=PH)
        kbd = ar(7168, 256)
        t_kbd = dma(kbd, A["peer_keys"], "kbd_in", after=before_last)
        for c in range(2):
            gemm4("w_peer_q", 2, 512, X, False, lambda g, bank, tk, c=c: [
                copy_out(qpT[:, 4 * c + g, :], bank[:, :], [tk])], xt)
        qtoks = [(V.key, V.count), (S.key, S.count)]
        sc = ar(7424, 2048).rearrange("p (l k) -> p l k", l=16)
        s2 = ar(9472, 2048).rearrange("p (l k) -> p l k", l=16)
        v16 = ar(11520, 256).rearrange("p (l k) -> p l k", l=16)
        i16 = ar(11776, 256).bitcast(U32).rearrange("p (l k) -> p l k", l=16)
        i16f = ar(12032, 256).rearrange("p (l k) -> p l k", l=16)
        cand = ar(7424, 2048).rearrange("p (h c) -> p h c", h=8)
        cnd2 = ar(9472, 2048).rearrange("p (h c) -> p h c", h=8)
        top = ar(12288, 128).rearrange("p (h k) -> p h k", h=8)
        pos = ar(12416, 128).bitcast(U32).rearrange("p (h k) -> p h k", h=8)
        pj = [ar(12544 + 128 * j, 128).bitcast(U32) for j in range(2)]
        pf = [ar(12800 + 128 * j, 128) for j in range(2)]
        sel = [ar(13056 + 128 * j, 128) for j in range(3)]
        selT = [ar(13440 + 512 * j, 512) for j in range(3)]
        iota16 = con[:, CC["iota16"]:CC["iota16"] + 16].unsqueeze(1).to_broadcast([P128, 128, 16])

        def top16(lists):
            t1, t2, t3 = [], [], []
            for v, i, s, k, w in lists:
                t1.append(V(lambda e, v=v, s=s: e.max(v[:, 0:8], s), w, own=False))
                yield
            for (v, i, s, k, w), t in zip(lists, t1):
                V(lambda e, v=v, s=s, i=i: e.max_index(i[:, 0:8], v[:, 0:8], s), [t], own=False)
                yield
            for (v, i, s, k, w), t in zip(lists, t1):
                t2.append(V(lambda e, v=v, s=s, k=k: e.match_replace(k, v[:, 0:8], s, TAKEN), [t], own=False))
                yield
            for (v, i, s, k, w), t in zip(lists, t2):
                t3.append(V(lambda e, v=v, k=k: e.max(v[:, 8:16], k), [t], own=False))
                yield
            for (v, i, s, k, w), t in zip(lists, t3):
                V(lambda e, v=v, k=k, i=i: e.max_index(i[:, 8:16], v[:, 8:16], k), [t], own=False)
                yield

        def key_scores(t):
            for hh in range(4):
                b, bank, bf = banks.take((4, 5, 6, 7))
                for j in range(2):
                    tk = mm(bank[:, j * 256:(j + 1) * 256], qpT[:, 2 * hh + j, t * 128:(t + 1) * 128], kbd, True, True,
                            qtoks + [t_kbd] + bf, mark=(j == 1))
                t2 = S(lambda e, hh=hh, bank=bank: e.activation(
                    sc[:, 4 * hh:4 * hh + 4, :].rearrange("p l k -> p (l k)"), bank[:, :], ACT.Copy),
                    [tk] + chosen)
                banks.free(b, [t2])
            return t2

        chosen = []

        chosen_gates = []

        def choose(t, t2):
            yield from top16([(v16[:, l, :], i16[:, l, :], sc[:, l, :], s2[:, l, :], [t2, (V.key, V.count)])
                   for l in range(16)])
            V(lambda e: e.tensor_copy(i16f.rearrange("p l k -> p (l k)"), i16.rearrange("p l k -> p (l k)")))
            vv = v16.rearrange("p (h s) k -> p h s k", s=2)
            V(lambda e: e.tensor_tensor(cand.rearrange("p h (a b) -> p h a b", a=16),
                                        vv[:, :, 0, :].unsqueeze(3).to_broadcast([P128, 8, 16, 16]),
                                        vv[:, :, 1, :].unsqueeze(2).to_broadcast([P128, 8, 16, 16]), ALU.add))
            tc_ = (V.key, V.count)
            yield from top16([(top[:, h, :], pos[:, h, :], cand[:, h, :], cnd2[:, h, :], [tc_]) for h in range(8)])
            chosen[:] = [(V.key, V.count)]
            posf = pos.rearrange("p h k -> p (h k)")
            V(lambda e: e.tensor_scalar(pj[0], posf, 4, None, ALU.logical_shift_right))
            V(lambda e: e.tensor_scalar(pj[1], posf, 15, None, ALU.bitwise_and))
            for j in range(2):
                V(lambda e, j=j: e.tensor_copy(pf[j], pj[j]))
                yield
                eq = s2.rearrange("p l k -> p (l k)").rearrange("p (a b) -> p a b", b=16)
                V(lambda e, j=j: e.tensor_tensor(eq, pf[j].unsqueeze(2).to_broadcast([P128, 128, 16]), iota16,
                                                 ALU.is_equal))
                yield
                eq4 = s2.rearrange("p l k -> p (l k)").rearrange("p (h a b) -> p h a b", h=8, b=16)
                iv = i16f.rearrange("p (h s) k -> p h s k", s=2)[:, :, j, :].unsqueeze(2).to_broadcast([P128, 8, 16, 16])
                V(lambda e, eq4=eq4, iv=iv: e.tensor_tensor(eq4, eq4, iv, ALU.mult))
                yield
                V(lambda e, j=j, eq=eq: e.tensor_reduce(sel[j], eq, AX.X, ALU.add), sel_free)
                yield
            gt = sel[2].rearrange("p (h k) -> p h k", h=8)
            t1 = V(lambda e: e.tensor_tensor(gt, top, top[:, :, 0:1].to_broadcast([P128, 8, 16]), ALU.subtract),
                   sel_free)
            yield "exp"
            t1 = S(lambda e: e.activation(gt, gt, ACT.Exp), [t1])
            V(lambda e: e.tensor_reduce(st_x[:, 8:16], gt, AX.X, ALU.add), [t1])
            V(lambda e: e.reciprocal(st_x[:, 8:16], st_x[:, 8:16]))
            chosen_gates[:] = [V(lambda e: e.tensor_tensor(
                gt, gt, st_x[:, 8:16].unsqueeze(2).to_broadcast([P128, 8, 16]), ALU.mult))]

        sel_free = []

        def turn_choice(t, t1):
            b, bank, bf = banks.take((4, 5, 6, 7))
            for j in range(3):
                tk = tp(bank[:, j * 128:(j + 1) * 128], sel[j], 128, [t1] + bf, mark=(j == 2))
            for j in range(3):
                t2 = V(lambda e, j=j, t=t: e.tensor_copy(selT[j][:, t * 128:(t + 1) * 128],
                                                         bank[:, j * 128:(j + 1) * 128]), [tk])
            banks.free(b, [t2])
            sel_free[:] = [tk]
            return t2

        gs = Ring([ar(17024 + 4096 * j, 4096) for j in range(2)])
        ohr = Ring([(ar(at, 512), ar(at + 512, 512)) for at in (2048, 14976, 16000)])
        iota4 = con[:, 128:256].unsqueeze(1).to_broadcast([P128, 4, 128])
        g_stores = {}

        def dense_gates(t, ready, background):
            for tb in range(P128 // TB * t, P128 // TB * (t + 1)):
                si, gbuf, gfree = gs.take()
                g3 = gbuf.rearrange("p (i t) -> p i t", t=TB)
                for q in range(TB // 4):
                    oi, (oh2, oh1), ofree = ohr.take()
                    tt = tb * TB + q * 4

                    def of(j, tt=tt):
                        return selT[j][:, tt:tt + 4].unsqueeze(2).to_broadcast([P128, 4, 128])
                    o2 = oh2.rearrange("p (t i) -> p t i", t=4)
                    for j in range(4):
                        V(lambda e, o=oh1[:, j * 128:(j + 1) * 128], c=tt + j: e.tensor_scalar(
                            o, con[:, 128:256], selT[0][:, c:c + 1], selT[2][:, c:c + 1], ALU.is_equal, ALU.mult),
                          [ready] + ofree, own=False)
                    tv = V(lambda e, o2=o2, a=of(1): e.tensor_tensor(o2, iota4, a, ALU.is_equal), ofree, own=False)
                    b, bank, bf = banks.take((4, 5, 6, 7))
                    for j in range(4):
                        tk = mm(bank[:, j * 128:(j + 1) * 128], oh2[:, j * 128:(j + 1) * 128],
                                oh1[:, j * 128:(j + 1) * 128], True, True, [tv] + bf, mark=(j == 3))
                    ohr.free(oi, [tk])
                    out = g3[:, :, q * 4:q * 4 + 4].rearrange("p i t -> p t i")
                    t2 = S(lambda e, out=out, bank=bank: e.activation(
                        out, bank[:, :].rearrange("p (t i) -> p t i", t=4), ACT.Copy), [tk] + gfree, own=False)
                    banks.free(b, [t2])
                    background(q)
                ts = dma(g_scratch[tb], g3, f"g_st{si}", after=[t2])
                gs.free(si, [ts])
                g_stores[si] = ts

        ngroups = KEYS // ETG
        pre_begin = list(xt) + last_x + [(P.key, P.count), (S.key, S.count), (V.key, V.count)]
        pre_b = Ring([ar(512 * j, 512) for j in range(4)])
        pre_stores = {}

        def ahead():
            for g in range(0, ngroups, 2):
                for u in range(ETG // 4):
                    e0 = g // 2 * ETG + 4 * u

                    def ev(j, bank, tk, e0=e0):
                        ai, ab, af = pre_b.take()
                        t1 = S(lambda e: e.activation(ab, bank[:, :], ACT.Gelu), [tk] + af + pre_begin, own=False)
                        ts = dma(a_scratch[e0 + j], ab, f"a_st{ai}", after=[t1])
                        pre_b.free(ai, [ts])
                        pre_stores[ai] = ts
                        return [t1]
                    yield from gemm4_steps("peer_uT", 2, 512, X, False, ev, [], among=(0, 1, 2, 3))
        work_ahead = ahead()

        def steps(n):
            for _ in range(n):
                next(work_ahead, None)
        choice = choose(0, key_scores(0))
        while next(choice, "exp") != "exp":
            pass
        steps(AHEAD_FIRST)
        for t in range(NT):
            for _ in choice:
                pass
            turned_choice = turn_choice(t, chosen_gates[0])
            choice = choose(t + 1, key_scores(t + 1)) if t + 1 < NT else iter(())

            def between(q):
                for _ in range(CHOICE_STEPS):
                    next(choice, None)
                steps(1)
            dense_gates(t, turned_choice, between)
        steps(10 ** 6)
        stores = list(g_stores.values()) + list(pre_stores.values())
        peer_begin = all_done() + stores
        F_ = phase(True)
        act_b = Ring([ar(2048 + 512 * j, 512) for j in range(3)])
        gring = Ring([ar(3584 + 2048 * j, 2048) for j in range(2)])
        aring = Ring([ar(1024 * j, 1024) for j in range(2)])
        f_free = [[], []]

        def split_f(full, hi, lo, after, free):
            t1 = S(lambda e: e.activation(hi, full, ACT.Copy), list(after) + list(free), own=False)
            return t1, G(lambda e: e.tensor_tensor(lo, full, hi.bitcast(F32), ALU.subtract), [t1] + list(free),
                         own=False)

        def up(g):
            toks = []
            for u in range(ETG // 4):
                e0 = g * ETG + 4 * u
                gi, gb, gf = gring.take()
                gv = gb.rearrange("p (b i t) -> p b i t", i=4, t=TB)
                tg = dma(gv, g_scratch[:, :, e0:e0 + 4, :].rearrange("b p i t -> p b i t"), f"g{gi}_in",
                         after=gf + peer_begin)

                def ev(j, bank, tk, u=u, gv=gv, tg=tg):
                    ai, ab, af = act_b.take()
                    t1 = S(lambda e: e.activation(ab, bank[:, :], ACT.Gelu), [tk] + af + peer_begin, own=False)
                    a3 = ab.rearrange("p (b t) -> p b t", t=TB)
                    t2 = V(lambda e: e.tensor_tensor(a3, a3, gv[:, :, j, :], ALU.mult), [t1, tg], own=False)
                    fh, fl = (f[:, 4 * u + j, :] for f in F_[g % 2])
                    t3, t4 = split_f(ab, fh, fl, [t2], f_free[g % 2])
                    act_b.free(ai, [t4])
                    toks[:] = [t3, t4, t2]
                    return [t1]
                if g % 2:
                    gemm4("peer_uT", 2, 512, X, False, ev, [])
                else:
                    for j in range(0, 4, 2):
                        ai, ab, af = aring.take()
                        a2 = ab.rearrange("p (e t) -> p e t", e=2)
                        at = g // 2 * ETG + 4 * u + j
                        ta = dma(a2, a_scratch[at:at + 2].rearrange("e p t -> p e t"), f"a{ai}_in",
                                 after=af + peer_begin)
                        for i in range(2):
                            a3 = a2[:, i, :].rearrange("p (b t) -> p b t", t=TB)
                            t2 = V(lambda e, a3=a3, gv=gv, c=j + i: e.tensor_tensor(a3, a3, gv[:, :, c, :], ALU.mult),
                                   [ta, tg], own=False)
                        fh, fl = (f[:, 4 * u + j:4 * u + j + 2, :] for f in F_[g % 2])
                        t3, t4 = split_f(a2, fh, fl, [t2], f_free[g % 2])
                        aring.free(ai, [t4])
                        toks[:] = [t3, t4, t2]
                gring.free(gi, [toks[2]])
            return toks[0:2]

        def down(g, ready):
            for c in range(2):
                def ev(t, bank, tk, c=c):
                    dst = H[:, t, c * 512:(c + 1) * 512]
                    t1 = V(lambda e: e.tensor_tensor(dst, bank[:, :], dst, ALU.add), [tk], own=False)
                    if g == ngroups - 1 and c == 1:
                        rows_ple.advance(t, [t1])
                    return [t1]
                tk = gemm4("peer_v", 2, 512, F_[g % 2], True, ev, ready, hold=g == ngroups - 1 and c == 1)
            f_free[g % 2] = [tk]

        nxt = up(0)
        for g in range(ngroups):
            ready = nxt
            if g + 1 < ngroups:
                nxt = up(g + 1)
            else:
                before_last = all_done()
                rows_ple = Rows(tiles(H), ND, "g_ple", early=before_last)
            down(g, ready)
        if stop == "peer":
            finish_with(H, all_done())
            return emit_all(nc, ctx, sem_names, P, V, S, G, Q)

        def ple(rows, pT_src, bias_src, after, ready=None):
            pT = ar(7168, 1024)
            br = ar(6144, 1024)
            t_p = dma(pT.rearrange("p (k t) -> p k t", k=2), pT_src.rearrange("(k p) t -> p k t", p=P128), "pT_in",
                      after=after)
            ps = tuple(f[:, 0:2, :] for f in F_[0])
            split = split_f(pT.rearrange("p (k t) -> p k t", k=2), ps[0], ps[1], [t_p], after)
            if bias_src is not None:
                t_b = dma(br[0:1, :], bias_src, "bias_in", after=after)
            sg = Ring([ar(3072 + 512 * j, 512) for j in range(4)])
            for c in range(2):
                gates = {}

                def ev_gate(t, bank, tk):
                    si, buf, f = sg.take()
                    t1 = S(lambda e: e.activation(buf, bank[:, :], ACT.Sigmoid), [tk] + f + list(after))
                    gates[t] = (si, buf, t1)
                    return [t1]
                kw = {} if bias_src is None else {"bias": br[0:1, c * 512:(c + 1) * 512], "bias_after": [t_b]}
                if c == 0:
                    gemm4_behind(rows, "w_gate", 2, 512, ev_gate, **kw)
                else:
                    gemm4("w_gate", 2, 512, X, True, ev_gate, [], **kw)

                def ev_proj(t, bank, tk, c=c):
                    si, buf, t1 = gates[t]
                    dst = H[:, t, c * 512:(c + 1) * 512]
                    t2 = V(lambda e: e.tensor_tensor(buf, bank[:, :], buf, ALU.mult), [tk, t1])
                    t3 = V(lambda e: e.tensor_tensor(dst, dst, buf, ALU.add))
                    sg.free(si, [t3])
                    if c == 1 and ready:
                        ready(t, t3)
                    return [t2]
                gemm4("w_proj", 1, 512, ps, True, ev_proj, list(split), hold=c == 1 and ready is not None)

        gf = ar(5120, 1024)
        t_gf = dma(gf, A["rows"][:, 0:1024], "gf_in", after=before_last)
        squared, junk = {}, ar(6144, D)

        def final_square(t, tok):
            ss = st_ss[:, 32 + t:33 + t]
            squared[t] = S(lambda e: e.activation(junk, H[:, t, :], ACT.Square, accum_out=ss), [tok, before_last])

        def final_scale(t):
            r, a, b, c, ss = (st[:, 32 + t:33 + t] for st in (st_r, st_a, st_b, st_c, st_ss))
            tr = rstd_of(ss, D, r, (a, b, c), [squared[t]])
            t1 = V(lambda e: e.scalar_tensor_tensor(H[:, t, :], H[:, t, :], r, gf, ALU.mult, ALU.mult), [tr, t_gf])
            rows_mix.advance(t, [t1])

        def final_ready(t, tok):
            final_square(t, tok)
            if t >= 1:
                final_scale(t - 1)
        rows_mix = Rows(tiles(H), ND, "g_mix_0")
        ple(rows_ple, A["pT"], None, before_last, final_ready)
        final_scale(NT - 1)
        if stop == "block1":
            finish_with(H, all_done())
            return emit_all(nc, ctx, sem_names, P, V, S, G, Q)

        cos2, sin2 = stat_rope[:, 0:32], stat_rope[:, 32:64]
        pos_i = ar(3072, 4).bitcast(I32)
        posf2, ang, turns, red, over = (ar(3104 + 32 * j, n) for j, n in enumerate((4, 32, 32, 32, 32)))
        begin = all_done()
        t_pos = dma(pos_i, A["pos"], "pos_in", after=begin)
        V(lambda e: e.tensor_copy(posf2, pos_i), [t_pos] + begin)
        V(lambda e: e.tensor_tensor(ang.rearrange("p (t r) -> p t r", t=NT),
                                    posf2.unsqueeze(2).to_broadcast([P128, NT, 8]),
                                    cst("inv", 8).unsqueeze(1).to_broadcast([P128, NT, 8]), ALU.mult))
        MAGIC = 12582912.0
        C1, C2 = 6.28125, 0.0019350051879882812
        C3 = 2 * np.pi - C1 - C2
        V(lambda e: e.tensor_scalar(turns, ang, float(1 / (2 * np.pi)), MAGIC, ALU.mult, ALU.add))
        V(lambda e: e.tensor_scalar(turns, turns, MAGIC, None, ALU.subtract))
        V(lambda e: e.scalar_tensor_tensor(red, turns, -C1, ang, ALU.mult, ALU.add))
        V(lambda e: e.scalar_tensor_tensor(red, turns, -C2, red, ALU.mult, ALU.add))
        V(lambda e: e.scalar_tensor_tensor(red, turns, float(-C3), red, ALU.mult, ALU.add))
        PI_LO = 3.1415925
        V(lambda e: e.tensor_scalar(ang, red, PI_LO, -PI_LO, ALU.min, ALU.max))
        V(lambda e: e.tensor_scalar(red, red, float(np.pi / 2), None, ALU.add))
        V(lambda e: e.tensor_scalar(over, red, float(np.pi), float(-2 * np.pi), ALU.is_gt, ALU.mult))
        V(lambda e: e.tensor_tensor(red, red, over, ALU.add))
        t_r = V(lambda e: e.tensor_scalar(red, red, PI_LO, -PI_LO, ALU.min, ALU.max))
        S(lambda e: e.activation(sin2, ang, ACT.Sin), [t_r])
        t_rope = S(lambda e: e.activation(cos2, red, ACT.Sin))

        def cs2(x, nh):
            return x.rearrange("p (t r) -> p t r", t=NT).unsqueeze(2).to_broadcast([P128, NT, nh, 8])

        mask = lambda qt: cst("causal", 512)[:, (3 - qt) * 128:512]
        before = lambda rt: cst("before", 512)[:, (3 - rt) * 128:512]
        ones = cst("before", 128)
        causal_w = lambda qt: (qt + 1) * 128

        def layer(l, rows):
            nonlocal F_
            phase(False, TOP_2)
            begin = all_done()
            tok = ar(3072, NT * 592).rearrange("p (t n) -> p t n", t=NT)
            mv = ar(5440, 2048).rearrange("p (t n) -> p t n", t=NT)
            mo = ar(7488, 2048).rearrange("p (t n) -> p t n", t=NT)
            qk = ar(9536, 4096).rearrange("p (c n) -> p c n", c=8)
            raws = Ring([ar(13632 + 516 * j, 516) for j in range(3)])
            iT = ar(13632, 512)
            aq = ar(15180, 2048).rearrange("p (t n) -> p t n", t=NT)
            lfb = Ring([ar(15180 + 896 * j, 896) for j in range(2)])
            iq = ar(17228, 2048).rearrange("p (t n) -> p t n", t=NT)
            sbias = ar(17228, 2048).rearrange("p (t n) -> p t n", t=NT)
            hm = ar(17228, 2048).rearrange("p (t n) -> p t n", t=NT)
            score = ar(19276, 2048).rearrange("p (t n) -> p t n", t=NT)
            att = ar(19276, 2048).rearrange("p (t n) -> p t n", t=NT)
            kdup = ar(19276, 1024).rearrange("p (t g u d) -> p t g u d", t=NT, g=2, u=2)
            ikdup = ar(20300, 512).rearrange("p (t u d) -> p t u d", t=NT, u=2)
            qslots = [ar(512 * j, 512) for j in range(2)]
            kT = ar(1024, 1024).rearrange("p (g n) -> p g n", g=2)
            ikT = ar(2048, 512)
            work = ar(2560, 512)
            t_row = dma(row[:, :], A["rows"][:, 1024 + 208 * l:1232 + 208 * l], "row_in", after=begin)
            cq_split = top_for_cq(True)
            rows_cq = Rows([tok[:, t, 0:256] for t in range(NT)], 2, f"g_cq_{l}", dst=cq_split)

            def ev_tok(t, bank, tk):
                t1 = copy_out(tok[:, t, 0:512], bank[:, :], [tk])
                rows_cq.advance(t, [t1])
                return [t1]
            gemm4_behind(rows, "w_in_2", 2, 512, ev_tok, hold=True)
            product = gemm4_steps("w_in_2 b", 2, 80, X, True, lambda t, bank, tk: [
                copy_out(tok[:, t, 512:592], bank[:, 0:80], [tk])], [])
            rows_cq.scale(NT - 1)
            for t in range(NT):
                next(product)
            cq = rows_cq.finish(scaled=True)
            for _ in product:
                pass
            tok_done = [(V.key, V.count), (S.key, S.count)]
            for name, dst in (("w_q_up_2", aq), ("w_iq_up_2", iq)):
                t_q = gemm4(name, 1, 512, cq_split, True, lambda t, bank, tk, dst=dst: [
                    copy_out(dst[:, t, :], bank[:, :], [tk])], cq)
            q_done = [(V.key, V.count), (S.key, S.count)]
            top_for_cq(False)
            Pb, PTb = soft_bufs(21324)
            small = ar(24908, 256)
            def head_norm(x, nh, gname, after):
                sq = ar(21324 + 1024, NT * nh * 64).rearrange("p (t h d) -> p t h d", t=NT, h=nh)
                n = NT * nh
                V(lambda e: e.tensor_tensor(sq, x, x, ALU.mult), after)
                V(lambda e: e.tensor_reduce(st_ss[:, 0:n].rearrange("p (t h) -> p t h", t=NT), sq, AX.X, ALU.add))
                rstd_of(st_ss[:, 0:n], 64, st_r[:, 0:n], (st_a[:, 0:n], st_b[:, 0:n], st_c[:, 0:n]))
                r = st_r[:, 0:n].rearrange("p (t h) -> p t h", t=NT).unsqueeze(3).to_broadcast([P128, NT, nh, 64])
                V(lambda e: e.tensor_tensor(x, x, r, ALU.mult))
                g = row[:, RC[f"{gname}_0"] - 1024:RC[f"{gname}_0"] - 1024 + 64]
                g = g.unsqueeze(1).unsqueeze(1).to_broadcast([P128, NT, nh, 64])
                V(lambda e: e.tensor_tensor(x, x, g, ALU.mult), [t_row])

            def head_rope(x, nh, after=()):
                tm = [ar(21324 + 256 * j, 256)[:, 0:NT * nh * 8].rearrange("p (t h x) -> p t h x", t=NT, h=nh)
                      for j in range(4)]
                x1, x2 = x[:, :, :, 0:8], x[:, :, :, 8:16]
                return rope(x1, x2, x1, x2, cs2(cos2, nh), cs2(sin2, nh), tm, list(after) + [t_rope])
            x_iq = iq.rearrange("p t (h d) -> p t h d", h=8)
            x_ik = tok[:, :, 512:576].unsqueeze(2)
            x_aq = aq.rearrange("p t (h d) -> p t h d", h=8)
            x_ak = tok[:, :, 256:384].rearrange("p t (h d) -> p t h d", h=2)
            head_rope(x_iq, 8, q_done + tok_done)
            head_norm(x_ik, 1, "g_ik", [])
            head_rope(x_ik, 1)
            head_norm(x_aq, 8, "g_qn", [])
            head_rope(x_aq, 8)
            head_norm(x_ak, 2, "g_kn", [])
            head_rope(x_ak, 2)
            iw = tok[:, :, 576:584]
            V(lambda e: e.tensor_scalar(iw, iw, IDX_SCALE, None, ALU.mult))
            for u in range(2):
                V(lambda e, u=u: e.tensor_copy(ikdup[:, :, u, :], tok[:, :, 512:576]))
                prep = V(lambda e, u=u: e.tensor_copy(kdup[:, :, :, u, :], x_ak))
            for c in range(2):
                def ev_conv(g, bank, tk, c=c):
                    ch = 4 * c + g
                    ri, rw, rf = raws.take()
                    V(lambda e: e.memset(rw[:, 0:3], 0.0), rf + begin)
                    t1 = S(lambda e: e.activation(rw[:, 3:515], bank[:, :], ACT.Copy), [tk] + rf + begin)
                    o = qk[:, ch, :]
                    for j in range(4):
                        at = GC[f"conv_w_{l}"] + 8 * j + ch
                        g_, x_ = gain[:, at:at + 1], rw[:, j:j + 512]
                        if j == 0:
                            V(lambda e, x_=x_, g_=g_: e.tensor_scalar(o, x_, g_, None, ALU.mult), [t1])
                        else:
                            t2 = V(lambda e, x_=x_, g_=g_: e.scalar_tensor_tensor(o, x_, g_, o, ALU.mult, ALU.add))
                    at = GC[f"conv_b_{l}"] + ch
                    conv_out.append((o, gain[:, at:at + 1], t2))
                    raws.free(ri, [t2])
                    return [t1]
                conv_out = []
                gemm4("w_in_2", 2, 512, X, False, ev_conv, [])
                for o, bcol, t2 in conv_out:
                    t_qk = S(lambda e, o=o, bcol=bcol: e.activation(o, o, ACT.Silu, bias=bcol), [t2])
            tmp_free = [(P.key, P.count)] + last_x
            tk_i = head_T([ikdup[:, t].rearrange("p u d -> p (u d)") for t in range(NT)], ikT, [prep], tmp_free)
            for g in range(2):
                tk_a = head_T([kdup[:, t, g].rearrange("p u d -> p (u d)") for t in range(NT)], kT[:, g, :], [prep],
                              tmp_free)
                tk_i += tk_a
            turned = tk_i + [(P.key, P.count)]
            rel = Ring(Pb)
            for h in range(8):
                if h % 2 == 0:
                    qd = qslots[h // 2 % 2]
                    tq = head_T([iq[:, t, h * 64:h * 64 + 128] for t in range(NT)], qd, [prep], turned + [(P.key, P.count)])
                lo = 64 * (h % 2)
                for qt in range(NT):
                    w = causal_w(qt)
                    b, bank, bf = banks.take()
                    tk = mm(bank[:, 0:w], qd[lo:lo + 64, qt * 128:(qt + 1) * 128], ikT[lo:lo + 64, 0:w], True, True,
                            turned + tq + bf, mark=True)
                    ri, rb, rf = rel.take()
                    t1 = S(lambda e, rb=rb, bank=bank, w=w: e.activation(rb[:, 0:w], bank[:, 0:w], ACT.Relu),
                           [tk] + rf + turned, own=False)
                    banks.free(b, [t1])
                    sc_, wc = score[:, qt, 0:w], iw[:, qt, h:h + 1]
                    if h == 0:
                        t2 = V(lambda e, rb=rb, w=w, sc_=sc_, wc=wc: e.tensor_scalar(sc_, rb[:, 0:w], wc, None, ALU.mult),
                               [t1] + turned)
                    else:
                        t2 = V(lambda e, rb=rb, w=w, sc_=sc_, wc=wc: e.scalar_tensor_tensor(
                            sc_, rb[:, 0:w], wc, sc_, ALU.mult, ALU.add), [t1])
                    rel.free(ri, [t2])
            gates = tok[:, :, 584:592]
            ifb = row[:, 192:200].unsqueeze(1).to_broadcast([P128, NT, 8])
            V(lambda e: e.tensor_tensor(gates, gates, ifb, ALU.add), [t_row])
            lf = small[:, 0:16].rearrange("p (t h) -> p t h", t=NT)
            ex = small[:, 16:32].rearrange("p (t h) -> p t h", t=NT)
            mn = small[:, 32:48].rearrange("p (t h) -> p t h", t=NT)
            cumF = small[:, 48:64].rearrange("p (t h) -> p t h", t=NT)
            S(lambda e: e.activation(ex, gates[:, :, 4:8], ACT.Abs), [(V.key, V.count)])
            S(lambda e: e.activation(ex, ex, ACT.Exp, scale=-1.0))
            t1 = S(lambda e: e.activation(ex, ex, ACT.Ln, bias=1.0))
            V(lambda e: e.tensor_scalar(mn, gates[:, :, 4:8], 0.0, None, ALU.min))
            t_lf = V(lambda e: e.tensor_tensor(lf, mn, ex, ALU.subtract), [t1])
            b, bank, bf = banks.take()
            for t in range(NT):
                tk = tp(bank[0:4, t * 128:(t + 1) * 128], gates[:, t, 0:4], 128, [t_lf] + bf, mark=(t == 3))
            t_iT = S(lambda e, bank=bank: e.activation(iT[0:4, :], bank[0:4, :], ACT.Copy), [tk])
            banks.free(b, [t_iT])
            b, bank, bf = banks.take()
            for qt in range(NT):
                for rt in range(qt + 1):
                    tk = mm(bank[:, 4 * qt:4 * qt + 4], cst("upto", 128) if rt == qt else ones, lf[:, rt, :],
                            rt == 0, rt == qt, [t_lf] + bf, mark=(rt == qt))
            t_F = V(lambda e, bank=bank: e.tensor_copy(cumF.rearrange("p t h -> p (t h)"), bank[:, 0:16]), [tk])
            banks.free(b, [t_F])

            V(lambda e: e.tensor_copy(sbias[:, 0, 0:128], mask(0)), [(P.key, P.count)])
            for qt in range(1, NT):
                w = causal_w(qt)
                s_, wk = score[:, qt, 0:w], work[:, 0:w]
                dg = score[:, qt, w - 128:w]
                V(lambda e, dg=dg: e.tensor_tensor(dg, dg, mask(0), ALU.add))
                for r in range(NSEL // 8):
                    a_, b_ = (s_, wk) if r % 2 == 0 else (wk, s_)
                    V(lambda e, a_=a_: e.max(st_x[:, 0:8], a_))
                    V(lambda e, a_=a_, b_=b_: e.match_replace(b_, st_x[:, 0:8], a_, TAKEN))
                V(lambda e, qt=qt, w=w, s_=s_: e.tensor_scalar(sbias[:, qt, 0:w], s_, TAKEN / 2, NEG, ALU.is_gt,
                                                               ALU.mult))
            sel_done = (V.key, V.count)
            gemm4("w_in_2", 2, 512, X, True, lambda t, bank, tk: [S(lambda e: e.activation(
                mv[:, t, :], bank[:, :], ACT.Copy), [tk], own=False)], [])
            gemm4("w_in_2", 2, 512, X, True, lambda t, bank, tk: [S(lambda e: e.activation(
                mo[:, t, :], bank[:, :], ACT.Sigmoid), [tk], own=False)], [])
            def prep_a(h):
                if h % 2 == 0:
                    qd = qslots[h // 2 % 2]
                    pair[0] = (qd, head_T([aq[:, t, h * 64:h * 64 + 128] for t in range(NT)], qd, [prep],
                                          [(P.key, P.count)]))
                qd, tt = pair[0]
                lo = 64 * (h % 2)
                return qd[lo:lo + 64, :], kT[lo:lo + 64, h // 4, :], tt
            end = attend(8, 64, prep_a, lambda h, c: tok[:, c, 384 + 64 * (h // 4):448 + 64 * (h // 4)],
                         lambda h, qt, w: (sbias[:, qt, 0:w], [], 0.125), causal_w, Pb, PTb,
                         scaled_out(lambda h: att[:, :, h * 64:(h + 1) * 64], 64),
                         [sel_done, (P.key, P.count), (S.key, S.count)])
            tm = {0: Rows(tiles(att), 4, None, norm=False, early=[end, (P.key, P.count)]).all([])}
            start = [end, (P.key, P.count), (S.key, S.count), t_qk, t_iT, t_F]
            mlstm_end = mlstm(qk, mv, lf, iT, cumF, lfb, Pb, PTb, small, hm, start)
            product = gemm4_steps("w_out_2", 2, 512, X, True, add_h(0), tm)
            for t in range(NT):
                next(product)
            x = hm.rearrange("p t (h d) -> p t h d", h=4)
            sq = ar(21324, 2048).rearrange("p (t h d) -> p t h d", t=NT, h=4)
            V(lambda e: e.tensor_tensor(sq, x, x, ALU.mult), [mlstm_end, (P.key, P.count)])
            V(lambda e: e.tensor_reduce(st_ss[:, 0:16].rearrange("p (t h) -> p t h", t=NT), sq, AX.X, ALU.add))
            rstd_of(st_ss[:, 0:16], 128, st_r[:, 0:16], (st_a[:, 0:16], st_b[:, 0:16], st_c[:, 0:16]))
            r = st_r[:, 0:16].rearrange("p (t h) -> p t h", t=NT).unsqueeze(3).to_broadcast([P128, NT, 4, 128])
            V(lambda e: e.tensor_tensor(x, x, r, ALU.mult))
            tg = V(lambda e: e.tensor_tensor(hm, hm, mo, ALU.mult))
            tm[1] = Rows(tiles(hm), 4, f"g_mh_{l}", c_at=4, norm=False).all([tg])
            for _ in product:
                pass
            before_last = all_done()
            rows_mlp = Rows(tiles(H), ND, f"g_mlp_{l}")
            gemm4("w_out_2", 2, 512, X, True, add_h(1, rows_mlp), tm, hold=True)
            xt = rows_mlp.finish()
            if stop == f"Lattn{l}":
                return True
            F_ = phase(True)
            begin = before_last
            relu_b = Ring([ar(3072 + 512 * j, 512) for j in range(4)])
            mid_free = [begin, begin]

            def up_ff(q):
                mid, ready = F_[q % 2], []
                for c in range(2):
                    def ev_relu(g, bank, tk, c=c):
                        bi, fb, ff = relu_b.take()
                        t1 = S(lambda e: e.activation(fb, bank[:, :], ACT.Relu), [tk] + ff + begin, own=False)
                        t2 = V(lambda e: e.tensor_tensor(fb, fb, fb, ALU.mult), [t1], own=False)
                        fh, fl = (f[:, 4 * c + g, :] for f in mid)
                        t3, t4 = split_f(fb, fh, fl, [t2], mid_free[q % 2])
                        relu_b.free(bi, [t4])
                        ready[:] = [t3, t4]
                        return [t1]
                    gemm4("w_ff1_2", 2, 512, X, False, ev_relu, xt)
                return ready

            ready, last = up_ff(0), DFF // 1024 - 1
            for q in range(last + 1):
                now, before_last = ready, all_done()
                if q < last:
                    ready = up_ff(q + 1)
                rows_ple = Rows(tiles(H), ND, f"g_ple_{l}") if q == last else None
                for c in range(2):
                    tk = gemm4("w_ff2_2", 2, 512, F_[q % 2], True, add_h(c, rows_ple), now,
                               hold=q == last and c == 1)
                mid_free[q % 2] = [tk]
            if stop == f"Lff{l}":
                return True
            rows_mix = Rows(tiles(H), ND, "g_mix_1") if l == 0 else None
            ple(rows_ple, A["p2T"][l], A["b_ple_gate_2"][l:l + 1, :], before_last,
                (lambda t, tok: rows_mix.advance(t, [tok])) if l == 0 else None)
            following[:] = [rows_mix]
            return stop == f"layer{l}"

        def mlstm(qk, mv, lf, iT, cumF, lfb, Pb, PTb, small, hm, start):
            prob, ptr = Ring(Pb), Ring(PTb)
            lfm = {}

            def spread(h):
                i, buf, f = lfb.take()
                fr = list(f) + list(start)
                for rt in range(NT):
                    V(lambda e, rt=rt: e.tensor_scalar(buf[:, 384 + rt * 128:512 + rt * 128], cst("upto", 128),
                                                       lf[:, rt, h:h + 1], None, ALU.mult), fr, own=(rt == 0))
                    if rt < NT - 1:
                        V(lambda e, rt=rt: e.tensor_scalar(buf[:, rt * 128:(rt + 1) * 128], ones,
                                                           lf[:, rt, h:h + 1], None, ALU.mult), fr, own=False)
                lfm[h] = (i, buf, (V.key, V.count))

            units = [(h, qt) for h in range(4) for qt in range(NT)]
            st, ob = {}, {}
            mval = small[:, 64:80]
            nmv = small[:, 80:96]
            den = small[:, 96:112]
            em = small[:, 112:128]
            rin = small[:, 128:144]

            def scores(u):
                h, qt = units[u]
                w = causal_w(qt)
                if qt == 0:
                    spread(h)
                li, lb, lt = lfm[h]
                b, bank, bf = banks.take(SC)
                for rt in range(qt, -1, -1):
                    lhs = lb[:, 384 + rt * 128:512 + rt * 128] if rt == qt else lb[:, rt * 128:(rt + 1) * 128]
                    mm(bank[:, 0:(rt + 1) * 128], lhs, before(rt), rt == qt, False, [lt] + list(start) + bf)
                tk = mm(bank[:, 0:w], con[0:4, CC["head"] + 128 * h:CC["head"] + 128 * h + 128], iT[0:4, 0:w], False,
                        True, mark=True)
                if qt == NT - 1:
                    lfb.free(li, [tk])
                b2, bank2, bf2 = banks.take(SC)
                tk2 = mm(bank2[:, 0:w], qk[:, h, qt * 128:(qt + 1) * 128], qk[:, 4 + h, 0:w], True, True, bf2,
                         mark=True)
                i, pr, pf = prob.take()
                c = 4 * h + qt
                m, nm = mval[:, c:c + 1], nmv[:, c:c + 1]
                V(lambda e: e.tensor_tensor_reduce(pr[:, 0:w], bank[:, 0:w], mask(qt), 1.0, -3e38, ALU.add, ALU.max, m),
                  [tk] + pf + list(start))
                t1 = (V.key, V.count)
                V(lambda e: e.tensor_tensor(m, m, cumF[:, qt, h:h + 1], ALU.max))
                t2 = V(lambda e: e.tensor_scalar(nm, m, -1.0, None, ALU.mult))
                banks.free(b, [t1])
                t3 = S(lambda e: e.activation(pr[:, 0:w], pr[:, 0:w], ACT.Exp, bias=nm), [t2])
                st[u] = (i, pr, t3, b2, bank2, tk2)

            def turn(u):
                h, qt = units[u]
                w = causal_w(qt)
                i, pr, t3, b2, bank2, tk2 = st[u]
                dn = den[:, 4 * h + qt:4 * h + qt + 1]
                t4 = V(lambda e: e.tensor_tensor_reduce(pr[:, 0:w], bank2[:, 0:w], pr[:, 0:w], 128 ** -0.5, 0.0,
                                                        ALU.mult, ALU.add, dn), [t3, tk2])
                banks.free(b2, [t4])
                b, bank, bf = banks.take(SC)
                for c in range(w // 128):
                    tk = tp(bank[:, c * 128:(c + 1) * 128], pr[:, c * 128:(c + 1) * 128], 128, [t4] + bf,
                            mark=(c == w // 128 - 1))
                prob.free(i, [tk])
                j, pt, ptf = ptr.take()
                t5 = copy_out(pt[:, 0:w], bank[:, 0:w], [tk] + ptf)
                banks.free(b, [t5])
                st[u] = (j, pt, t5)

            def pv(u):
                h, qt = units[u]
                j, pt, t5 = st[u]
                if qt == 0:
                    ob[h] = banks.take(OB)
                b, bank, bf = ob[h]
                for c in range(qt + 1):
                    tk = mm(bank[:, qt * 128:(qt + 1) * 128], pt[:, c * 128:(c + 1) * 128],
                            mv[:, c, h * 128:(h + 1) * 128], c == 0, c == qt, [t5] + bf, mark=(c == qt))
                ptr.free(j, [tk])
                if qt == NT - 1:
                    s_ = slice(4 * h, 4 * h + 4)
                    S(lambda e: e.activation(em[:, s_], nmv[:, s_], ACT.Exp), [tk])
                    t6 = S(lambda e: e.activation(rin[:, s_], den[:, s_], ACT.Abs))
                    V(lambda e: e.tensor_tensor(rin[:, s_], rin[:, s_], em[:, s_], ALU.max), [t6])
                    V(lambda e: e.reciprocal(rin[:, s_], rin[:, s_]))
                    t7 = V(lambda e: e.tensor_tensor(
                        hm[:, :, h * 128:(h + 1) * 128], bank[:, :].rearrange("p (t d) -> p t d", t=NT),
                        rin[:, s_].unsqueeze(2).to_broadcast([P128, NT, 128]), ALU.mult))
                    banks.free(b, [t7])
                    st["end"] = t7

            n = len(units)
            for i in range(n + 3):
                if i < n:
                    scores(i)
                if 1 <= i < n + 1:
                    turn(i - 1)
                if i >= 3:
                    pv(i - 3)
            return st["end"]

        following = [rows_mix]
        for l in range(2):
            if layer(l, following[0]):
                break
        finish_with(H, all_done())
        return emit_all(nc, ctx, sem_names, P, V, S, G, Q)


def emit_all(nc, ctx, sem_names, P, V, S, G, Q):
    sems = {n: ctx.enter_context(nc.semaphore(f"s_{n}")) for n in sem_names}
    block = ctx.enter_context(nc.Block())

    @block.sync
    def _(e):
        Q.emit(e, sems)

    @block.tensor
    def _(e):
        P.emit(e, sems)

    @block.vector
    def _(e):
        V.emit(e, sems)

    @block.scalar
    def _(e):
        S.emit(e, sems)

    @block.gpsimd
    def _(e):
        G.emit(e, sems)


def host_arrays(i):
    def col(v):
        return np.asarray(v, np.float32).reshape(-1, P128).T
    parts = [col(i["g_mix"][0]), col(i["g_cq"][0]), col(i["g_ckv"][0]),
             np.concatenate([col(i["g_out_mla"][0]), col(i["g_out_dil"][0])], 1), col(i["g_ffn"][0]),
             col(i["g_ple"][0])]
    rows = [np.broadcast_to(i["g_final"][None, :], (P128, D))]
    for l in range(2):
        parts += [col(i["g_mix_2"][l]), col(i["g_cq_2"][l]), col(i["g_mh_2"][l].reshape(-1)), col(i["g_mlp_2"][l]),
                  col(i["g_ple_2"][l]), np.concatenate([col(i["conv_w_2"][l, j]) for j in range(4)], 1),
                  col(i["conv_b_2"][l])]
        r = np.concatenate([i["g_qn_2"][l], i["g_kn_2"][l], i["g_ik_2"][l], i["i_bias_2"][l], i["f_bias_2"][l],
                            np.zeros(8, np.float32)])
        rows.append(np.broadcast_to(r[None, :], (P128, 208)))
    kbd = np.zeros((P128, 256), np.float32)
    kbd[0:64, 0:128] = i["peer_keys1"][0].T
    kbd[64:128, 128:256] = i["peer_keys2"][0].T
    consts, dil = constants()
    c = np.ascontiguousarray
    return {
        "x": i["x"][0], "consts": consts, "dil_bias": dil, "gains": c(np.concatenate(parts, 1)),
        "rows": c(np.concatenate(rows, 1)), "w_in": i["w_in"][0], "w_uq": i["w_uq"][0], "w_ukv": i["w_ukv"][0],
        "w_out": i["w_out"][0], "w_peer_q": i["w_peer_q"][0], "peer_keys": kbd,
        "peer_uT": c(i["peer_u"][0].T), "peer_v": i["peer_v"][0], "w_ple_gate": i["w_ple_gate"][0],
        "w_ple_proj": i["w_ple_proj"][0], "pT": c(i["p"][0, 0].T),
        "pos": c(i["positions_2"][0].reshape(NT, P128).T),
        "p2T": c(i["p_2"][:, 0].transpose(0, 2, 1)), "w_in_2": i["w_in_2"], "w_q_up_2": i["w_q_up_2"],
        "w_iq_up_2": i["w_iq_up_2"], "w_out_2": i["w_out_2"], "w_ff1_2": i["w_ff1_2"], "w_ff2_2": i["w_ff2_2"],
        "w_ple_gate_2": i["w_ple_gate_2"], "b_ple_gate_2": i["b_ple_gate_2"], "w_ple_2": i["w_ple_2"],
    }


def kernel(**inputs):
    import concourse.bacc as bacc
    from concourse.bass_utils import run_bass_kernel_spmd

    nc = bacc.Bacc("TRN2", target_bir_lowering=False, num_devices=1)
    arrays, aps = {}, {}
    for name, a in host_arrays({k: np.asarray(v) for k, v in inputs.items()}).items():
        a = np.ascontiguousarray(a)
        arrays[name + "_dram"] = a
        aps[name] = nc.dram_tensor(name + "_dram", a.shape, mybir.dt.from_np(a.dtype), kind="ExternalInput").ap()
    out = nc.dram_tensor("out_dram", (T, D), F32, kind="ExternalOutput").ap()
    aps["out"] = out
    build(nc, aps)
    r = run_bass_kernel_spmd(nc, [arrays], core_ids=[0])
    return r.results[0]["out_dram"].reshape(1, T, D)
```
